# Optimizing a Trainium2 kernel written in Bass

```python
import math
import jax, jax.numpy as jnp
from jax import lax
import numpy as np

D_MODEL = 1024
BATCH = 1
SEQ = 512
DEPTH = 1
DEC_BATCH = 8
DEC_SEQ = 1
PAST_LEN = 1024
PAGE_SIZE = 128

ATTN_WIDTH = D_MODEL // 2
MLSTM_WIDTH = D_MODEL - ATTN_WIDTH
A_HEAD_DIM = 64
A_HEADS = ATTN_WIDTH // A_HEAD_DIM
M_HEADS = 4
M_HEAD_DIM = MLSTM_WIDTH // M_HEADS
MOBA_BLOCK = 256
MOBA_TOPK = 3
Q_CHUNK = 64
MLSTM_CHUNK = 64
D_FF = 4 * D_MODEL
RMS_EPS = 1e-6
NEG_INF = float('-inf')
OFF_QA = 0
OFF_KA = ATTN_WIDTH
OFF_VA = 2 * ATTN_WIDTH
OFF_QM = 3 * ATTN_WIDTH
OFF_KM = OFF_QM + MLSTM_WIDTH
OFF_VM = OFF_QM + 2 * MLSTM_WIDTH
OFF_OM = OFF_QM + 3 * MLSTM_WIDTH
OFF_G = OFF_QM + 4 * MLSTM_WIDTH
IN_WIDTH = OFF_G + 2 * M_HEADS

kernel_name = 'hymba_moba_mlstm_step'

def rmsnorm(x, w):
    xf = x.astype(jnp.float32)
    y = xf * lax.rsqrt(jnp.mean(xf * xf, axis=-1, keepdims=True) + RMS_EPS)
    return (y * w.astype(jnp.float32)).astype(x.dtype)

def moba_attention(q, k, v, q_start):
    B, Lq, H, dh = q.shape
    L = k.shape[1]
    scale = dh ** -0.5
    cq = min(Q_CHUNK, Lq)
    n_chunks = -(-Lq // cq)
    lq_pad = n_chunks * cq
    lk_pad = -(-(q_start + lq_pad) // MOBA_BLOCK) * MOBA_BLOCK
    q_p = jnp.pad(q, ((0, 0), (0, lq_pad - Lq), (0, 0), (0, 0)))
    k_p = jnp.pad(k, ((0, 0), (0, lk_pad - L), (0, 0), (0, 0)))
    v_p = jnp.pad(v, ((0, 0), (0, lk_pad - L), (0, 0), (0, 0)))
    n_full = L // MOBA_BLOCK
    top = min(MOBA_TOPK, n_full)
    if top > 0:
        kb = k[:, :n_full * MOBA_BLOCK].reshape(B, n_full, MOBA_BLOCK, H, dh).transpose(0, 3, 1, 2, 4)
        vb = v[:, :n_full * MOBA_BLOCK].reshape(B, n_full, MOBA_BLOCK, H, dh).transpose(0, 3, 1, 2, 4)
        k_mean = jnp.mean(kb.astype(jnp.float32), axis=3)
        bi = jnp.arange(B)[:, None, None, None]
        hi = jnp.arange(H)[None, :, None, None]
    qc = q_p.reshape(B, n_chunks, cq, H, dh).transpose(1, 0, 3, 2, 4)

    def one_chunk(args):
        q_blk, c = args
        start = q_start + c * cq
        qpos = start + jnp.arange(cq)
        own_start = (start // MOBA_BLOCK) * MOBA_BLOCK
        k_own = lax.dynamic_slice_in_dim(k_p, own_start, MOBA_BLOCK, axis=1)
        v_own = lax.dynamic_slice_in_dim(v_p, own_start, MOBA_BLOCK, axis=1)
        kpos = own_start + jnp.arange(MOBA_BLOCK)
        s_own = jnp.einsum('bhtd,bshd->bhts', q_blk, k_own, preferred_element_type=jnp.float32) * scale
        s_own = jnp.where(kpos[None, None, None, :] <= qpos[None, None, :, None], s_own, NEG_INF)
        if top == 0:
            p_own = jax.nn.softmax(s_own, axis=-1).astype(v.dtype)
            return jnp.einsum('bhts,bshd->bhtd', p_own, v_own)
        cur_blk = qpos // MOBA_BLOCK
        gate = jnp.einsum('bhtd,bhnd->bhtn', q_blk.astype(jnp.float32), k_mean)
        past = jnp.arange(n_full)[None, :] < cur_blk[:, None]
        gate = jnp.where(past[None, None], gate, NEG_INF)
        _, idx = lax.top_k(gate, top)
        sel_ok = idx < cur_blk[None, None, :, None]
        k_sel = kb[bi, hi, idx]
        v_sel = vb[bi, hi, idx]
        s_sel = jnp.einsum('bhtd,bhtjsd->bhtjs', q_blk, k_sel, preferred_element_type=jnp.float32) * scale
        s_sel = jnp.where(sel_ok[..., None], s_sel, NEG_INF).reshape(B, H, cq, top * MOBA_BLOCK)
        p = jax.nn.softmax(jnp.concatenate([s_sel, s_own], axis=-1), axis=-1)
        p_sel = p[..., :top * MOBA_BLOCK].reshape(B, H, cq, top, MOBA_BLOCK).astype(v.dtype)
        p_own = p[..., top * MOBA_BLOCK:].astype(v.dtype)
        return (jnp.einsum('bhtjs,bhtjsd->bhtd', p_sel, v_sel)
                + jnp.einsum('bhts,bshd->bhtd', p_own, v_own))

    outs = lax.map(one_chunk, (qc, jnp.arange(n_chunks)))
    return outs.transpose(1, 0, 3, 2, 4).reshape(B, lq_pad, H, dh)[:, :Lq]

def mlstm_chunkwise(q, k, v, i_pre, f_pre, C0, n0, m0):
    B, S, NH, dh = q.shape
    cs = min(MLSTM_CHUNK, S)
    nc = -(-S // cs)
    sp = nc * cs
    valid = jnp.arange(sp) < S
    f32 = jnp.float32

    def pad(a):
        return jnp.pad(a, [(0, 0), (0, sp - S)] + [(0, 0)] * (a.ndim - 2))

    def to_chunks(a):
        return pad(a).astype(f32).reshape(B, nc, cs, NH, dh).transpose(1, 0, 3, 2, 4)

    qc = to_chunks(q) * (dh ** -0.5)
    kc = to_chunks(k)
    vc = to_chunks(v)
    li = jnp.where(valid[None, :, None], pad(i_pre).astype(f32), NEG_INF)
    lf = jnp.where(valid[None, :, None], jax.nn.log_sigmoid(pad(f_pre).astype(f32)), 0.0)
    li = li.reshape(B, nc, cs, NH).transpose(1, 0, 3, 2)
    lf = lf.reshape(B, nc, cs, NH).transpose(1, 0, 3, 2)
    tri = jnp.tril(jnp.ones((cs, cs), dtype=bool))

    def step(carry, inp):
        C, n, m = carry
        qb, kb, vb, lib, lfb = inp
        b = jnp.cumsum(lfb, axis=-1)
        D = jnp.where(tri, b[..., :, None] - b[..., None, :] + lib[..., None, :], NEG_INF)
        m_t = jnp.maximum(b + m[..., None], jnp.max(D, axis=-1))
        W = jnp.exp(D - m_t[..., None])
        decay = jnp.exp(b + m[..., None] - m_t)
        qk = jnp.einsum('bhtd,bhsd->bhts', qb, kb) * W
        num = (jnp.einsum('bhts,bhsd->bhtd', qk, vb)
               + decay[..., None] * jnp.einsum('bhtd,bhde->bhte', qb, C))
        den = jnp.sum(qk, axis=-1) + decay * jnp.einsum('bhtd,bhd->bht', qb, n)
        h = num / jnp.maximum(jnp.abs(den), jnp.exp(-m_t))[..., None]
        m_new = m_t[..., -1]
        w_end = jnp.exp(b[..., -1:] - b + lib - m_new[..., None])
        dec_end = jnp.exp(b[..., -1] + m - m_new)
        C_new = dec_end[..., None, None] * C + jnp.einsum('bhs,bhsd,bhse->bhde', w_end, kb, vb)
        n_new = dec_end[..., None] * n + jnp.einsum('bhs,bhsd->bhd', w_end, kb)
        return (C_new, n_new, m_new), h

    carry0 = (C0.astype(f32), n0.astype(f32), m0.astype(f32))
    (C, n, m), hs = lax.scan(step, carry0, (qc, kc, vc, li, lf))
    h = hs.transpose(1, 0, 3, 2, 4).reshape(B, sp, NH, dh)[:, :S]
    return h, C, n, m

def hybrid_layer(x, k_past, v_past, C0, n0, m0, q_start,
                 ln1_w, w_in, b_gates, mlstm_norm_w, w_out, ln2_w, w_up, w_down):
    B, S, _ = x.shape
    xn = rmsnorm(x, ln1_w)
    z = xn @ w_in
    qa = z[..., OFF_QA:OFF_KA].reshape(B, S, A_HEADS, A_HEAD_DIM)
    ka = z[..., OFF_KA:OFF_VA].reshape(B, S, A_HEADS, A_HEAD_DIM)
    va = z[..., OFF_VA:OFF_QM].reshape(B, S, A_HEADS, A_HEAD_DIM)
    qm = z[..., OFF_QM:OFF_KM].reshape(B, S, M_HEADS, M_HEAD_DIM)
    km = z[..., OFF_KM:OFF_VM].reshape(B, S, M_HEADS, M_HEAD_DIM)
    vm = z[..., OFF_VM:OFF_OM].reshape(B, S, M_HEADS, M_HEAD_DIM)
    om = z[..., OFF_OM:OFF_G]
    gates = z[..., OFF_G:].astype(jnp.float32) + b_gates.astype(jnp.float32)
    i_pre = gates[..., :M_HEADS]
    f_pre = gates[..., M_HEADS:]
    if k_past is None:
        k_all, v_all = ka, va
    else:
        k_all = jnp.concatenate([k_past.astype(ka.dtype), ka], axis=1)
        v_all = jnp.concatenate([v_past.astype(va.dtype), va], axis=1)
    attn = moba_attention(qa, k_all, v_all, q_start).reshape(B, S, ATTN_WIDTH)
    h, C, n, m = mlstm_chunkwise(qm, km, vm, i_pre, f_pre, C0, n0, m0)
    h = h * lax.rsqrt(jnp.mean(h * h, axis=-1, keepdims=True) + RMS_EPS)
    h = h * mlstm_norm_w.astype(jnp.float32).reshape(M_HEADS, M_HEAD_DIM)
    h = (h.reshape(B, S, MLSTM_WIDTH) * jax.nn.sigmoid(om.astype(jnp.float32))).astype(x.dtype)
    mix = jnp.concatenate([attn.astype(x.dtype), h], axis=-1)
    x = x + mix @ w_out
    hn = rmsnorm(x, ln2_w)
    x = x + jnp.square(jax.nn.relu(hn @ w_up)) @ w_down
    return x, ka, va, C, n, m

def setup_inputs(seed: int = 0) -> dict:
    key = jax.random.key(seed)
    ks = jax.random.split(key, 20)
    f32 = jnp.float32
    n_pages = PAST_LEN // PAGE_SIZE
    n_phys = (DEC_BATCH * n_pages * 5) // 4
    nrm = jax.random.normal
    x_prompt = nrm(ks[0], (BATCH, SEQ, D_MODEL), f32)
    x_sample = nrm(ks[1], (DEC_BATCH, DEC_SEQ, D_MODEL), f32)
    cache_k = nrm(ks[2], (DEPTH, n_phys, PAGE_SIZE, A_HEADS, A_HEAD_DIM), f32)
    cache_v = nrm(ks[3], (DEPTH, n_phys, PAGE_SIZE, A_HEADS, A_HEAD_DIM), f32)
    page_table = jax.random.permutation(ks[4], n_phys)[:DEC_BATCH * n_pages].reshape(DEC_BATCH, n_pages).astype(jnp.int32)
    state_C = 2.0 * nrm(ks[5], (DEPTH, DEC_BATCH, M_HEADS, M_HEAD_DIM, M_HEAD_DIM), f32)
    state_n = 2.0 * nrm(ks[6], (DEPTH, DEC_BATCH, M_HEADS, M_HEAD_DIM), f32)
    state_m = nrm(ks[7], (DEPTH, DEC_BATCH, M_HEADS), f32)
    ln1_w = 1.0 + 0.05 * nrm(ks[8], (DEPTH, D_MODEL), f32)
    w_in = nrm(ks[9], (DEPTH, D_MODEL, IN_WIDTH), f32) * D_MODEL ** -0.5
    b_i = 0.1 * nrm(ks[10], (DEPTH, M_HEADS), f32)
    b_f = 3.0 + 0.5 * nrm(ks[11], (DEPTH, M_HEADS), f32)
    b_gates = jnp.concatenate([b_i, b_f], axis=-1)
    mlstm_norm_w = 1.0 + 0.05 * nrm(ks[12], (DEPTH, MLSTM_WIDTH), f32)
    w_out = nrm(ks[13], (DEPTH, ATTN_WIDTH + MLSTM_WIDTH, D_MODEL), f32) * D_MODEL ** -0.5
    ln2_w = 1.0 + 0.05 * nrm(ks[14], (DEPTH, D_MODEL), f32)
    w_up = nrm(ks[15], (DEPTH, D_MODEL, D_FF), f32) * D_MODEL ** -0.5
    w_down = nrm(ks[16], (DEPTH, D_FF, D_MODEL), f32) * D_FF ** -0.5
    lnf_w = 1.0 + 0.05 * nrm(ks[17], (D_MODEL,), f32)
    return {'x_prompt': x_prompt, 'x_sample': x_sample, 'cache_k': cache_k, 'cache_v': cache_v,
            'page_table': page_table, 'state_C': state_C, 'state_n': state_n, 'state_m': state_m,
            'ln1_w': ln1_w, 'w_in': w_in, 'b_gates': b_gates, 'mlstm_norm_w': mlstm_norm_w,
            'w_out': w_out, 'ln2_w': ln2_w, 'w_up': w_up, 'w_down': w_down, 'lnf_w': lnf_w}

def reference(x_prompt, x_sample, cache_k, cache_v, page_table, state_C, state_n, state_m,
              ln1_w, w_in, b_gates, mlstm_norm_w, w_out, ln2_w, w_up, w_down, lnf_w):
    Bp = x_prompt.shape[0]
    Bs = x_sample.shape[0]
    past_len = page_table.shape[1] * PAGE_SIZE
    xp, xs = x_prompt, x_sample
    kp_l, vp_l, Cp_l, np_l, mp_l = [], [], [], [], []
    ks_l, vs_l, Cs_l, ns_l, ms_l = [], [], [], [], []
    for l in range(DEPTH):
        lw = (ln1_w[l], w_in[l], b_gates[l], mlstm_norm_w[l], w_out[l], ln2_w[l], w_up[l], w_down[l])
        C0 = jnp.zeros((Bp, M_HEADS, M_HEAD_DIM, M_HEAD_DIM), jnp.float32)
        n0 = jnp.zeros((Bp, M_HEADS, M_HEAD_DIM), jnp.float32)
        m0 = jnp.zeros((Bp, M_HEADS), jnp.float32)
        xp, kp, vp, Cp, n_p, mp = hybrid_layer(xp, None, None, C0, n0, m0, 0, *lw)
        k_past = cache_k[l][page_table].reshape(Bs, past_len, A_HEADS, A_HEAD_DIM)
        v_past = cache_v[l][page_table].reshape(Bs, past_len, A_HEADS, A_HEAD_DIM)
        xs, ksm, vsm, Cs, n_s, ms = hybrid_layer(xs, k_past, v_past, state_C[l], state_n[l], state_m[l],
                                                 past_len, *lw)
        kp_l.append(kp); vp_l.append(vp); Cp_l.append(Cp); np_l.append(n_p); mp_l.append(mp)
        ks_l.append(ksm); vs_l.append(vsm); Cs_l.append(Cs); ns_l.append(n_s); ms_l.append(ms)
    y_prompt = rmsnorm(xp, lnf_w)
    y_sample = rmsnorm(xs, lnf_w)
    return (y_prompt, y_sample,
            jnp.stack(kp_l), jnp.stack(vp_l), jnp.stack(Cp_l), jnp.stack(np_l), jnp.stack(mp_l),
            jnp.stack(ks_l), jnp.stack(vs_l), jnp.stack(Cs_l), jnp.stack(ns_l), jnp.stack(ms_l))


_drawn_inputs = setup_inputs


def setup_inputs(seed=0):
    import zlib

    import numpy as np

    out = dict(_drawn_inputs(seed))
    spreads = {}
    factors = {'mlstm_norm_w': 2.926}
    for name, (base, spread) in spreads.items():
        noise = np.random.default_rng([zlib.crc32(name.encode()), seed]).standard_normal(out[name].shape)
        drawn = base * np.exp(spread * noise) if base else spread * noise
        out[name] = __import__('jax').numpy.asarray(drawn.astype(out[name].dtype))
    for name, factor in factors.items():
        out[name] = (out[name] * factor).astype(out[name].dtype)
    return out
```

```python
from contextlib import ExitStack

import numpy as np
import concourse.bass as bass
from concourse import mybir

ALU = mybir.AluOpType
ACT = mybir.ActivationFunctionType
AX = mybir.AxisListType
F32 = mybir.dt.float32
F32R = mybir.dt.float32r
I32 = mybir.dt.int32

P = 128
D = 1024
KT = D // P
SEQ = 512
NT = SEQ // P
NS = 8
TOK = SEQ + NS
HALF = TOK // 2
AH, AD = 8, 64
MH, MD = 4, 128
PAGES, PAGE = 8, 128
AW = AH * AD
EPS = 1e-6
MASKED = -1e30
ASCALE = AD ** -0.5
MSCALE = MD ** -0.5

QA, KA, VA, QM, KM, VM, OM = (4 * i for i in range(7))
GATE_COL = 28 * P
IN_ORDER = [c + t for c in (QA, QM, KM, VM, KA, VA, OM) for t in range(4)]
N_IN, N_OUT = 28, 8
G_OUT = N_IN
G_MLP = N_IN + N_OUT
QUARTERS = 4
N_MAIN = G_MLP + 16 * QUARTERS
WSLOTS = 4
AHEAD = 3

BASE = 16512


def made_at(g):
    return 2 * (g + 1)


def z_ready(c):
    return made_at(IN_ORDER.index(c))


def plan():
    tasks = [[] for _ in range(G_MLP)]

    def at(g, *names):
        tasks[g] += names

    at(1, ("rows",))
    at(2, ("gcols",))
    at(4, ("qs_tok",))
    at(5, ("qb", 0), ("qb", 1))
    chunk = 0
    for g in range(6, 22):
        for _ in range(2):
            b, c = divmod(chunk, 4)
            at(g, ("score", b, c))
            if c == 3 and b + 2 < NS:
                at(g, ("qb", b + 2))
            chunk += 1
    at(16, ("sm_prep",), ("vs_tok",), ("sm_c", 0), ("sm_c", 1), ("tok", VM, 0), ("tok", VM, 1), ("sm_r", 0))
    at(17, ("sm_r", 1), ("sm_c", 2), ("tok", VM, 2), ("tok", VM, 3), ("sm_c", 3), ("sm_r", 2),
       ("tok", KM, 0), ("tok", KM, 1))
    at(18, ("sm_r", 3), ("sm_c", 4), ("tok", KM, 2), ("tok", KM, 3), ("sm_c", 5), ("sm_r", 4), ("ml_a", 0))
    at(19, ("sm_r", 5), ("sm_c", 6), ("sm_c", 7), ("sm_r", 6), ("ml_a", 1), ("ml_o", 0), ("sm_r", 7))
    at(20, ("sm_den",), ("ml_a", 2), ("ml_t", 0), ("ml_o", 1))
    at(21, ("tok", KA, 0), ("tok", KA, 1), ("sm_out",), ("ml_a", 3), ("ml_t", 1), ("ml_o", 2))
    at(22, ("tok", KA, 2), ("tok", KA, 3), ("ml_t", 2), ("ml_o", 3))
    at(23, ("gate",), ("ml_t", 3), ("ml_mc", 0), ("ml_mc", 1))
    at(24, ("mx_t",), ("own",), ("ml_mc", 2), ("ml_mc", 3), ("ks_tok",), ("tok", VA, 0), ("tok", VA, 1),
       ("tok", VA, 2), ("tok", VA, 3), ("va_s",), ("om", 0))
    at(25, ("mx_b",), ("att_s", 0), ("om", 1))
    at(26, ("zsum",), ("att_s", 1), ("att_t", 0), ("att_o", 0), ("pv", 0), ("om", 2))
    at(27, ("om", 3))
    for h in range(2, AH + 1):
        if h < AH:
            at(27, ("att_s", h))
        at(27, ("att_t", h - 1), ("pv", h - 1), ("att_o", h - 1))
    at(27, ("pv_end",))
    for j in range(KT):
        at(27, ("mix", j))
    for j in range(KT):
        at(G_OUT + j // 2, ("xt", j))
    at(G_OUT, ("xt_s",))
    at(33, ("ss", 0), ("ss", 1), ("ss", 2))
    at(34, ("ss", 3), ("ss", 4), ("ss", 5))
    at(35, ("ss", 6), ("ss", 7), ("rstd2",))

    scratch = {
        "gcols": 1, "qs_tok": 1, "qb": 1, "vs_tok": 1, "tok": 1, "sm_prep": 2, "sm_c": 1, "sm_r": 1, "ml_a": 4,
        "ml_o": 2, "ml_t": 1, "ml_mc": 1, "sm_den": 1, "sm_out": 2, "ks_tok": 1, "gate": 1, "mx_t": 1,
        "own": 1, "va_s": 1, "mx_b": 1, "zsum": 1, "att_s": 3, "att_t": 4, "att_o": 1, "pv": 1, "xt": 1,
        "xt_s": 1,
    }
    jobs = {}

    def job(*key):
        jobs[key] = len(jobs)

    job("param", 0)
    for j in range(KT + 1):
        job("xn", j)
    job("gates", 0)
    job("gates", 1)
    for names in tasks:
        for name in names:
            n = scratch.get(name[0], 0)
            if name[0] == "att_o" and name[1] % 2 == 1:
                n = 2
            if name[0] == "ss" and name[1] == 0:
                n = 2
            for i in range(n):
                job(*name, i)
    for i in range(NT + 1):
        job("yt", i, 0)
        job("yt", i, 1)
    return tasks, jobs


TASKS, JOBS = plan()


def build(nc, x_prompt, x_sample, cache_k, cache_v, page_table, state_C, state_n, state_m, ln1_w, w_in,
          b_gates, mlstm_norm_w, w_out, ln2_w, w_up, w_down, lnf_w, y_prompt, y_sample, k_prompt, v_prompt,
          C_prompt, n_prompt, m_prompt, k_sample, v_sample, C_sample, n_sample, m_sample):
    n_phys = cache_k.shape[1]
    ctx = ExitStack()
    with ctx:
        ctx.enter_context(nc.allow_non_contiguous_dma(reason="a few hundred elements of gates and states"))
        end = [BASE]

        def place(name, shape, dt=F32, at=None):
            size = 4
            for n in shape[1:]:
                size *= n
            off = end[0] if at is None else at
            t = nc.alloc_sbuf_tensor_at(name, shape, dt, offset=off)
            if at is None:
                end[0] = off + (size + 31) // 32 * 32
            return t, off

        raw, _ = place("raw", [P, 2, KT, 2 * P])
        w_hi, _ = place("w_hi", [P, WSLOTS, KT, P], F32R)
        w_lo, _ = place("w_lo", [P, WSLOTS, KT, P], F32R)
        act_hi, _ = place("act_hi", [P, KT, TOK], F32R)
        act_lo, _ = place("act_lo", [P, KT, TOK], F32R)
        zT, z_at = place("zT", [P, N_IN, TOK])
        h_hi, _ = place("h_hi", [P, KT, TOK], F32R, at=z_at)
        h_lo, _ = place("h_lo", [P, KT, TOK], F32R, at=z_at + 4 * KT * TOK)
        tail_at = z_at + 4 * 2 * KT * TOK
        relu, _ = place("relu", [P, 2, TOK], at=tail_at)
        relu2, _ = place("relu2", [P, 2, TOK], at=tail_at + 4 * 2 * TOK)
        rstd2, _ = place("rstd2", [P, TOK], at=tail_at + 4 * 4 * TOK)
        x_sq, _ = place("x_sq", [P, 2, TOK], at=tail_at + 4 * 5 * TOK)
        y_out, _ = place("y_out", [P, 2, D], at=z_at)
        y_junk, _ = place("y_junk", [P, 512], at=z_at + 4 * 2 * D)
        km_tok, _ = place("km_tok", [P, NT, AW], at=z_at + 4 * VM * TOK)
        om_at = z_at + 4 * OM * TOK
        qs_tok, _ = place("qs_tok", [NS, AW], at=om_at)
        vs_tok, _ = place("vs_tok", [NS, AW], at=om_at + 4 * AW)
        k_stage, _ = place("k_stage", [P, 2, AW], at=om_at + 8 * AW)
        xT, x_at = place("xT", [P, KT, TOK])
        rows, _ = place("rows", [4, 6, TOK], at=x_at)
        att = 1280
        mA, _ = place("mA", [P, 2, att], at=x_at)
        m_h, _ = place("m_h", [P, NT, MD], at=x_at + 8 * att)
        m_kw, _ = place("m_kw", [P, NT, MD], at=x_at + 8 * att + 2048)
        sm_at = x_at + 8 * att + 4096
        sm_b, _ = place("sm_b", [P, MH, 3, NS], at=sm_at)
        sm_kw, _ = place("sm_kw", [P, MH, NS], at=sm_at + 384)
        sm_n, _ = place("sm_n", [P, NS, MH], at=sm_at + 512)
        sm_q, _ = place("sm_q", [P, NS, MH], at=sm_at + 640)
        sm_h, _ = place("sm_h", [P, NS, MH], at=sm_at + 768)
        sm_t, _ = place("sm_t", [P, NS, MH], at=sm_at + 896)
        n_rows, _ = place("n_rows", [NS * MH, MD], at=sm_at + 1024)
        n_new_rows, _ = place("n_new_rows", [NS * MH, MD], at=sm_at + 1536)
        pr, _ = place("pr", [P, 2, att], at=x_at)
        pT, _ = place("pT", [P, att], at=x_at + 8 * att)
        kv, kv_at = place("kv", [P, PAGES, AW])
        x_tok, _ = place("x_tok", [P, NT, D], at=kv_at)
        x_tok2, _ = place("x_tok2", [P, NT, D], at=kv_at)
        prod, prod_at = place("prod", [P, 2, 2 * AW])
        x_s, _ = place("x_s", [NS, D], at=prod_at)
        x_s2, _ = place("x_s2", [NS, D], at=prod_at)
        att_tok, _ = place("att_tok", [P, NT, P], at=prod_at)
        C_stage, _ = place("C_stage", [P, MH, MD], at=prod_at + 2048)
        junk, _ = place("junk", [P, D], at=x_at)
        lnf_b, _ = place("lnf_b", [P, D], at=prod_at + 4096)
        t_at = prod_at + 4096
        gate, _ = place("gate", [P, NS, 4, AH], at=t_at)
        gate_min, _ = place("gate_min", [P, NS, AH], at=t_at + 1024)
        taken, _ = place("taken", [P, NS, AH], at=t_at + 1280)
        page_max, _ = place("page_max", [P, NS, AH], at=t_at + 1536)
        own, _ = place("own", [P, NS, AH], at=t_at + 1792)
        smax, _ = place("smax", [P, NS, AH], at=t_at + 2048)
        own_p, _ = place("own_p", [P, NS, AH], at=t_at + 2304)
        zrec, _ = place("zrec", [P, NS, AH], at=t_at + 2560)
        pv_s, _ = place("pv_s", [P, NS, AH], at=t_at + 2816)
        own_prod, _ = place("own_prod", [P, 4, NS], at=t_at + 3072)
        mx_col, _ = place("mx_col", [NS * AH, 1], at=t_at + 3200)
        v_tok, _ = place("v_tok", [P, NT, AW])
        vm_tok, vm_at = place("vm_tok", [P, NT, MH, MD + 1])
        wg_hi, _ = place("wg_hi", [P, KT, P], F32R, at=vm_at)
        wg_lo, _ = place("wg_lo", [P, KT, P], F32R, at=vm_at + 4 * D)
        cs_at = z_at + 4 * VA * TOK
        Cs, _ = place("Cs", [P, 4, MH, MD], at=cs_at)
        par_rows, _ = place("par_rows", [20, P], at=cs_at)
        wg_raw, _ = place("wg_raw", [P, KT, 8], at=cs_at + 512)
        xn_s, _ = place("xn_s", [P, KT, NS], at=cs_at + 768)
        S, _ = place("S", [P, NS, PAGES, AH])
        Qb, _ = place("Qb", [P, 2, AW])
        M_row, _ = place("M_row", [4, TOK])
        ident, _ = place("ident", [P, P])
        causal, _ = place("causal", [P, P])
        ones, _ = place("ones", [P, 1])
        even, _ = place("even", [P, 2])
        par, _ = place("par", [P, 20])
        ss, _ = place("ss", [P, 8])
        rs, _ = place("rs", [P, 8])
        power, _ = place("power", [P, 1])
        g_col, _ = place("g_col", [P, 2, NT, MH])
        MS, _ = place("MS", [P, MH])
        w_end, _ = place("w_end", [P, MH, NT])
        m_den, _ = place("m_den", [P, NT])
        m_ss, _ = place("m_ss", [P, NT])
        m_rs, _ = place("m_rs", [P, NT])
        m_s, _ = place("m_s", [4, NS])
        y_ss, _ = place("y_ss", [P, NT + 1, 2])
        y_ms, _ = place("y_ms", [P, NT + 1])
        y_rs, _ = place("y_rs", [P, NT + 1])
        nc_col, _ = place("nc_col", [P, MH])
        rmax, _ = place("rmax", [P, 2, NT])
        nmax, _ = place("nmax", [P, 2, NT])
        rsum, _ = place("rsum", [P, 2, NT])
        rrec, _ = place("rrec", [P, 2, NT])
        bias_i, _ = place("bias_i", [4, 1])
        bias_f, _ = place("bias_f", [P, 1])
        m0_row, _ = place("m0_row", [4, NS])
        s_rows, _ = place("s_rows", [4, 3, NS])
        pt, _ = place("pt", [1, NS * PAGES], I32)
        assert end[0] <= nc.sbuf_usable_end, (end[0], nc.sbuf_usable_end)

        acc = ctx.enter_context(nc.psum_tensor("acc", [P, 4, 512], F32))
        scr = ctx.enter_context(nc.psum_tensor("scr", [P, 4, 512], F32))

        def sem(name):
            return ctx.enter_context(nc.semaphore(name))

        s_x_in0 = sem("x_in0")
        s_x_in1 = sem("x_in1")
        s_x_in2 = sem("x_in2")
        s_x_in3 = sem("x_in3")
        s_x_in4 = sem("x_in4")
        s_par_in = sem("par_in")
        s_wg_in = sem("wg_in")
        s_small_in = sem("small_in")
        s_n_in = sem("n_in")
        s_pt_in = sem("pt_in")
        s_raw0 = sem("raw0")
        s_raw1 = sem("raw1")
        s_x2_in = sem("x2_in")
        s_x2s_in = sem("x2s_in")
        s_lnf_in = sem("lnf_in")
        s_C_in0 = sem("C_in0")
        s_C_in1 = sem("C_in1")
        s_C_in2 = sem("C_in2")
        s_C_in3 = sem("C_in3")
        s_C_out0 = sem("C_out0")
        s_C_out1 = sem("C_out1")
        s_C_out2 = sem("C_out2")
        s_C_out3 = sem("C_out3")
        s_k_out0 = sem("k_out0")
        s_k_out1 = sem("k_out1")
        s_ident_ok = sem("ident_ok")
        s_ones_ok = sem("ones_ok")
        s_causal_ok = sem("causal_ok")
        s_wg_zero = sem("wg_zero")
        s_wg_hi_ok = sem("wg_hi_ok")
        s_wg_lo_ok = sem("wg_lo_ok")
        s_x_sq_ok = sem("x_sq_ok")
        s_x_ms_ok = sem("x_ms_ok")
        s_x_rs_ok = sem("x_rs_ok")
        s_xn_ready = sem("xn_ready")
        s_xhi_ok = sem("xhi_ok")
        s_xs_ok = sem("xs_ok")
        s_w_hi_ok = sem("w_hi_ok")
        s_w_lo_ok = sem("w_lo_ok")
        s_half_done = sem("half_done")
        s_acc_evac = sem("acc_evac")
        s_scr_full = sem("scr_full")
        s_f_abs = sem("f_abs")
        s_f_log = sem("f_log")
        s_m_ok = sem("m_ok")
        s_srow_ok = sem("srow_ok")
        s_rows_ok = sem("rows_ok")
        s_srow_exp = sem("srow_exp")
        s_vm_ones = sem("vm_ones")
        s_kmul_ok = sem("kmul_ok")
        s_kred_ok = sem("kred_ok")
        s_samp_dve = sem("samp_dve")
        s_samp_sub = sem("samp_sub")
        s_samp_exp = sem("samp_exp")
        s_pv_end_ok = sem("pv_end_ok")
        s_sm_b_ok = sem("sm_b_ok")
        s_C_decayed = sem("C_decayed")
        s_sm_dve = sem("sm_dve")
        s_sm_pow = sem("sm_pow")
        s_sm_end = sem("sm_end")
        s_ml_tri = sem("ml_tri")
        s_ml_ms = sem("ml_ms")
        s_ml_pow = sem("ml_pow")
        s_ml_hr = sem("ml_hr")
        s_ml_wend = sem("ml_wend")
        s_ml_kw = sem("ml_kw")
        s_att_nmax = sem("att_nmax")
        s_om_exp = sem("om_exp")
        s_gated = sem("gated")
        s_mix_hi = sem("mix_hi")
        s_mix_lo = sem("mix_lo")
        s_x1_sq = sem("x1_sq")
        s_sq_read = sem("sq_read")
        s_rstd_ok = sem("rstd_ok")
        s_x2_hi = sem("x2_hi")
        s_x2_lo = sem("x2_lo")
        s_hs_hi = sem("hs_hi")
        s_hs_lo = sem("hs_lo")
        s_y_sq = sem("y_sq")
        s_y_ms_ok = sem("y_ms_ok")
        s_y_pow = sem("y_pow")
        s_out_v = sem("out_v")
        s_out_small = sem("out_small")
        s_out_C = sem("out_C")
        s_y_st0 = sem("y_st0")
        s_y_st1 = sem("y_st1")
        s_dve_chain = sem("dve_chain")
        s_act_chain = sem("act_chain")
        s_pool_chain = sem("pool_chain")
        scr_free = [sem(f"scr_free{i}") for i in range(4)]
        kv_in = [sem(f"kv_in{i}") for i in range(PAGES)]
        raw_in = [s_raw0, s_raw1]
        x_in = [s_x_in0, s_x_in1, s_x_in2, s_x_in3, s_x_in4]
        C_in = [s_C_in0, s_C_in1, s_C_in2, s_C_in3]
        C_out = [s_C_out0, s_C_out1, s_C_out2, s_C_out3]
        k_out = [s_k_out0, s_k_out1]
        st_y = [s_y_st0, s_y_st1]

        def bank(*key):
            return scr[:, JOBS[key] % 4, :]

        def open_job(pe, *key):
            n = JOBS[key]
            if n >= 4:
                pe.wait_ge(scr_free[n % 4], n // 4)
            return scr[:, n % 4, :]

        def full(eng, *key):
            eng.wait_ge(s_scr_full, JOBS[key] + 1)
            return bank(*key)

        def free(ins, *key):
            ins.then_inc(scr_free[JOBS[key] % 4], 1)

        def evacuated(eng, *key):
            n = JOBS[key]
            eng.wait_ge(scr_free[n % 4], n // 4 + 1)

        def lookahead(g):
            return g + AHEAD if g + AHEAD < N_MAIN else None

        block = ctx.enter_context(nc.Block())

        A_COL = [0, 512, 896, 1152]
        P_COL = [0, 128, 384, 768]

        @block.sync
        def _(sp):
            for i in range(NT):
                sp.dma_start(x_tok[:, i, :], x_prompt[0, i * P:(i + 1) * P, :]).then_inc(x_in[i], 16)

            def unit(r, src, first=True):
                if r >= 2:
                    sp.wait_ge(s_w_lo_ok, 2 * (r - 1))
                sp.dma_start(raw[:, r % 2, :, :], src.rearrange("(k p) n -> p k n", p=P))\
                  .then_inc(raw_in[r % 2], 16)

            def in_unit(r):
                c = IN_ORDER[2 * r] * P
                unit(r, w_in[0, :, c:c + 2 * P])

            def pages(cache, b, step):
                for j in range(PAGES):
                    page = sp.value_load(pt[0:1, b * PAGES + j:b * PAGES + j + 1], min_val=0, max_val=n_phys - 1)
                    if 1 <= step <= NS:
                        sp.wait_ge(s_kmul_ok, 4 * (step - 1) + j // 2 + 1)
                    elif step > NS:
                        evacuated(sp, "pv", b - 1, 0)
                    src = cache[0, bass.ds(page, 1), :, :, :].rearrange("o p h d -> p (o h d)")
                    sp.dma_start(kv[:, j, :], src).then_inc(kv_in[j], 16)

            in_unit(0)
            in_unit(1)
            sp.wait_ge(s_pt_in, 16)
            evacuated(sp, "xn", KT - 1)
            evacuated(sp, "xn", KT)
            pages(cache_k, 0, 0)
            for r in range(2, 14):
                in_unit(r)
                if 1 <= r - 5 < NS:
                    pages(cache_k, r - 5, r - 5)
                elif r - 5 == NS:
                    pages(cache_v, 0, NS)
            unit(14, w_out[0, :, 0:2 * P])
            unit(15, w_out[0, :, 2 * P:4 * P])
            for b in range(1, NS):
                pages(cache_v, b, NS + b)
            evacuated(sp, "pv", NS - 1, 0)
            for i in range(NT):
                sp.dma_start(x_tok2[:, i, :], x_prompt[0, i * P:(i + 1) * P, :]).then_inc(s_x2_in, 16)
            evacuated(sp, "att_o", AH - 1, 1)
            sp.wait_ge(s_out_C, 16 * (MH + 1))
            sp.dma_start(x_s2[:, :], x_sample[:, 0, :]).then_inc(s_x2s_in, 16)
            sp.wait_ge(s_pv_end_ok, 2)
            sp.dma_start(lnf_b[:, :], lnf_w.rearrange("(o n) -> o n", o=1).broadcast_to([P, D])
                         ).then_inc(s_lnf_in, 16)
            for r in range(16, 18):
                unit(r, w_out[0, :, (r - 14) * 2 * P:(r - 13) * 2 * P])

            def mlp(i):
                for u in range(8):
                    r = 18 + 8 * i + u
                    sp.wait_ge(s_w_lo_ok, 2 * (r - 1))
                    if u < 4:
                        src = w_up[0, :, bass.ds(i * D + u * 2 * P, 2 * P)]
                    else:
                        src = w_down[0, bass.ds(i * D, D), (u - 4) * 2 * P:(u - 3) * 2 * P]
                    sp.dma_start(raw[:, u % 2, :, :], src.rearrange("(k p) n -> p k n", p=P))\
                      .then_inc(raw_in[u % 2], 16)

            with sp.Fori(0, QUARTERS) as i:
                mlp(i)
            for i in range(NT + 1):
                evacuated(sp, "yt", i, 0)
                evacuated(sp, "yt", i, 1)
                if i < NT:
                    sp.dma_start(y_prompt[0, i * P:(i + 1) * P, :], y_out[:, i % 2, :]).then_inc(st_y[i % 2], 16)
                else:
                    sp.dma_start(y_sample[:, 0, :], y_out[0:NS, i % 2, :]).then_inc(st_y[i % 2], 16)
            sp.wait_ge(s_y_st0, 48)
            sp.wait_ge(s_y_st1, 32)

        @block.tensor
        def _(pe):
            def main(g, slot, side, hi, lo, k_ready=None):
                pe.wait_ge(s_w_lo_ok, g + 1)
                for half in range(2):
                    cols = slice(half * HALF, (half + 1) * HALF)
                    if not isinstance(g, int) or g >= 2:
                        pe.wait_ge(s_acc_evac, 2 * (g - 2) + half + 1)
                    out = acc[:, 2 * side + half, 0:HALF]
                    for k in range(KT):
                        if half == 0 and k_ready is not None:
                            k_ready(k)
                        pe.matmul(out, w_hi[:, slot, k, :], hi[:, k, cols], start=(k == 0), stop=False)
                        pe.matmul(out, w_hi[:, slot, k, :], lo[:, k, cols], start=False, stop=False)
                        mm = pe.matmul(out, w_lo[:, slot, k, :], hi[:, k, cols], start=False,
                                       stop=(k == KT - 1))
                    mm.then_inc(s_half_done, 1)

            def done(mm):
                mm.then_inc(s_scr_full, 1)

            def to_tok(key, tiles, cols, n):
                out = open_job(pe, *key)
                for t in range(4):
                    mm = pe.transpose(out[0:n, t * P:(t + 1) * P], zT[:, tiles + t, cols], ident[:, :])
                done(mm)

            def every(col, n=P):
                return col.to_broadcast([n, P])

            pe.wait_ge(s_ident_ok, 3)
            pe.wait_ge(s_par_in, 48)
            out = open_job(pe, "param", 0)
            done(pe.transpose(out[:, 0:20], par_rows[:, :], ident[0:20, 0:20]))
            for j in range(KT):
                out = open_job(pe, "xn", j)
                for i in range(NT):
                    if j == 0:
                        pe.wait_ge(s_xn_ready, i + 1)
                    mm = pe.transpose(out[:, i * P:(i + 1) * P], x_tok[:, i, j * P:(j + 1) * P], ident[:, :])
                done(mm)
            out = open_job(pe, "xn", KT)
            pe.wait_ge(s_xn_ready, NT + 1)
            for j in range(KT):
                mm = pe.transpose(out[:, j * NS:(j + 1) * NS], x_s[:, j * P:(j + 1) * P], ident[0:NS, 0:NS])
            done(mm)
            pe.wait_ge(s_wg_lo_ok, 2)
            for j in range(KT):
                evacuated(pe, "xn", j)
            pe.wait_ge(s_xs_ok, 1)
            for half in range(2):
                cols = slice(half * HALF, (half + 1) * HALF)
                out = open_job(pe, "gates", half)[:, 0:HALF]
                for k in range(KT):
                    pe.matmul(out, wg_hi[:, k, :], act_hi[:, k, cols], start=(k == 0), stop=False)
                    pe.matmul(out, wg_hi[:, k, :], act_lo[:, k, cols], start=False, stop=False)
                    mm = pe.matmul(out, wg_lo[:, k, :], act_hi[:, k, cols], start=False, stop=(k == KT - 1))
                done(mm)

            def task(name, *a):
                if name == "gcols":
                    pe.wait_ge(s_rows_ok, 1)
                    out = open_job(pe, "gcols", 0)
                    for r, row in enumerate((3, 5)):
                        for i in range(NT):
                            mm = pe.transpose(out[:, (r * NT + i) * MH:(r * NT + i + 1) * MH],
                                              rows[:, row, i * P:(i + 1) * P], ident[0:4, 0:4])
                    done(mm)
                elif name == "qs_tok":
                    pe.wait_ge(s_acc_evac, z_ready(QA + 3))
                    to_tok(("qs_tok", 0), QA, slice(SEQ, TOK), NS)
                elif name == "vs_tok":
                    pe.wait_ge(s_acc_evac, z_ready(VM + 3))
                    to_tok(("vs_tok", 0), VM, slice(SEQ, TOK), NS)
                elif name == "ks_tok":
                    to_tok(("ks_tok", 0), KA, slice(SEQ, TOK), NS)
                elif name == "va_s":
                    to_tok(("va_s", 0), VA, slice(SEQ, TOK), NS)
                elif name == "tok":
                    group, i = a
                    pe.wait_ge(s_acc_evac, z_ready(group + 3))
                    to_tok(("tok", group, i, 0), group, slice(i * P, (i + 1) * P), P)
                elif name == "qb":
                    b, = a
                    evacuated(pe, "qs_tok", 0)
                    out = open_job(pe, "qb", b, 0)
                    done(pe.matmul(out, every(ident[0:NS, b:b + 1], NS), qs_tok[:, :], start=True, stop=True))
                elif name == "sm_prep":
                    out = open_job(pe, "sm_prep", 0)
                    for h in range(MH):
                        mm = pe.matmul(out[:, h * 3 * NS:(h + 1) * 3 * NS], every(ident[0:4, h:h + 1], 4),
                                       s_rows[:, :, :].rearrange("p a b -> p (a b)"), start=True, stop=True)
                    done(mm)
                    pe.wait_ge(s_n_in, 16)
                    out = open_job(pe, "sm_prep", 1)
                    done(pe.transpose(out[:, 0:NS * MH], n_rows[:, :], ident[0:NS * MH, 0:NS * MH]))
                elif name == "sm_c":
                    b, = a
                    evacuated(pe, "vs_tok", 0)
                    out = open_job(pe, "sm_c", b, 0)
                    done(pe.matmul(out, every(ident[0:NS, b:b + 1], NS), vs_tok[:, :], start=True, stop=True))
                elif name == "sm_r":
                    b, = a
                    evacuated(pe, "sm_c", b, 0)
                    out = open_job(pe, "sm_r", b, 0)
                    for h in range(MH):
                        mm = pe.matmul(out[:, h:h + 1], Cs[:, b % 4, h, :], zT[:, QM + h, SEQ + b:SEQ + b + 1],
                                       start=True, stop=True)
                    done(mm)
                elif name == "sm_den":
                    pe.wait_ge(s_sm_dve, 1)
                    out = open_job(pe, "sm_den", 0)
                    done(pe.matmul(out[:, 0:NS * MH], every(ones[:, :]), sm_q[:, :, :].rearrange("p a b -> p (a b)"),
                                   start=True, stop=True))
                elif name == "sm_out":
                    pe.wait_ge(s_sm_dve, 2)
                    out = open_job(pe, "sm_out", 0)
                    done(pe.matmul(out[:, 0:NS * MH], every(ones[:, :]), sm_t[:, :, :].rearrange("p a b -> p (a b)"),
                                   start=True, stop=True))
                    out = open_job(pe, "sm_out", 1)
                    done(pe.transpose(out[0:NS * MH, 0:P], sm_n[:, :, :].rearrange("p a b -> p (a b)"), ident[:, :]))
                elif name == "ml_a":
                    h, = a
                    out = open_job(pe, "ml_a", h, 0)
                    done(pe.matmul(out, every(ident[0:4, h:h + 1], 4), M_row[:, 0:SEQ], start=True, stop=True))
                    for n, parts in enumerate(((0,), (1,), (2, 3))):
                        out = open_job(pe, "ml_a", h, n + 1)
                        col = 0
                        for j in parts:
                            w = SEQ - j * P
                            mm = pe.matmul(out[:, col:col + w], zT[:, KM + h, j * P:(j + 1) * P],
                                           zT[:, QM + h, j * P:SEQ], start=True, stop=True)
                            col += w
                        done(mm)
                elif name == "ml_o":
                    h, = a
                    if h == 0:
                        for i in range(NT):
                            evacuated(pe, "tok", VM, i, 0)
                    for n in range(3):
                        evacuated(pe, "ml_a", h, n + 1)
                    for half in range(2):
                        out = open_job(pe, "ml_o", h, half)
                        for n, i in enumerate((2 * half, 2 * half + 1)):
                            for j in range(i + 1):
                                mm = pe.matmul(out[:, n * (MD + 1):(n + 1) * (MD + 1)],
                                               mA[:, h % 2, A_COL[j] + (i - j) * P:A_COL[j] + (i - j + 1) * P],
                                               vm_tok[:, j, h, :], start=(j == 0), stop=(j == i))
                        done(mm)
                elif name == "ml_t":
                    h, = a
                    pe.wait_ge(s_ml_hr, h + 1)
                    out = open_job(pe, "ml_t", h, 0)
                    for i in range(NT):
                        mm = pe.transpose(out[:, i * P:(i + 1) * P], m_h[:, i, :], ident[:, :])
                    done(mm)
                elif name == "ml_mc":
                    h, = a
                    pe.wait_ge(s_ml_kw, h + 1)
                    out = open_job(pe, "ml_mc", h, 0)
                    for j in range(NT):
                        mm = pe.matmul(out[:, 0:MD + 1], m_kw[:, j, :], vm_tok[:, j, h, :],
                                       start=(j == 0), stop=(j == NT - 1))
                    done(mm)
                elif name == "gate":
                    pe.wait_ge(s_kred_ok, 4 * NS)
                    out = open_job(pe, "gate", 0)
                    done(pe.matmul(out, every(ones[:, :]), S[:, :, :, :].rearrange("p b g h -> p (b g h)"),
                                   start=True, stop=True))
                elif name == "mx_t":
                    pe.wait_ge(s_samp_dve, 1)
                    out = open_job(pe, "mx_t", 0)
                    done(pe.transpose(out[0:NS * AH, 0:P], page_max[:, :, :].rearrange("p b h -> p (b h)"),
                                      ident[:, :]))
                elif name == "own":
                    pe.wait_ge(s_samp_dve, 2)
                    out = open_job(pe, "own", 0)
                    for odd in range(2):
                        mm = pe.matmul(out[:, odd * 32:(odd + 1) * 32], every(even[:, odd:odd + 1]),
                                       own_prod[:, :, :].rearrange("p t b -> p (t b)"), start=True, stop=True)
                    done(mm)
                elif name == "mx_b":
                    evacuated(pe, "mx_t", 0)
                    out = open_job(pe, "mx_b", 0)
                    done(pe.matmul(out[:, 0:NS * AH], every(mx_col[:, :], NS * AH), ident[0:NS * AH, 0:NS * AH],
                                   start=True, stop=True))
                elif name == "zsum":
                    pe.wait_ge(s_samp_dve, 3)
                    out = open_job(pe, "zsum", 0)
                    done(pe.matmul(out[:, 0:NS * AH], every(ones[:, :]),
                                   page_max[:, :, :].rearrange("p b h -> p (b h)"), start=True, stop=True))
                elif name == "pv":
                    b, = a
                    pe.wait_ge(s_samp_exp, 1)
                    for j in range(PAGES):
                        pe.wait_ge(kv_in[j], 16 * (NS + b + 1))
                    out = open_job(pe, "pv", b, 0)
                    for t in range(4):
                        for j in range(PAGES):
                            mm = pe.matmul(out[:, 2 * t:2 * t + 2], kv[:, j, t * P:(t + 1) * P],
                                           S[:, b, j, 2 * t:2 * t + 2], start=(j == 0), stop=(j == PAGES - 1))
                    done(mm)
                elif name == "att_s":
                    h, = a
                    t, lo = h // 2, 64 * (h % 2)
                    for n, parts in enumerate(((0, 1), (2,), (3,))):
                        out = open_job(pe, "att_s", h, n)
                        col = 0
                        for i in parts:
                            w = (i + 1) * P
                            mm = pe.matmul(out[:, col:col + w], zT[lo:lo + 64, QA + t, i * P:(i + 1) * P],
                                           zT[lo:lo + 64, KA + t, 0:w], start=True, stop=True)
                            col += w
                        done(mm)
                elif name == "att_t":
                    h, = a
                    for n in range(3):
                        evacuated(pe, "att_s", h, n)
                    for j in range(NT):
                        out = open_job(pe, "att_t", h, j)
                        for i in range(j, NT):
                            mm = pe.transpose(out[:, (i - j) * P:(i - j + 1) * P],
                                              pr[:, h % 2, P_COL[i] + j * P:P_COL[i] + (j + 1) * P], ident[:, :])
                        done(mm)
                elif name == "att_o":
                    h, = a
                    if h == 0:
                        for i in range(NT):
                            evacuated(pe, "tok", VA, i, 0)
                    for j in range(NT):
                        evacuated(pe, "att_t", h, j)
                    out = open_job(pe, "att_o", h, 0)
                    for i in range(NT):
                        for j in range(i + 1):
                            mm = pe.matmul(out[:, i * AD:(i + 1) * AD],
                                           pT[:, A_COL[j] + (i - j) * P:A_COL[j] + (i - j + 1) * P],
                                           v_tok[:, j, h * AD:(h + 1) * AD], start=(j == 0), stop=(j == i))
                    done(mm)
                    if h % 2 == 1:
                        evacuated(pe, "att_o", h, 0)
                        evacuated(pe, "att_o", h - 1, 0)
                        out = open_job(pe, "att_o", h, 1)
                        for i in range(NT):
                            mm = pe.transpose(out[:, i * P:(i + 1) * P], att_tok[:, i, :], ident[:, :])
                        done(mm)
                elif name == "xt":
                    j, = a
                    pe.wait_ge(s_x2_in, 16 * NT)
                    out = open_job(pe, "xt", j, 0)
                    for i in range(NT):
                        mm = pe.transpose(out[:, i * P:(i + 1) * P], x_tok2[:, i, j * P:(j + 1) * P], ident[:, :])
                    done(mm)
                elif name == "xt_s":
                    pe.wait_ge(s_x2s_in, 16)
                    out = open_job(pe, "xt_s", 0)
                    for j in range(KT):
                        mm = pe.transpose(out[:, j * NS:(j + 1) * NS], x_s2[:, j * P:(j + 1) * P],
                                          ident[0:NS, 0:NS])
                    done(mm)
                elif name == "ss":
                    j, = a
                    if j == 0:
                        open_job(pe, "ss", 0, 0)
                        open_job(pe, "ss", 0, 1)
                    pe.wait_ge(s_x1_sq, j + 1)
                    for half in range(2):
                        mm = pe.matmul(bank("ss", 0, half)[:, 0:HALF], every(ones[:, :]),
                                       x_sq[:, j % 2, half * HALF:(half + 1) * HALF], start=(j == 0),
                                       stop=(j == KT - 1))
                        if j == KT - 1:
                            done(mm)
                        elif half == 1:
                            mm.then_inc(s_sq_read, 1)

            for g in range(N_IN):
                main(g, g % WSLOTS, g % 2, act_hi, act_lo)
                for name in TASKS[g]:
                    task(*name)
            for g in range(G_OUT, G_MLP):
                def mixed(k):
                    pe.wait_ge(s_mix_lo, k + 1)
                main(g, g % WSLOTS, g % 2, act_hi, act_lo, mixed if g == G_OUT else None)
                for name in TASKS[g]:
                    task(*name)

            def quarter(i, first):
                for t in range(16):
                    g = G_MLP + 16 * i + t
                    if t < 8:
                        def normed(k):
                            pe.wait_ge(s_x2_lo, k + 1)
                        main(g, t % WSLOTS, t % 2, act_hi, act_lo, normed if first and t == 0 else None)
                    else:
                        def hidden(k):
                            pe.wait_ge(s_hs_lo, 8 * i + k + 1)
                        main(g, t % WSLOTS, t % 2, h_hi, h_lo, hidden if t == 8 else None)

            quarter(0, True)
            with pe.Fori(1, QUARTERS) as i:
                quarter(i, False)
            pe.wait_ge(s_acc_evac, 2 * N_MAIN)
            for i in range(NT + 1):
                n = P if i < NT else NS
                for part in range(2):
                    out = open_job(pe, "yt", i, part)
                    for j in range(4):
                        mm = pe.transpose(out[0:n, j * P:(j + 1) * P],
                                          xT[:, 4 * part + j, i * P:i * P + n], ident[:, :])
                    done(mm)

        def weight_hi(act, g, slot, r_slot, r_round):
            act.wait_ge(raw_in[r_slot], 16 * (r_round + 1))
            if not isinstance(g, int) or g >= WSLOTS:
                act.wait_ge(s_half_done, 2 * (g - WSLOTS + 1))
            side = slot % 2
            act.activation(w_hi[:, slot, :, :], raw[:, r_slot, :, side * P:(side + 1) * P], ACT.Copy)\
               .then_inc(s_w_hi_ok, 1)

        def weight_lo(pool, g, slot, r_slot):
            pool.wait_ge(s_w_hi_ok, g + 1)
            side = slot % 2
            pool.tensor_tensor(w_lo[:, slot, :, :], raw[:, r_slot, :, side * P:(side + 1) * P],
                               w_hi[:, slot, :, :].bitcast(F32), ALU.subtract).then_inc(s_w_lo_ok, 1)

        @block.scalar
        def _(act):
            chain = [0]

            def link(ins):
                chain[0] += 1
                ins.then_inc(s_act_chain, 1)
                act.wait_ge(s_act_chain, chain[0])

            def split(g):
                weight_hi(act, g, g % WSLOTS, g // 2 % 2, g // 4)

            act.dma_start(pt[:, :], page_table.rearrange("(o b) n -> o (b n)", o=1)).then_inc(s_pt_in, 16)
            act.dma_start(x_s[:, :], x_sample[:, 0, :]).then_inc(x_in[NT], 16)
            act.dma_start(par_rows[0:8, :], ln1_w.rearrange("o (k p) -> (o k) p", p=P)).then_inc(s_par_in, 16)
            act.dma_start(par_rows[8:16, :], ln2_w.rearrange("o (k p) -> (o k) p", p=P)).then_inc(s_par_in, 16)
            act.dma_start(par_rows[16:20, :], mlstm_norm_w.rearrange("o (k p) -> (o k) p", p=P))\
               .then_inc(s_par_in, 16)
            act.dma_start(wg_raw[:, :, :], w_in[0, :, GATE_COL:GATE_COL + 8].rearrange("(k p) n -> p k n", p=P))\
               .then_inc(s_wg_in, 16)
            act.dma_start(bias_i[:, :], b_gates[0:1, 0:4].rearrange("o n -> n o")).then_inc(s_small_in, 16)
            act.dma_start(bias_f[32:36, :], b_gates[0:1, 4:8].rearrange("o n -> n o")).then_inc(s_small_in, 16)
            act.dma_start(m0_row[:, :], state_m[0].rearrange("b h -> h b")).then_inc(s_small_in, 16)
            act.dma_start(n_rows[:, :], state_n[0].rearrange("b h d -> (b h) d")).then_inc(s_n_in, 16)
            for i in range(NT + 1):
                act.wait_ge(x_in[i], 16)
                n = P if i < NT else NS
                x = x_tok[:, i, :] if i < NT else x_s[:, :]
                if i >= 1:
                    act.wait_ge(s_x_sq_ok, i)
                act.activation(junk[0:n, :], x, ACT.Square, accum_out=ss[0:n, i:i + 1]).then_inc(s_x_sq_ok, 1)
            act.wait_ge(s_wg_in, 16)
            act.wait_ge(s_wg_zero, 2)
            act.activation(wg_hi[:, :, 0:4], wg_raw[:, :, 0:4], ACT.Copy).then_inc(s_wg_hi_ok, 1)
            act.activation(wg_hi[:, :, 32:36], wg_raw[:, :, 4:8], ACT.Copy).then_inc(s_wg_hi_ok, 1)
            out = full(act, "param", 0)
            ins = act.activation(par[:, :], out[:, 0:20], ACT.Copy)
            free(ins, "param", 0)
            evacuated(act, "param", 0)
            split(0)
            for j in range(KT):
                out = full(act, "xn", j)
                act.activation(act_hi[:, j, 0:SEQ], out, ACT.Copy, scale=par[:, j:j + 1]).then_inc(s_xhi_ok, 1)
                if j == 3:
                    split(1)
            split(2)

            def copy_out(dst, src, *key):
                free(act.activation(dst, src, ACT.Copy), *key)

            def task(name, *a):
                if name == "rows":
                    act.wait_ge(s_f_abs, 1)
                    link(act.activation(rows[:, 2, :], rows[:, 2, :], ACT.Exp, scale=-1.0))
                    act.activation(rows[:, 2, :], rows[:, 2, :], ACT.Ln, bias=1.0).then_inc(s_f_log, 1)
                    act.wait_ge(s_m_ok, 1)
                    act.activation(rows[:, 5, 0:SEQ], rows[:, 2, 0:SEQ], ACT.Exp, scale=-1.0)\
                       .then_inc(s_rows_ok, 1)
                    act.dma_start(m_prompt[0, 0:1, :].rearrange("o h -> h o"), rows[:, 2, SEQ - 1:SEQ])\
                       .then_inc(s_out_small, 16)
                    act.wait_ge(s_srow_ok, 1)
                    act.activation(s_rows[:, 0:2, :], s_rows[:, 0:2, :], ACT.Exp).then_inc(s_srow_exp, 1)
                    act.activation(s_rows[:, 2, :], m_s[:, :], ACT.Exp, scale=-1.0).then_inc(s_srow_exp, 1)
                    act.dma_start(m_sample[0].rearrange("b h -> h b"), m_s[:, :]).then_inc(s_out_small, 16)
                    for b in range(4):
                        load_state(b)
                elif name == "qs_tok":
                    copy_out(qs_tok[:, :], full(act, "qs_tok", 0)[0:NS, :], "qs_tok", 0)
                elif name == "vs_tok":
                    copy_out(vs_tok[:, :], full(act, "vs_tok", 0)[0:NS, :], "vs_tok", 0)
                elif name == "ks_tok":
                    act.wait_ge(s_kmul_ok, 4 * NS)
                    copy_out(Qb[0:NS, 0, :], full(act, "ks_tok", 0)[0:NS, :], "ks_tok", 0)
                    evacuated(act, "ks_tok", 0)
                    act.dma_start(k_sample[0, :, 0, :, :].rearrange("b h d -> b (h d)"), Qb[0:NS, 0, :])\
                       .then_inc(s_out_small, 16)
                elif name == "va_s":
                    copy_out(Qb[0:NS, 1, :], full(act, "va_s", 0)[0:NS, :], "va_s", 0)
                    evacuated(act, "va_s", 0)
                    act.dma_start(v_sample[0, :, 0, :, :].rearrange("b h d -> b (h d)"), Qb[0:NS, 1, :])\
                       .then_inc(s_out_small, 16)
                elif name == "qb":
                    b, = a
                    out = full(act, "qb", b, 0)
                    if b >= 2:
                        act.wait_ge(s_kmul_ok, 4 * (b - 1))
                    copy_out(Qb[:, b % 2, :], out, "qb", b, 0)
                elif name == "tok":
                    group, i = a
                    key = ("tok", group, i, 0)
                    out = full(act, *key)
                    if group == VM:
                        act.wait_ge(s_vm_ones, 1)
                        copy_out(vm_tok[:, i, :, 0:MD], out.rearrange("p (h d) -> p h d", h=MH), *key)
                    elif group == KM:
                        copy_out(km_tok[:, i, :], out, *key)
                    elif group == VA:
                        copy_out(v_tok[:, i, :], out, *key)
                        evacuated(act, *key)
                        act.dma_start(v_prompt[0, 0, i * P:(i + 1) * P, :, :].rearrange("t h d -> t (h d)"),
                                      v_tok[:, i, :]).then_inc(s_out_v, 16)
                    else:
                        if i >= 2:
                            act.wait_ge(k_out[i % 2], 16)
                        copy_out(k_stage[:, i % 2, :], out, *key)
                        evacuated(act, *key)
                        act.dma_start(k_prompt[0, 0, i * P:(i + 1) * P, :, :].rearrange("t h d -> t (h d)"),
                                      k_stage[:, i % 2, :]).then_inc(k_out[i % 2], 16)
                elif name == "sm_r":
                    b, = a
                    evacuated(act, "sm_c", b, 0)
                    act.dma_start(C_sample[0, b].rearrange("h d e -> d h e"), Cs[:, b % 4, :, :])\
                       .then_inc(C_out[b % 4], 16)
                    if 2 <= b < 6:
                        n = b - 2
                        full(act, "sm_r", n, 0)
                        act.wait_ge(C_out[n], 16)
                        load_state(n + 4)
                elif name == "sm_out":
                    evacuated(act, "sm_out", 1)
                    act.dma_start(n_sample[0].rearrange("b h d -> (b h) d"), n_new_rows[:, :])\
                       .then_inc(s_out_small, 16)
                elif name == "ml_a":
                    h, = a
                    out = full(act, "ml_a", h, 0)
                    if h == 0:
                        act.wait_ge(s_out_small, 32)
                        evacuated(act, "gcols", 0)
                    link(act.activation(MS[:, h:h + 1], out[:, SEQ - 1:SEQ], ACT.Copy, scale=-1.0))
                    act.activation(w_end[:, h, :], g_col[:, 0, :, h], ACT.Exp, bias=MS[:, h:h + 1])\
                       .then_inc(s_ml_wend, 1)
                    for j in range(NT):
                        w = SEQ - j * P
                        ins = act.activation(mA[:, h % 2, A_COL[j]:A_COL[j] + w], out[:, j * P:SEQ], ACT.Exp,
                                             scale=-1.0, bias=g_col[:, 0, j, h:h + 1])
                    free(ins, "ml_a", h, 0)
                elif name == "ml_t":
                    h, = a
                    out = full(act, "ml_t", h, 0)
                    free(act.activation(zT[:, QM + h, 0:SEQ], out, ACT.Copy, scale=par[:, 16 + h:17 + h]),
                         "ml_t", h, 0)
                elif name == "ml_mc":
                    h, = a
                    evacuated(act, "ml_mc", h, 0)
                    act.dma_start(C_prompt[0, 0, h, :, :], C_stage[:, h, :]).then_inc(s_out_C, 16)
                    if h == MH - 1:
                        act.dma_start(n_prompt[0, 0].rearrange("h d -> d h"), nc_col[:, :]).then_inc(s_out_C, 16)
                elif name == "mx_b":
                    act.wait_ge(s_samp_sub, 1)
                    flat = S[:, :, :, :].rearrange("p b g h -> p (b g h)")
                    act.activation(flat, flat, ACT.Exp, scale=ASCALE).then_inc(s_samp_exp, 1)
                    flat = own_p[:, :, :].rearrange("p b h -> p (b h)")
                    act.activation(flat, flat, ACT.Exp, scale=ASCALE).then_inc(s_samp_exp, 1)
                elif name == "att_s":
                    h, = a
                    if h == 0:
                        evacuated(act, "ml_t", MH - 1, 0)
                    for n, parts in enumerate(((0, 1), (2,), (3,))):
                        out = bank("att_s", h, n)
                        act.wait_ge(s_att_nmax, 3 * h + n + 1)
                        col = 0
                        for i in parts:
                            w = (i + 1) * P
                            ins = act.activation(pr[:, h % 2, P_COL[i]:P_COL[i] + w], out[:, col:col + w], ACT.Exp,
                                                 scale=ASCALE, bias=nmax[:, h % 2, i:i + 1],
                                                 accum_out=rsum[:, h % 2, i:i + 1])
                            col += w
                        free(ins, "att_s", h, n)
                elif name == "att_t":
                    h, = a
                    for j in (0, 2):
                        out = full(act, "att_t", h, j)
                        w = SEQ - j * P
                        copy_out(pT[:, A_COL[j]:A_COL[j] + w], out[:, 0:w], "att_t", h, j)
                elif name == "att_o":
                    h, = a
                    if h % 2 == 1:
                        copy_out(zT[:, QA + h // 2, 0:SEQ], full(act, "att_o", h, 1), "att_o", h, 1)
                elif name == "om":
                    h, = a
                    act.wait_ge(s_acc_evac, z_ready(OM + h))
                    act.activation(zT[:, OM + h, :], zT[:, OM + h, :], ACT.Exp, scale=-1.0).then_inc(s_om_exp, 1)
                elif name == "mix":
                    j, = a
                    if j == 0:
                        act.wait_ge(s_half_done, 2 * N_IN)
                        act.wait_ge(s_pv_end_ok, 2)
                    if j < 4:
                        evacuated(act, "att_o", 2 * j + 1, 1)
                        src = zT[:, QA + j, :]
                    else:
                        act.wait_ge(s_gated, j - 3)
                        src = zT[:, QM + j - 4, :]
                    act.activation(act_hi[:, j, :], src, ACT.Copy).then_inc(s_mix_hi, 1)
                elif name == "xt":
                    j, = a
                    out = full(act, "xt", j, 0)
                    if j == 0:
                        act.wait_ge(s_mix_lo, KT)
                        act.wait_ge(s_out_small, 16 * 5)
                    copy_out(xT[:, j, 0:SEQ], out, "xt", j, 0)
                elif name == "xt_s":
                    copy_out(xT[:, :, SEQ:TOK], full(act, "xt_s", 0)[:, 0:KT * NS].rearrange("p (j b) -> p j b", j=KT),
                             "xt_s", 0)
                elif name == "ss":
                    j, = a
                    act.wait_ge(s_acc_evac, 2 * (G_OUT + j + 1))
                    if j >= 2:
                        act.wait_ge(s_sq_read, j - 1)
                    act.activation(x_sq[:, j % 2, :], xT[:, j, :], ACT.Square).then_inc(s_x1_sq, 1)

            def load_state(b):
                act.dma_start(Cs[:, b % 4, :, :], state_C[0, b].rearrange("h d e -> d h e")).then_inc(C_in[b % 4], 16)

            for g in range(G_MLP):
                split(g + AHEAD)
                for name in TASKS[g]:
                    task(*name)
            act.wait_ge(s_half_done, 2 * G_MLP)
            for j in range(KT):
                act.activation(act_hi[:, j, :], xT[:, j, :], ACT.Copy, scale=par[:, 8 + j:9 + j])\
                   .then_inc(s_x2_hi, 1)

            def quarter(i, last):
                for t in range(16):
                    g = G_MLP + 16 * i + t
                    if not last or t + AHEAD < 16:
                        n = t + AHEAD
                        weight_hi(act, g + AHEAD, n % WSLOTS, n // 2 % 2, (G_MLP // 4) + 4 * i + n // 4)
                    if t < 8:
                        act.wait_ge(s_acc_evac, 2 * (g + 1))
                        if t >= 2:
                            act.wait_ge(s_hs_lo, 8 * i + t - 1)
                        act.activation(relu2[:, t % 2, :], relu[:, t % 2, :], ACT.Square)
                        act.activation(h_hi[:, t, :], relu[:, t % 2, :], ACT.Square).then_inc(s_hs_hi, 1)

            with act.Fori(0, QUARTERS - 1) as i:
                quarter(i, False)
            quarter(QUARTERS - 1, True)
            for i in range(NT + 1):
                n = P if i < NT else NS
                for part in range(2):
                    out = full(act, "yt", i, part)
                    if i + part >= 1:
                        act.wait_ge(s_y_sq, 2 * i + part)
                    act.activation(y_junk[0:n, :], out[0:n, :], ACT.Square, accum_out=y_ss[0:n, i, part:part + 1])\
                       .then_inc(s_y_sq, 1)
            act.wait_ge(s_out_v, 16 * NT)
            act.wait_ge(s_out_C, 16 * (MH + 1))
            act.wait_ge(s_out_small, 16 * 5)
            act.wait_ge(s_k_out0, 32)
            act.wait_ge(s_k_out1, 32)
            for b in range(4):
                act.wait_ge(C_out[b], 32)

        @block.gpsimd
        def _(pool):
            def rsqrt(x, n, free_size):
                return pool.tensor_tensor(x, x, power[0:n, :].to_broadcast([n, free_size]), ALU.pow)

            pool.memset(ident[:, :], 0.0).then_inc(s_pool_chain, 1)
            pool.memset(causal[:, :], 0.0).then_inc(s_pool_chain, 1)
            pool.memset(ones[:, :], 1.0).then_inc(s_ones_ok, 1)
            pool.memset(power[:, :], -0.5).then_inc(s_pool_chain, 1)
            pool.memset(even[:, :], 0.0).then_inc(s_pool_chain, 1)
            pool.memset(wg_hi[:, :, :].bitcast(F32), 0.0).then_inc(s_wg_zero, 1)
            pool.memset(wg_lo[:, :, :].bitcast(F32), 0.0).then_inc(s_wg_zero, 1)
            pool.wait_ge(s_pool_chain, 4)
            pool.affine_select(out=ident[:, :], in_=ident[:, :], compare_op=ALU.not_equal, fill=1.0, base=0,
                               pattern=[[-1, P]], channel_multiplier=1).then_inc(s_ident_ok, 1)
            pool.affine_select(out=causal[:, :], in_=causal[:, :], compare_op=ALU.is_ge, fill=MASKED, base=0,
                               pattern=[[-1, P]], channel_multiplier=1).then_inc(s_causal_ok, 1)
            pool.affine_select(out=even[:, 0:1], in_=even[:, 0:1], compare_op=ALU.is_ge, fill=1.0, base=-64,
                               pattern=[[1, 1]], channel_multiplier=1).then_inc(s_ident_ok, 1)
            pool.affine_select(out=even[:, 1:2], in_=even[:, 1:2], compare_op=ALU.is_ge, fill=1.0, base=63,
                               pattern=[[1, 1]], channel_multiplier=-1).then_inc(s_ident_ok, 1)
            for i in range(NT + 1):
                n = P if i < NT else NS
                pool.wait_ge(s_x_ms_ok, i + 1)
                rsqrt(rs[0:n, i:i + 1], n, 1).then_inc(s_x_rs_ok, 1)
            pool.wait_ge(s_wg_hi_ok, 2)
            pool.tensor_tensor(wg_lo[:, :, 0:4], wg_raw[:, :, 0:4], wg_hi[:, :, 0:4].bitcast(F32), ALU.subtract)\
                .then_inc(s_wg_lo_ok, 1)
            pool.tensor_tensor(wg_lo[:, :, 32:36], wg_raw[:, :, 4:8], wg_hi[:, :, 32:36].bitcast(F32),
                               ALU.subtract).then_inc(s_wg_lo_ok, 1)
            for g in range(AHEAD):
                weight_lo(pool, g, g % WSLOTS, g // 2 % 2)

            def task(name, *a):
                if name == "rows":
                    full(pool, "gates", 1)
                    pool.memset(vm_tok[:, :, :, MD:MD + 1], 1.0).then_inc(s_vm_ones, 1)
                elif name == "score":
                    b, c = a
                    n = 4 * b + c
                    if c == 0:
                        evacuated(pool, "qb", b, 0)
                    for j in (2 * c, 2 * c + 1):
                        pool.wait_ge(kv_in[j], 16 * (b + 1))
                    if n >= 2:
                        pool.wait_ge(s_kred_ok, n - 1)
                    pool.tensor_tensor(prod[:, n % 2, :].rearrange("p (j n) -> p j n", j=2),
                                       kv[:, 2 * c:2 * c + 2, :],
                                       Qb[:, b % 2:b % 2 + 1, :].to_broadcast([P, 2, AW]), ALU.mult)\
                        .then_inc(s_kmul_ok, 1)
                elif name == "sm_c":
                    b, = a
                    pool.wait_ge(s_sm_b_ok, 1)
                    pool.wait_ge(C_in[b % 4], 16 * (b // 4 + 1))
                    pool.tensor_tensor(Cs[:, b % 4, :, :], Cs[:, b % 4, :, :],
                                       sm_b[:, :, 0, b:b + 1].to_broadcast([P, MH, MD]), ALU.mult)\
                        .then_inc(s_C_decayed, 1)
                elif name == "sm_out":
                    evacuated(pool, "sm_out", 0)
                    rsqrt(sm_t[:, :, :].rearrange("p b h -> p (b h)"), P, NS * MH).then_inc(s_sm_pow, 1)
                elif name == "ml_a":
                    h, = a
                    evacuated(pool, "ml_a", h, 0)
                    for j in range(NT):
                        blk = mA[:, h % 2, A_COL[j]:A_COL[j] + P]
                        pool.affine_select(out=blk, in_=blk, compare_op=ALU.is_ge, fill=0.0, base=0,
                                           pattern=[[1, P]], channel_multiplier=-1).then_inc(s_ml_tri, 1)
                elif name == "ml_o":
                    h, = a
                    pool.wait_ge(s_ml_ms, h + 1)
                    rsqrt(m_rs[:, :], P, NT).then_inc(s_ml_pow, 1)
                elif name == "rstd2":
                    evacuated(pool, "ss", 0, 0)
                    evacuated(pool, "ss", 0, 1)
                    rsqrt(rstd2[:, :], P, TOK).then_inc(s_rstd_ok, 1)

            for g in range(G_MLP):
                weight_lo(pool, g + AHEAD, (g + AHEAD) % WSLOTS, (g + AHEAD) // 2 % 2)
                for name in TASKS[g]:
                    task(*name)

            def quarter(i, last):
                for t in range(16):
                    g = G_MLP + 16 * i + t
                    if not last or t + AHEAD < 16:
                        n = t + AHEAD
                        weight_lo(pool, g + AHEAD, n % WSLOTS, n // 2 % 2)
                    if t < 8:
                        pool.wait_ge(s_hs_hi, 8 * i + t + 1)
                        pool.tensor_tensor(h_lo[:, t, :], relu2[:, t % 2, :], h_hi[:, t, :].bitcast(F32),
                                           ALU.subtract).then_inc(s_hs_lo, 1)

            with pool.Fori(0, QUARTERS - 1) as i:
                quarter(i, False)
            quarter(QUARTERS - 1, True)
            for i in range(NT + 1):
                n = P if i < NT else NS
                pool.wait_ge(s_y_ms_ok, i + 1)
                rsqrt(y_ms[0:n, i:i + 1], n, 1).then_inc(s_y_pow, 1)

        @block.vector
        def _(dve):
            chain = [0]

            def link(ins):
                chain[0] += 1
                ins.then_inc(s_dve_chain, 1)
                dve.wait_ge(s_dve_chain, chain[0])

            for i in range(NT + 1):
                n = P if i < NT else NS
                dve.wait_ge(s_x_sq_ok, i + 1)
                dve.tensor_scalar(rs[0:n, i:i + 1], ss[0:n, i:i + 1], 1.0 / D, EPS, ALU.mult, ALU.add)\
                   .then_inc(s_x_ms_ok, 1)
            for i in range(NT + 1):
                n = P if i < NT else NS
                x = x_tok[:, i, :] if i < NT else x_s[:, :]
                dve.wait_ge(s_x_rs_ok, i + 1)
                dve.tensor_scalar(x, x, rs[0:n, i:i + 1], None, ALU.mult).then_inc(s_xn_ready, 1)
            for j in range(KT):
                out = full(dve, "xn", j)
                dve.wait_ge(s_xhi_ok, j + 1)
                free(dve.scalar_tensor_tensor(out=act_lo[:, j, 0:SEQ], in0=out, scalar=par[:, j:j + 1],
                                              in1=act_hi[:, j, 0:SEQ].bitcast(F32), op0=ALU.mult,
                                              op1=ALU.subtract), "xn", j)
            out = full(dve, "xn", KT)[:, 0:KT * NS].rearrange("p (j b) -> p j b", j=KT)
            free(dve.tensor_tensor(xn_s[:, :, :], out, par[:, 0:KT].unsqueeze(2).to_broadcast([P, KT, NS]),
                                   ALU.mult), "xn", KT)
            evacuated(dve, "xn", KT)
            link(dve.tensor_copy(act_hi[:, :, SEQ:TOK], xn_s[:, :, :]))
            dve.tensor_tensor(act_lo[:, :, SEQ:TOK], xn_s[:, :, :], act_hi[:, :, SEQ:TOK].bitcast(F32),
                              ALU.subtract).then_inc(s_xs_ok, 1)

            def sample_bh(c):
                return zT[:, c:c + MH, SEQ:TOK].rearrange("p h b -> p b h")

            def heads(r):
                return sm_b[:, :, r, :].rearrange("p h b -> p b h")

            def per_page(x):
                return x[:, :, :].unsqueeze(2).to_broadcast([P, NS, PAGES, AH])

            def task(name, *a):
                if name == "rows":
                    dve.wait_ge(s_small_in, 48)
                    for half in range(2):
                        cols = slice(half * HALF, (half + 1) * HALF)
                        out = full(dve, "gates", half)
                        dve.tensor_scalar(rows[:, 0, cols], out[0:4, 0:HALF], bias_i[:, :], None, ALU.add)
                        free(dve.tensor_scalar(rows[:, 1, cols], out[32:36, 0:HALF], bias_f[32:36, :], None,
                                               ALU.add), "gates", half)
                    evacuated(dve, "gates", 0)
                    evacuated(dve, "gates", 1)
                    dve.scalar_tensor_tensor(out=rows[:, 2, :], in0=rows[:, 1, :], scalar=-1.0, in1=rows[:, 1, :],
                                             op0=ALU.mult, op1=ALU.max).then_inc(s_f_abs, 1)
                    dve.memset(rows[:, 5, :], 0.0)
                    dve.wait_ge(s_f_log, 1)
                    link(dve.scalar_tensor_tensor(out=rows[:, 1, :], in0=rows[:, 1, :], scalar=0.0,
                                                  in1=rows[:, 2, :], op0=ALU.min, op1=ALU.subtract))
                    link(dve.tensor_tensor_scan(rows[:, 4, 0:SEQ], rows[:, 1, 0:SEQ], rows[:, 5, 0:SEQ], 0.0,
                                                ALU.add, ALU.add))
                    link(dve.tensor_tensor(rows[:, 3, 0:SEQ], rows[:, 0, 0:SEQ], rows[:, 4, 0:SEQ], ALU.subtract))
                    link(dve.tensor_tensor_scan(M_row[:, 0:SEQ], rows[:, 3, 0:SEQ], rows[:, 3, 0:SEQ], 0.0,
                                                ALU.max, ALU.max))
                    dve.tensor_tensor(rows[:, 2, 0:SEQ], rows[:, 4, 0:SEQ], M_row[:, 0:SEQ], ALU.add)\
                       .then_inc(s_m_ok, 1)
                    i_s, lf_s = rows[:, 0, SEQ:TOK], rows[:, 1, SEQ:TOK]
                    link(dve.tensor_tensor(s_rows[:, 0, :], lf_s, m0_row[:, :], ALU.add))
                    link(dve.tensor_tensor(m_s[:, :], s_rows[:, 0, :], i_s, ALU.max))
                    dve.tensor_tensor(s_rows[:, 1, :], i_s, m_s[:, :], ALU.subtract)
                    dve.tensor_tensor(s_rows[:, 0, :], s_rows[:, 0, :], m_s[:, :], ALU.subtract)\
                       .then_inc(s_srow_ok, 1)
                elif name == "gcols":
                    out = full(dve, "gcols", 0)
                    free(dve.tensor_copy(g_col[:, :, :, :].rearrange("p r i h -> p (r i h)"),
                                         out[:, 0:2 * NT * MH]), "gcols", 0)
                elif name == "score":
                    b, c = a
                    n = 4 * b + c
                    dve.wait_ge(s_kmul_ok, n + 1)
                    dve.tensor_reduce(S[:, b, 2 * c:2 * c + 2, :].rearrange("p j h -> p (j h)"),
                                      prod[:, n % 2, :].rearrange("p (g d) -> p g d", d=AD), AX.X, ALU.add)\
                       .then_inc(s_kred_ok, 1)
                elif name == "sm_prep":
                    out = full(dve, "sm_prep", 0)
                    free(dve.tensor_copy(sm_b[:, :, :, :].rearrange("p h r b -> p (h r b)"),
                                         out[:, 0:MH * 3 * NS]), "sm_prep", 0)
                    evacuated(dve, "sm_prep", 0)
                    dve.tensor_tensor(sm_kw[:, :, :], zT[:, KM:KM + MH, SEQ:TOK], sm_b[:, :, 1, :], ALU.mult)\
                       .then_inc(s_sm_b_ok, 1)
                    out = full(dve, "sm_prep", 1)
                    free(dve.tensor_tensor(sm_n[:, :, :], out[:, 0:NS * MH].rearrange("p (b h) -> p b h", b=NS),
                                           heads(0), ALU.mult), "sm_prep", 1)
                    evacuated(dve, "sm_prep", 1)
                    dve.wait_ge(s_sm_b_ok, 1)
                    link(dve.tensor_tensor(sm_n[:, :, :], sm_n[:, :, :],
                                           sm_kw[:, :, :].rearrange("p h b -> p b h"), ALU.add))
                    dve.tensor_tensor(sm_q[:, :, :], sample_bh(QM), sm_n[:, :, :], ALU.mult).then_inc(s_sm_dve, 1)
                elif name == "sm_c":
                    b, = a
                    out = full(dve, "sm_c", b, 0)
                    dve.wait_ge(s_C_decayed, b + 1)
                    for h in range(MH):
                        ins = dve.scalar_tensor_tensor(out=Cs[:, b % 4, h, :], in0=out[:, h * MD:(h + 1) * MD],
                                                       scalar=sm_kw[:, h, b:b + 1], in1=Cs[:, b % 4, h, :],
                                                       op0=ALU.mult, op1=ALU.add)
                    free(ins, "sm_c", b, 0)
                elif name == "sm_r":
                    b, = a
                    out = full(dve, "sm_r", b, 0)
                    free(dve.tensor_copy(sm_h[:, b, :], out[:, 0:MH]), "sm_r", b, 0)
                elif name == "sm_den":
                    for b in range(NS):
                        evacuated(dve, "sm_r", b, 0)
                    out = full(dve, "sm_den", 0)[:, 0:NS * MH].rearrange("p (b h) -> p b h", b=NS)
                    link(dve.scalar_tensor_tensor(out=sm_t[:, :, :], in0=out, scalar=-MSCALE, in1=heads(2),
                                                  op0=ALU.mult, op1=ALU.max))
                    free(dve.scalar_tensor_tensor(out=sm_t[:, :, :], in0=out, scalar=MSCALE, in1=sm_t[:, :, :],
                                                  op0=ALU.mult, op1=ALU.max), "sm_den", 0)
                    evacuated(dve, "sm_den", 0)
                    link(dve.reciprocal(sm_t[:, :, :], sm_t[:, :, :]))
                    link(dve.scalar_tensor_tensor(out=sm_h[:, :, :], in0=sm_h[:, :, :], scalar=MSCALE,
                                                  in1=sm_t[:, :, :], op0=ALU.mult, op1=ALU.mult))
                    dve.tensor_tensor(sm_t[:, :, :], sm_h[:, :, :], sm_h[:, :, :], ALU.mult).then_inc(s_sm_dve, 1)
                elif name == "sm_out":
                    out = full(dve, "sm_out", 0)
                    free(dve.tensor_scalar(sm_t[:, :, :].rearrange("p b h -> p (b h)"), out[:, 0:NS * MH],
                                           1.0 / MD, EPS, ALU.mult, ALU.add), "sm_out", 0)
                    out = full(dve, "sm_out", 1)
                    free(dve.tensor_copy(n_new_rows[:, :], out[0:NS * MH, 0:P]), "sm_out", 1)
                    dve.wait_ge(s_sm_pow, 1)
                    link(dve.tensor_tensor(sm_h[:, :, :], sm_h[:, :, :], sm_t[:, :, :], ALU.mult))
                    dve.tensor_tensor(sample_bh(QM), sm_h[:, :, :],
                                      par[:, 16:20].unsqueeze(1).to_broadcast([P, NS, MH]), ALU.mult)\
                       .then_inc(s_sm_end, 1)
                elif name == "ml_a":
                    h, = a
                    for n, parts in enumerate(((0,), (1,), (2, 3))):
                        out = full(dve, "ml_a", h, n + 1)
                        col = 0
                        for j in parts:
                            w = SEQ - j * P
                            dve.wait_ge(s_ml_tri, 4 * h + j + 1)
                            blk = mA[:, h % 2, A_COL[j]:A_COL[j] + w]
                            ins = dve.scalar_tensor_tensor(out=blk, in0=out[:, col:col + w], scalar=MSCALE,
                                                           in1=blk, op0=ALU.mult, op1=ALU.mult)
                            col += w
                        free(ins, "ml_a", h, n + 1)
                elif name == "ml_o":
                    h, = a
                    if h >= 1:
                        full(dve, "ml_t", h - 1, 0)
                    for half in range(2):
                        out = full(dve, "ml_o", h, half)[:, 0:2 * (MD + 1)].rearrange("p (i e) -> p i e", i=2)
                        two = slice(2 * half, 2 * half + 2)
                        link(dve.scalar_tensor_tensor(out=m_den[:, two], in0=out[:, :, MD], scalar=-1.0,
                                                      in1=g_col[:, 1, two, h], op0=ALU.mult, op1=ALU.max))
                        link(dve.tensor_tensor(m_den[:, two], out[:, :, MD], m_den[:, two], ALU.max))
                        link(dve.reciprocal(m_den[:, two], m_den[:, two]))
                        free(dve.tensor_tensor(m_h[:, two, :], out[:, :, 0:MD],
                                               m_den[:, two].unsqueeze(2).to_broadcast([P, 2, MD]), ALU.mult),
                             "ml_o", h, half)
                    evacuated(dve, "ml_o", h, 0)
                    evacuated(dve, "ml_o", h, 1)
                    link(dve.tensor_tensor(m_kw[:, :, :], m_h[:, :, :], m_h[:, :, :], ALU.mult))
                    link(dve.tensor_reduce(m_ss[:, :], m_kw[:, :, :], AX.X, ALU.add))
                    dve.tensor_scalar(m_rs[:, :], m_ss[:, :], 1.0 / MD, EPS, ALU.mult, ALU.add).then_inc(s_ml_ms, 1)
                    dve.wait_ge(s_ml_pow, h + 1)
                    dve.tensor_tensor(m_h[:, :, :], m_h[:, :, :],
                                      m_rs[:, :].unsqueeze(2).to_broadcast([P, NT, MD]), ALU.mult)\
                       .then_inc(s_ml_hr, 1)
                elif name == "ml_mc":
                    h, = a
                    dve.wait_ge(s_ml_wend, h + 1)
                    if h == 0:
                        for i in range(NT):
                            evacuated(dve, "tok", KM, i, 0)
                    else:
                        full(dve, "ml_mc", h - 1, 0)
                    dve.tensor_tensor(m_kw[:, :, :], km_tok[:, :, h * MD:(h + 1) * MD],
                                      w_end[:, h, :].unsqueeze(2).to_broadcast([P, NT, MD]), ALU.mult)\
                       .then_inc(s_ml_kw, 1)
                    out = full(dve, "ml_mc", h, 0)
                    dve.tensor_copy(nc_col[:, h:h + 1], out[:, MD:MD + 1])
                    free(dve.tensor_copy(C_stage[:, h, :], out[:, 0:MD]), "ml_mc", h, 0)
                elif name == "gate":
                    out = full(dve, "gate", 0)
                    blocks = gate[:, :, :, :]
                    free(dve.tensor_reduce(blocks.rearrange("p b n h -> p (b n) h"),
                                           out.rearrange("p (m two h) -> p m h two", two=2, h=AH), AX.X, ALU.add),
                         "gate", 0)
                    evacuated(dve, "gate", 0)
                    link(dve.tensor_reduce(gate_min[:, :, :], blocks.rearrange("p b n h -> p b h n"), AX.X, ALU.min))
                    link(dve.tensor_tensor(blocks, blocks,
                                           gate_min[:, :, :].unsqueeze(2).to_broadcast([P, NS, 4, AH]),
                                           ALU.is_equal))
                    later = gate[:, :, 3, :]
                    for n, into in ((2, taken), (1, gate_min), (0, None)):
                        if into is not None:
                            link(dve.tensor_tensor(into[:, :, :], gate[:, :, n, :], later, ALU.max))
                        link(dve.tensor_tensor(gate[:, :, n, :], gate[:, :, n, :], later, ALU.is_gt))
                        if into is not None:
                            later = into[:, :, :]
                    link(dve.tensor_scalar(blocks, blocks, MASKED, None, ALU.mult))
                    by_page = S[:, :, :, :].rearrange("p b (n two) h -> p (b n) two h", two=2)
                    for two in range(2):
                        link(dve.tensor_tensor(by_page[:, :, two, :], by_page[:, :, two, :],
                                               blocks.rearrange("p b n h -> p (b n) h"), ALU.add))
                    dve.tensor_reduce(page_max[:, :, :], S[:, :, :, :].rearrange("p b g h -> p b h g"), AX.X,
                                      ALU.max).then_inc(s_samp_dve, 1)
                elif name == "mx_t":
                    out = full(dve, "mx_t", 0)
                    free(dve.reduce_max(mx_col[:, :], out[0:NS * AH, 0:P], AX.X), "mx_t", 0)
                    dve.tensor_tensor(own_prod[:, :, :], zT[:, QA:QA + 4, SEQ:TOK], zT[:, KA:KA + 4, SEQ:TOK],
                                      ALU.mult).then_inc(s_samp_dve, 1)
                elif name == "own":
                    out = full(dve, "own", 0)
                    for odd in range(2):
                        ins = dve.tensor_copy(own[:, :, :].rearrange("p b (t o) -> p t b o", o=2)[:, :, :, odd],
                                              out[:, odd * 32:(odd + 1) * 32].rearrange("p (t b) -> p t b", t=4))
                    free(ins, "own", 0)
                elif name == "mx_b":
                    evacuated(dve, "own", 0)
                    out = full(dve, "mx_b", 0)[:, 0:NS * AH].rearrange("p (b h) -> p b h", b=NS)
                    free(dve.tensor_tensor(smax[:, :, :], out, own[:, :, :], ALU.max), "mx_b", 0)
                    evacuated(dve, "mx_b", 0)
                    dve.tensor_tensor(own_p[:, :, :], own[:, :, :], smax[:, :, :], ALU.subtract)
                    dve.tensor_tensor(S[:, :, :, :], S[:, :, :, :], per_page(smax), ALU.subtract)\
                       .then_inc(s_samp_sub, 1)
                    dve.wait_ge(s_samp_exp, 1)
                    dve.tensor_reduce(page_max[:, :, :], S[:, :, :, :].rearrange("p b g h -> p b h g"), AX.X,
                                      ALU.add).then_inc(s_samp_dve, 1)
                elif name == "zsum":
                    dve.wait_ge(s_samp_exp, 2)
                    out = full(dve, "zsum", 0)[:, 0:NS * AH].rearrange("p (b h) -> p b h", b=NS)
                    free(dve.tensor_tensor(zrec[:, :, :], out, own_p[:, :, :], ALU.add), "zsum", 0)
                    evacuated(dve, "zsum", 0)
                    link(dve.reciprocal(zrec[:, :, :], zrec[:, :, :]))
                elif name == "pv":
                    b, = a
                    out = full(dve, "pv", b, 0)
                    free(dve.tensor_copy(pv_s[:, b, :], out[:, 0:AH]), "pv", b, 0)
                elif name == "pv_end":
                    for b in range(NS):
                        evacuated(dve, "pv", b, 0)
                    for odd in range(2):
                        rows64 = slice(64 * odd, 64 * odd + 64)

                        def by_tile(x):
                            return x[rows64, :, :].rearrange("p b (t o) -> p t b o", o=2)[:, :, :, odd]

                        tmp = own_prod[rows64, :, :]
                        link(dve.tensor_tensor(tmp, zT[rows64, VA:VA + 4, SEQ:TOK], by_tile(own_p), ALU.mult))
                        link(dve.tensor_tensor(tmp, tmp, by_tile(pv_s), ALU.add))
                        dve.tensor_tensor(zT[rows64, QA:QA + 4, SEQ:TOK], tmp, by_tile(zrec), ALU.mult)\
                           .then_inc(s_pv_end_ok, 1)
                elif name == "att_s":
                    h, = a
                    if h == 0:
                        dve.wait_ge(s_causal_ok, 1)
                    for n, parts in enumerate(((0, 1), (2,), (3,))):
                        out = full(dve, "att_s", h, n)
                        col = 0
                        for i in parts:
                            blk = out[:, col + i * P:col + (i + 1) * P]
                            ins = dve.tensor_tensor(blk, blk, causal[:, :], ALU.add)
                            col += (i + 1) * P
                        link(ins)
                        col = 0
                        for i in parts:
                            w = (i + 1) * P
                            ins = dve.reduce_max(rmax[:, h % 2, i:i + 1], out[:, col:col + w], AX.X)
                            col += w
                        link(ins)
                        dve.tensor_scalar(nmax[:, h % 2, parts[0]:parts[-1] + 1],
                                          rmax[:, h % 2, parts[0]:parts[-1] + 1], -ASCALE, None, ALU.mult)\
                           .then_inc(s_att_nmax, 1)
                elif name == "att_t":
                    h, = a
                    for j in (1, 3):
                        out = full(dve, "att_t", h, j)
                        w = SEQ - j * P
                        free(dve.tensor_copy(pT[:, A_COL[j]:A_COL[j] + w], out[:, 0:w]), "att_t", h, j)
                elif name == "att_o":
                    h, = a
                    for n in range(3):
                        evacuated(dve, "att_s", h, n)
                    link(dve.reciprocal(rrec[:, h % 2, :], rsum[:, h % 2, :]))
                    out = full(dve, "att_o", h, 0)[:, 0:NT * AD].rearrange("p (i d) -> p i d", i=NT)
                    if h % 2 == 0 and h >= 2:
                        full(dve, "att_o", h - 1, 1)
                    free(dve.tensor_tensor(att_tok[:, :, AD * (h % 2):AD * (h % 2) + AD], out,
                                           rrec[:, h % 2, :].unsqueeze(2).to_broadcast([P, NT, AD]), ALU.mult),
                         "att_o", h, 0)
                elif name == "om":
                    h, = a
                    dve.wait_ge(s_om_exp, h + 1)
                    dve.wait_ge(s_sm_end, 1)
                    evacuated(dve, "ml_t", h, 0)
                    link(dve.tensor_scalar(zT[:, OM + h, :], zT[:, OM + h, :], 1.0, None, ALU.add))
                    link(dve.reciprocal(zT[:, OM + h, :], zT[:, OM + h, :]))
                    dve.tensor_tensor(zT[:, QM + h, :], zT[:, QM + h, :], zT[:, OM + h, :], ALU.mult)\
                       .then_inc(s_gated, 1)
                elif name == "mix":
                    j, = a
                    dve.wait_ge(s_mix_hi, j + 1)
                    src = zT[:, QA + j, :] if j < 4 else zT[:, QM + j - 4, :]
                    dve.tensor_tensor(act_lo[:, j, :], src, act_hi[:, j, :].bitcast(F32), ALU.subtract)\
                       .then_inc(s_mix_lo, 1)
                elif name == "rstd2":
                    for half in range(2):
                        out = full(dve, "ss", 0, half)
                        free(dve.tensor_scalar(rstd2[:, half * HALF:(half + 1) * HALF], out[:, 0:HALF], 1.0 / D,
                                               EPS, ALU.mult, ALU.add), "ss", 0, half)

            def evac_copy(g):
                for half in range(2):
                    dve.wait_ge(s_half_done, 2 * g + half + 1)
                    dve.tensor_copy(zT[:, IN_ORDER[g], half * HALF:(half + 1) * HALF],
                                    acc[:, 2 * (g % 2) + half, 0:HALF]).then_inc(s_acc_evac, 1)

            def evac_add(g, side, j, half):
                dve.wait_ge(s_half_done, 2 * g + half + 1)
                x = xT[:, j, half * HALF:(half + 1) * HALF]
                dve.tensor_tensor(x, acc[:, 2 * side + half, 0:HALF], x, ALU.add).then_inc(s_acc_evac, 1)

            for g in range(N_IN):
                if IN_ORDER[g] == VA:
                    for b in range(4):
                        dve.wait_ge(C_out[b], 32)
                if IN_ORDER[g] == OM:
                    dve.wait_ge(s_k_out0, 32)
                    dve.wait_ge(s_k_out1, 32)
                evac_copy(g)
                for name in TASKS[g]:
                    task(*name)
            for g in range(G_OUT, G_MLP):
                j = g - G_OUT
                evacuated(dve, "xt", j, 0)
                evacuated(dve, "xt_s", 0)
                for half in range(2):
                    evac_add(g, g % 2, j, half)
                for name in TASKS[g]:
                    task(*name)
            for j in range(KT):
                dve.wait_ge(s_x2_hi, j + 1)
                dve.scalar_tensor_tensor(out=act_lo[:, j, :], in0=xT[:, j, :], scalar=par[:, 8 + j:9 + j],
                                         in1=act_hi[:, j, :].bitcast(F32), op0=ALU.mult, op1=ALU.subtract)\
                   .then_inc(s_x2_lo, 1)
            dve.wait_ge(s_rstd_ok, 1)

            with dve.Fori(0, QUARTERS) as i:
                for t in range(16):
                    g = G_MLP + 16 * i + t
                    for half in range(2):
                        cols = slice(half * HALF, (half + 1) * HALF)
                        if t < 8:
                            dve.wait_ge(s_half_done, 2 * g + half + 1)
                            if t >= 2:
                                dve.wait_ge(s_hs_hi, 8 * i + t - 1)
                            dve.scalar_tensor_tensor(out=relu[:, t % 2, cols], in0=acc[:, 2 * (t % 2) + half, 0:HALF],
                                                     scalar=0.0, in1=rstd2[:, cols], op0=ALU.max, op1=ALU.mult)\
                               .then_inc(s_acc_evac, 1)
                        else:
                            evac_add(g, t % 2, t - 8, half)

            dve.wait_ge(s_lnf_in, 16)
            for i in range(NT + 1):
                n = P if i < NT else NS
                dve.wait_ge(s_y_sq, 2 * i + 2)
                link(dve.tensor_tensor(y_ms[0:n, i:i + 1], y_ss[0:n, i, 0:1], y_ss[0:n, i, 1:2], ALU.add))
                dve.tensor_scalar(y_ms[0:n, i:i + 1], y_ms[0:n, i:i + 1], 1.0 / D, EPS, ALU.mult, ALU.add)\
                   .then_inc(s_y_ms_ok, 1)
                dve.wait_ge(s_y_pow, i + 1)
                if i >= 2:
                    dve.wait_ge(st_y[i % 2], 16 * (i // 2))
                for part in range(2):
                    cols = slice(part * 512, part * 512 + 512)
                    out = full(dve, "yt", i, part)
                    free(dve.scalar_tensor_tensor(out=y_out[0:n, i % 2, cols], in0=out[0:n, :],
                                                  scalar=y_ms[0:n, i:i + 1], in1=lnf_b[0:n, cols], op0=ALU.mult,
                                                  op1=ALU.mult), "yt", i, part)


_INS = ["x_prompt", "x_sample", "cache_k", "cache_v", "page_table", "state_C", "state_n", "state_m", "ln1_w",
        "w_in", "b_gates", "mlstm_norm_w", "w_out", "ln2_w", "w_up", "w_down", "lnf_w"]
_OUTS = [(1, SEQ, D), (NS, 1, D), (1, 1, SEQ, AH, AD), (1, 1, SEQ, AH, AD), (1, 1, MH, MD, MD), (1, 1, MH, MD),
         (1, 1, MH), (1, NS, 1, AH, AD), (1, NS, 1, AH, AD), (1, NS, MH, MD, MD), (1, NS, MH, MD), (1, NS, MH)]


def kernel(**inputs):
    import numpy as _np
    import concourse.bacc as _bacc
    from concourse import mybir as _mybir
    from concourse.bass_utils import run_bass_kernel_spmd as _run

    nc = _bacc.Bacc("TRN2", target_bir_lowering=False, num_devices=1)
    arrays, args = {}, []
    for name in _INS:
        a = _np.ascontiguousarray(inputs[name])
        arrays[f"in_{name}_dram"] = a
        args.append(nc.dram_tensor(f"in_{name}_dram", a.shape, _mybir.dt.from_np(a.dtype), kind="ExternalInput").ap())
    for i, shape in enumerate(_OUTS):
        args.append(nc.dram_tensor(f"out_{i}_dram", shape, _mybir.dt.float32, kind="ExternalOutput").ap())
    build(nc, *args)
    r = _run(nc, [arrays], core_ids=[0])
    return tuple(r.results[0][f"out_{i}_dram"] for i in range(len(_OUTS)))
```

```python
from contextlib import ExitStack

import numpy as np
import concourse.bass as bass
from concourse import mybir

ALU = mybir.AluOpType
ACT = mybir.ActivationFunctionType
AX = mybir.AxisListType
F32 = mybir.dt.float32
F32R = mybir.dt.float32r
I32 = mybir.dt.int32

P = 128
D = 1024
KT = D // P
SEQ = 512
NT = SEQ // P
NS = 8
TOK = SEQ + NS
HALF = TOK // 2
AH, AD = 8, 64
MH, MD = 4, 128
PAGES, PAGE = 8, 128
AW = AH * AD
EPS = 1e-6
MASKED = -1e30
ASCALE = AD ** -0.5
MSCALE = MD ** -0.5

QA, KA, VA, QM, KM, VM, OM = (4 * i for i in range(7))
GATE_COL = 28 * P
IN_ORDER = [c + t for c in (QA, QM, KM, VM, KA, VA, OM) for t in range(4)]
N_IN, N_OUT = 28, 8
G_OUT = N_IN
G_MLP = N_IN + N_OUT
QUARTERS = 4
N_MAIN = G_MLP + 16 * QUARTERS
WSLOTS = 4
AHEAD = 3
DVE_LO = 28
MIX_ORDER = (4, 5, 6, 7, 0, 1, 2, 3)

BASE = 16512


def made_at(g):
    return 2 * (g + 1)


def z_ready(c):
    return made_at(IN_ORDER.index(c))


def plan():
    tasks = [[] for _ in range(G_MLP)]

    def at(g, *names):
        tasks[g] += names

    at(1, ("rows",))
    at(2, ("gcols",))
    at(4, ("qs_tok",))
    at(5, ("qb", 0), ("qb", 1))
    for g in range(6, 22):
        if g % 2 == 0 and 8 <= g <= 18:
            at(g, ("qb", (g - 4) // 2))
    at(16, ("sm_prep",), ("vs_tok",), ("sm_c", 0), ("sm_c", 1), ("tok", VM, 0), ("tok", VM, 1), ("sm_r", 0))
    at(17, ("sm_r", 1), ("sm_c", 2), ("tok", VM, 2), ("tok", VM, 3), ("sm_c", 3), ("sm_r", 2),
       ("tok", KM, 0), ("tok", KM, 1))
    at(18, ("sm_r", 3), ("sm_c", 4), ("tok", KM, 2), ("tok", KM, 3), ("sm_c", 5), ("sm_r", 4), ("ml_a", 0))
    at(19, ("ml_a", 1), ("sm_r", 5), ("sm_c", 6), ("sm_c", 7), ("sm_r", 6), ("ml_o", 0))
    at(20, ("ml_a", 2), ("sm_r", 7), ("ml_t", 0), ("ml_o", 1))
    at(21, ("ml_a", 3), ("ml_t", 1), ("sm_den",), ("tok", KA, 0), ("ml_o", 2), ("tok", KA, 1))
    at(22, ("ml_t", 2), ("ml_o", 3), ("sm_out",), ("ml_kw", 0), ("tok", KA, 2), ("tok", KA, 3))
    at(23, ("ml_t", 3), ("ml_mc", 0), ("gate",), ("ml_kw", 1))
    at(24, ("ml_mc", 1), ("mx_t",), ("ks_tok",), ("tok", VA, 0), ("tok", VA, 1), ("own",), ("ml_kw", 2),
       ("tok", VA, 2), ("tok", VA, 3), ("om", 0))
    at(25, ("ml_mc", 2), ("va_s",), ("mx_b",), ("att_s", 0), ("ml_kw", 3), ("om", 1))
    at(26, ("ml_mc", 3), ("zsum",), ("att_d", 0), ("om", 2))
    at(27, ("vp_a", 0), ("att_s", 1), ("vp_b", 0), ("om", 3))
    for chunk in range(4 * NS):
        at(6 + chunk // 2, ("score", chunk // 4, chunk % 4))
    for h in range(AH):
        if h > 0:
            at(27, ("att_d", h))
            if h + 1 < AH:
                at(27, ("att_s", h + 1))
        at(27, ("pv", h))
        if h + 1 < NS:
            at(27, ("vp_a", h + 1))
        at(27, ("att_t", h), ("pv_sum", h))
        if h + 1 < NS:
            at(27, ("vp_b", h + 1))
        if h >= AH - 2:
            at(27, ("mix", 2 * (h - AH + 2)), ("mix", 2 * (h - AH + 2) + 1))
        if h == AH - 1:
            at(27, ("pv_end",), ("mix", 4), ("mix", 5), ("mix", 6))
        at(27, ("att_o", h))
    at(27, ("mix", 7))
    for j in range(KT):
        at(G_OUT + j // 2, ("xt", j))
    at(G_OUT, ("xt_s",))
    for j in range(KT):
        at(min(G_OUT + j + 1, G_MLP - 1), ("x2", j))

    scratch = {
        "gcols": 1, "qs_tok": 1, "qb": 1, "vs_tok": 1, "tok": 1, "sm_prep": 2, "sm_c": 1, "sm_r": 1, "ml_a": 4,
        "ml_o": 2, "ml_t": 1, "ml_mc": 1, "sm_den": 1, "sm_out": 2, "ks_tok": 1, "gate": 1, "mx_t": 1,
        "own": 1, "va_s": 1, "mx_b": 1, "zsum": 1, "att_s": 3, "att_t": 3, "att_o": 1, "pv": 1,
        "pv_end": 1, "xt": 1, "xt_s": 1,
    }
    jobs = {}

    def job(*key):
        jobs[key] = len(jobs)

    job("param", 0)
    for j in range(KT + 1):
        job("xn", j)
    job("gates", 0)
    job("gates", 1)
    for names in tasks:
        for name in names:
            n = scratch.get(name[0], 0)
            for i in range(n):
                job(*name, i)
    job("sumsq", 0)
    job("rstd2", 0)
    job("rstd2", 1)
    for i in range(NT + 1):
        job("yt", i, 0)
        job("yt", i, 1)
    return tasks, jobs


TASKS, JOBS = plan()


def build(nc, x_prompt, x_sample, cache_k, cache_v, page_table, state_C, state_n, state_m, ln1_w, w_in,
          b_gates, mlstm_norm_w, w_out, ln2_w, w_up, w_down, lnf_w, y_prompt, y_sample, k_prompt, v_prompt,
          C_prompt, n_prompt, m_prompt, k_sample, v_sample, C_sample, n_sample, m_sample):
    n_phys = cache_k.shape[1]
    ctx = ExitStack()
    with ctx:
        ctx.enter_context(nc.allow_non_contiguous_dma(reason="a few hundred elements of gates and states"))
        end = [BASE]

        def place(name, shape, dt=F32, at=None):
            size = 4
            for n in shape[1:]:
                size *= n
            off = end[0] if at is None else at
            t = nc.alloc_sbuf_tensor_at(name, shape, dt, offset=off)
            if at is None:
                end[0] = off + (size + 31) // 32 * 32
            return t, off

        raw, _ = place("raw", [P, 2, KT, 2 * P])
        w_hi, _ = place("w_hi", [P, WSLOTS, KT, P], F32R)
        w_lo, _ = place("w_lo", [P, WSLOTS, KT, P], F32R)
        act_hi, act_hi_at = place("act_hi", [P, KT, TOK], F32R)
        act_lo, act_lo_at = place("act_lo", [P, KT, TOK], F32R)
        v_hi, _ = place("v_hi", [P, PAGES, TOK], F32R, at=act_hi_at)
        v_lo, _ = place("v_lo", [P, PAGES, TOK], F32R, at=act_lo_at)
        zT, z_at = place("zT", [P, N_IN, TOK])
        h_hi, _ = place("h_hi", [P, KT, TOK], F32R, at=z_at)
        h_lo, _ = place("h_lo", [P, KT, TOK], F32R, at=z_at + 4 * KT * TOK)
        tail_at = z_at + 4 * 2 * KT * TOK
        relu, _ = place("relu", [P, 2, TOK], at=tail_at)
        relu2, _ = place("relu2", [P, 2, TOK], at=tail_at + 4 * 2 * TOK)
        rstd2, _ = place("rstd2", [P, TOK], at=tail_at + 4 * 4 * TOK)
        mix_hi, _ = place("mix_hi", [P, KT, TOK], F32R, at=z_at + 4 * KM * TOK)
        mix_lo_att, _ = place("mix_lo_att", [P, 4, TOK], F32R, at=z_at + 4 * OM * TOK)
        mix_lo_ml, _ = place("mix_lo_ml", [P, 4, TOK], F32R, at=z_at + 4 * KA * TOK)
        x_sq, _ = place("x_sq", [P, 2, TOK], at=z_at + 4 * VA * TOK)
        sq_sum, _ = place("sq_sum", [P, TOK], at=z_at + 4 * (VA + 2) * TOK)
        y_out, _ = place("y_out", [P, 2, D], at=z_at)
        y_junk, _ = place("y_junk", [P, 512], at=z_at + 4 * 2 * D)
        km_tok, _ = place("km_tok", [P, NT, AW], at=z_at + 4 * VM * TOK)
        om_at = z_at + 4 * OM * TOK
        qs_tok, _ = place("qs_tok", [NS, AW], at=om_at)
        vs_tok, _ = place("vs_tok", [NS, AW], at=om_at + 4 * AW)
        k_stage, _ = place("k_stage", [P, 2, AW], at=om_at + 8 * AW)
        xT, x_at = place("xT", [P, KT, TOK])
        rows, _ = place("rows", [4, 6, TOK], at=x_at)
        att = 1280
        mA, _ = place("mA", [P, 2, att], at=x_at)
        m_h, _ = place("m_h", [P, NT, MD], at=x_at + 8 * att)
        m_kw, _ = place("m_kw", [P, NT, MD], at=x_at + 8 * att + 2048)
        sm_at = x_at + 8 * att + 4096
        sm_b, _ = place("sm_b", [P, MH, 3, NS], at=sm_at)
        sm_kw, _ = place("sm_kw", [P, MH, NS], at=sm_at + 384)
        sm_n, _ = place("sm_n", [P, NS, MH], at=sm_at + 512)
        sm_q, _ = place("sm_q", [P, NS, MH], at=sm_at + 640)
        sm_h, _ = place("sm_h", [P, NS, MH], at=sm_at + 768)
        sm_t, _ = place("sm_t", [P, NS, MH], at=sm_at + 896)
        n_rows, _ = place("n_rows", [NS * MH, MD], at=sm_at + 1024)
        n_new_rows, _ = place("n_new_rows", [NS * MH, MD], at=sm_at + 1536)
        pr, _ = place("pr", [P, 2, att], at=x_at)
        pT, _ = place("pT", [P, att], at=x_at + 8 * att)
        kv, kv_at = place("kv", [P, PAGES, AW])
        x_tok, _ = place("x_tok", [P, NT, D], at=kv_at)
        x_tok2, _ = place("x_tok2", [P, NT, D], at=kv_at)
        prod, prod_at = place("prod", [P, 2, 2 * AW])
        x_s, _ = place("x_s", [NS, D], at=prod_at)
        x_s2, _ = place("x_s2", [NS, D], at=prod_at)
        C_stage, _ = place("C_stage", [P, MH, MD], at=prod_at + 2048)
        S_split, _ = place("S_split", [P, NS, PAGES, 2 * AH], F32R, at=prod_at)
        junk, _ = place("junk", [P, D], at=x_at)
        lnf_b, _ = place("lnf_b", [P, D], at=prod_at + 4096)
        t_at = prod_at + 4096
        gate, _ = place("gate", [P, NS, 4, AH], at=t_at)
        gate_min, _ = place("gate_min", [P, NS, AH], at=t_at + 1024)
        taken, _ = place("taken", [P, NS, AH], at=t_at + 1280)
        page_max, _ = place("page_max", [P, NS, AH], at=t_at + 1536)
        own, _ = place("own", [P, NS, AH], at=t_at + 1792)
        smax, _ = place("smax", [P, NS, AH], at=t_at + 2048)
        own_p, _ = place("own_p", [P, NS, AH], at=t_at + 2304)
        zrec, _ = place("zrec", [P, NS, AH], at=t_at + 2560)
        own_prod, _ = place("own_prod", [P, 4, NS], at=t_at + 3072)
        mx_col, _ = place("mx_col", [NS * AH, 1], at=t_at + 3200)
        v_tok, _ = place("v_tok", [P, NT, AW])
        vm_tok, vm_at = place("vm_tok", [P, NT, MH, MD + 1])
        wg_hi, _ = place("wg_hi", [P, KT, P], F32R, at=vm_at)
        wg_lo, _ = place("wg_lo", [P, KT, P], F32R, at=vm_at + 4 * D)
        p_norm, _ = place("p_norm", [P, 2, NT, P], at=vm_at)
        pv_masked, _ = place("pv_masked", [2 * AH, 2, AW], at=vm_at + 8 * AW)
        cs_at = z_at + 4 * VA * TOK
        Cs, _ = place("Cs", [P, 4, MH, MD], at=cs_at)
        par_rows, _ = place("par_rows", [20, P], at=cs_at)
        wg_raw, _ = place("wg_raw", [P, KT, 8], at=cs_at + 512)
        xn_s, _ = place("xn_s", [P, KT, NS], at=cs_at + 768)
        S, _ = place("S", [P, NS, PAGES, AH])
        Qb, qb_at = place("Qb", [P, 2, AW])
        pv_tok, _ = place("pv_tok", [NS, AW], at=qb_at)
        pick, _ = place("pick", [2 * AH, 2 * NS - 1])
        own_head, _ = place("own_head", [2 * AH, AH])
        M_row, _ = place("M_row", [4, TOK])
        ident, _ = place("ident", [P, P])
        causal, _ = place("causal", [P, P])
        ones, _ = place("ones", [P, 1])
        even, _ = place("even", [P, 2])
        par, _ = place("par", [P, 20])
        ss, _ = place("ss", [P, 8])
        rs, _ = place("rs", [P, 8])
        power, _ = place("power", [P, 1])
        g_col, _ = place("g_col", [P, 2, NT, MH])
        MS, _ = place("MS", [P, MH])
        w_end, _ = place("w_end", [P, MH, NT])
        m_den, _ = place("m_den", [P, NT])
        m_ss, _ = place("m_ss", [P, NT])
        m_rs, _ = place("m_rs", [P, NT])
        m_s, _ = place("m_s", [4, NS])
        y_ss, _ = place("y_ss", [P, NT + 1, 2])
        y_ms, _ = place("y_ms", [P, NT + 1])
        y_rs, _ = place("y_rs", [P, NT + 1])
        nc_col, _ = place("nc_col", [P, MH])
        rmax, _ = place("rmax", [P, 2, NT])
        nmax, _ = place("nmax", [P, 2, NT])
        rsum, _ = place("rsum", [P, 2, NT])
        rrec, _ = place("rrec", [P, 2, NT])
        bias_i, _ = place("bias_i", [4, 1])
        bias_f, _ = place("bias_f", [P, 1])
        m0_row, _ = place("m0_row", [4, NS])
        s_rows, _ = place("s_rows", [4, 3, NS])
        pt, _ = place("pt", [1, NS * PAGES], I32)
        assert end[0] <= nc.sbuf_usable_end, (end[0], nc.sbuf_usable_end)

        acc = ctx.enter_context(nc.psum_tensor("acc", [P, 4, 512], F32))
        scr = ctx.enter_context(nc.psum_tensor("scr", [P, 4, 512], F32))

        def sem(name):
            return ctx.enter_context(nc.semaphore(name))

        s_x_in0 = sem("x_in0")
        s_x_in1 = sem("x_in1")
        s_x_in2 = sem("x_in2")
        s_x_in3 = sem("x_in3")
        s_x_in4 = sem("x_in4")
        s_par_in = sem("par_in")
        s_wg_in = sem("wg_in")
        s_small_in = sem("small_in")
        s_n_in = sem("n_in")
        s_pt_in = sem("pt_in")
        s_raw0 = sem("raw0")
        s_raw1 = sem("raw1")
        s_x2_in = sem("x2_in")
        s_x2s_in = sem("x2s_in")
        s_lnf_in = sem("lnf_in")
        s_C_in0 = sem("C_in0")
        s_C_in1 = sem("C_in1")
        s_C_in2 = sem("C_in2")
        s_C_in3 = sem("C_in3")
        s_C_out0 = sem("C_out0")
        s_C_out1 = sem("C_out1")
        s_C_out2 = sem("C_out2")
        s_C_out3 = sem("C_out3")
        s_k_out0 = sem("k_out0")
        s_k_out1 = sem("k_out1")
        s_ident_ok = sem("ident_ok")
        s_ones_ok = sem("ones_ok")
        s_causal_ok = sem("causal_ok")
        s_wg_zero = sem("wg_zero")
        s_wg_hi_ok = sem("wg_hi_ok")
        s_wg_lo_ok = sem("wg_lo_ok")
        s_x_sq_ok = sem("x_sq_ok")
        s_x_ms_ok = sem("x_ms_ok")
        s_x_rs_ok = sem("x_rs_ok")
        s_xn_ready = sem("xn_ready")
        s_xhi_ok = sem("xhi_ok")
        s_xs_ok = sem("xs_ok")
        s_w_hi_ok = sem("w_hi_ok")
        s_w_lo_ok = sem("w_lo_ok")
        s_half_done = sem("half_done")
        s_acc_evac = sem("acc_evac")
        s_scr_full = sem("scr_full")
        s_f_abs = sem("f_abs")
        s_f_log = sem("f_log")
        s_m_ok = sem("m_ok")
        s_srow_ok = sem("srow_ok")
        s_rows_ok = sem("rows_ok")
        s_srow_exp = sem("srow_exp")
        s_vm_ones = sem("vm_ones")
        s_kmul_ok = sem("kmul_ok")
        s_kred_ok = sem("kred_ok")
        s_samp_dve = sem("samp_dve")
        s_samp_sub = sem("samp_sub")
        s_samp_exp = sem("samp_exp")
        s_pv_end_ok = sem("pv_end_ok")
        s_sm_b_ok = sem("sm_b_ok")
        s_C_decayed = sem("C_decayed")
        s_sm_dve = sem("sm_dve")
        s_sm_pow = sem("sm_pow")
        s_sm_end = sem("sm_end")
        s_ml_tri = sem("ml_tri")
        s_ml_ms = sem("ml_ms")
        s_ml_pow = sem("ml_pow")
        s_ml_hr = sem("ml_hr")
        s_ml_wend = sem("ml_wend")
        s_ml_kw = sem("ml_kw")
        s_att_nmax = sem("att_nmax")
        s_norm_ok = sem("norm_ok")
        s_own_head = sem("own_head")
        s_pv_used = sem("pv_used")
        s_v_hi = sem("v_hi")
        s_v_lo = sem("v_lo")
        s_p_hi = sem("p_hi")
        s_p_lo = sem("p_lo")
        s_pv_sum = sem("pv_sum")
        s_pv_tok = sem("pv_tok")
        s_om_exp = sem("om_exp")
        s_gated = sem("gated")
        s_mix_hi = sem("mix_hi")
        s_mix_lo = sem("mix_lo")
        s_x1_sq = sem("x1_sq")
        s_sq_added = sem("sq_added")
        s_rs2_ms = sem("rs2_ms")
        s_rs2_pow = sem("rs2_pow")
        s_x2_hi = sem("x2_hi")
        s_x2_lo = sem("x2_lo")
        s_hs_hi = sem("hs_hi")
        s_hs_lo = sem("hs_lo")
        s_y_sq = sem("y_sq")
        s_y_ms_ok = sem("y_ms_ok")
        s_y_pow = sem("y_pow")
        s_out_v = sem("out_v")
        s_out_small = sem("out_small")
        s_out_C = sem("out_C")
        s_y_st0 = sem("y_st0")
        s_y_st1 = sem("y_st1")
        s_dve_chain = sem("dve_chain")
        s_act_chain = sem("act_chain")
        s_pool_chain = sem("pool_chain")
        scr_free = [sem(f"scr_free{i}") for i in range(4)]
        kv_in = [sem(f"kv_in{i}") for i in range(PAGES)]
        raw_in = [s_raw0, s_raw1]
        x_in = [s_x_in0, s_x_in1, s_x_in2, s_x_in3, s_x_in4]
        C_in = [s_C_in0, s_C_in1, s_C_in2, s_C_in3]
        C_out = [s_C_out0, s_C_out1, s_C_out2, s_C_out3]
        k_out = [s_k_out0, s_k_out1]
        st_y = [s_y_st0, s_y_st1]

        def bank(*key):
            return scr[:, JOBS[key] % 4, :]

        def open_job(pe, *key):
            n = JOBS[key]
            if n >= 4:
                pe.wait_ge(scr_free[n % 4], n // 4)
            return scr[:, n % 4, :]

        def full(eng, *key):
            eng.wait_ge(s_scr_full, JOBS[key] + 1)
            return bank(*key)

        def free(ins, *key):
            ins.then_inc(scr_free[JOBS[key] % 4], 1)

        def evacuated(eng, *key):
            n = JOBS[key]
            eng.wait_ge(scr_free[n % 4], n // 4 + 1)

        def lookahead(g):
            return g + AHEAD if g + AHEAD < N_MAIN else None

        block = ctx.enter_context(nc.Block())

        A_COL = [0, 512, 896, 1152]
        P_COL = [0, 128, 384, 768]

        def tiles(t):
            return [t[:, k, :] for k in range(t.shape[1])]

        x_parts = tiles(act_hi), tiles(act_lo)
        h_parts = tiles(h_hi), tiles(h_lo)
        page_pairs = {"vp_a": (0, 1), "vp_b": (2, 3)}
        mix_parts = tiles(mix_hi), tiles(mix_lo_att) + tiles(mix_lo_ml)

        @block.sync
        def _(sp):
            for i in range(NT):
                sp.dma_start(x_tok[:, i, :], x_prompt[0, i * P:(i + 1) * P, :]).then_inc(x_in[i], 16)

            def unit(r, src, first=True):
                if r >= 2:
                    sp.wait_ge(s_w_lo_ok, 2 * (r - 1))
                sp.dma_start(raw[:, r % 2, :, :], src.rearrange("(k p) n -> p k n", p=P))\
                  .then_inc(raw_in[r % 2], 16)

            def in_unit(r):
                c = IN_ORDER[2 * r] * P
                unit(r, w_in[0, :, c:c + 2 * P])

            def pages(cache, b, step):
                for j in range(PAGES):
                    page = sp.value_load(pt[0:1, b * PAGES + j:b * PAGES + j + 1], min_val=0, max_val=n_phys - 1)
                    if 1 <= step <= NS:
                        sp.wait_ge(s_kmul_ok, 4 * (step - 1) + j // 2 + 1)
                    elif step > NS:
                        sp.wait_ge(s_v_lo, 4 * (b - 1) + j // 2 + 1)
                    src = cache[0, bass.ds(page, 1), :, :, :].rearrange("o p h d -> p (o h d)")
                    sp.dma_start(kv[:, j, :], src).then_inc(kv_in[j], 16)

            in_unit(0)
            in_unit(1)
            sp.wait_ge(s_pt_in, 16)
            evacuated(sp, "xn", KT - 1)
            evacuated(sp, "xn", KT)
            pages(cache_k, 0, 0)
            for r in range(2, 14):
                in_unit(r)
                if 1 <= r - 5 < NS:
                    pages(cache_k, r - 5, r - 5)
                elif r - 5 == NS:
                    pages(cache_v, 0, NS)
            unit(14, w_out[0, :, 0:2 * P])
            unit(15, w_out[0, :, 2 * P:4 * P])
            for b in range(1, NS):
                pages(cache_v, b, NS + b)
            for i in range(NT):
                sp.wait_ge(s_v_lo, 4 * (NS - 1) + i + 1)
                sp.dma_start(x_tok2[:, i, :], x_prompt[0, i * P:(i + 1) * P, :]).then_inc(s_x2_in, 16)
            full(sp, "pv", NS - 1, 0)
            sp.dma_start(x_s2[:, :], x_sample[:, 0, :]).then_inc(s_x2s_in, 16)
            sp.wait_ge(s_pv_end_ok, 2)
            sp.dma_start(lnf_b[:, :], lnf_w.rearrange("(o n) -> o n", o=1).broadcast_to([P, D])
                         ).then_inc(s_lnf_in, 16)
            for r in range(16, 18):
                unit(r, w_out[0, :, (r - 14) * 2 * P:(r - 13) * 2 * P])

            def mlp(i):
                for u in range(8):
                    r = 18 + 8 * i + u
                    sp.wait_ge(s_w_lo_ok, 2 * (r - 1))
                    if u < 4:
                        src = w_up[0, :, bass.ds(i * D + u * 2 * P, 2 * P)]
                    else:
                        src = w_down[0, bass.ds(i * D, D), (u - 4) * 2 * P:(u - 3) * 2 * P]
                    sp.dma_start(raw[:, u % 2, :, :], src.rearrange("(k p) n -> p k n", p=P))\
                      .then_inc(raw_in[u % 2], 16)

            with sp.Fori(0, QUARTERS) as i:
                mlp(i)
            for i in range(NT + 1):
                evacuated(sp, "yt", i, 0)
                evacuated(sp, "yt", i, 1)
                if i < NT:
                    sp.dma_start(y_prompt[0, i * P:(i + 1) * P, :], y_out[:, i % 2, :]).then_inc(st_y[i % 2], 16)
                else:
                    sp.dma_start(y_sample[:, 0, :], y_out[0:NS, i % 2, :]).then_inc(st_y[i % 2], 16)
            sp.wait_ge(s_y_st0, 48)
            sp.wait_ge(s_y_st1, 32)

        @block.tensor
        def _(pe):
            def main(g, slot, side, parts, k_ready=None, order=range(KT), between=None):
                hi, lo = parts
                pe.wait_ge(s_w_lo_ok, g + 1)

                def three(half, n, k):
                    cols = slice(half * HALF, (half + 1) * HALF)
                    out = acc[:, 2 * side + half, 0:HALF]
                    pe.matmul(out, w_hi[:, slot, k, :], hi[k][:, cols], start=(n == 0), stop=False)
                    pe.matmul(out, w_hi[:, slot, k, :], lo[k][:, cols], start=False, stop=False)
                    mm = pe.matmul(out, w_lo[:, slot, k, :], hi[k][:, cols], start=False, stop=(n == KT - 1))
                    if n == KT - 1:
                        mm.then_inc(s_half_done, 1)

                def bank_free(half):
                    if not isinstance(g, int) or g >= 2:
                        pe.wait_ge(s_acc_evac, 2 * (g - 2) + half + 1)

                if k_ready is not None:
                    bank_free(1)
                    for n, k in enumerate(order):
                        k_ready(n)
                        three(0, n, k)
                        three(1, n, k)
                    return
                for half in range(2):
                    bank_free(half)
                    for n, k in enumerate(order):
                        three(half, n, k)
                    if half == 0 and between is not None:
                        between()

            def done(mm):
                mm.then_inc(s_scr_full, 1)

            def to_tok(key, tiles, cols, n):
                out = open_job(pe, *key)
                for t in range(4):
                    mm = pe.transpose(out[0:n, t * P:(t + 1) * P], zT[:, tiles + t, cols], ident[:, :])
                done(mm)

            def every(col, n=P):
                return col.to_broadcast([n, P])

            pe.wait_ge(s_ident_ok, 4)
            pe.wait_ge(s_par_in, 48)
            out = open_job(pe, "param", 0)
            done(pe.transpose(out[:, 0:20], par_rows[:, :], ident[0:20, 0:20]))
            for j in range(KT):
                out = open_job(pe, "xn", j)
                for i in range(NT):
                    if j == 0:
                        pe.wait_ge(s_xn_ready, i + 1)
                    mm = pe.transpose(out[:, i * P:(i + 1) * P], x_tok[:, i, j * P:(j + 1) * P], ident[:, :])
                done(mm)
            out = open_job(pe, "xn", KT)
            pe.wait_ge(s_xn_ready, NT + 1)
            for j in range(KT):
                mm = pe.transpose(out[:, j * NS:(j + 1) * NS], x_s[:, j * P:(j + 1) * P], ident[0:NS, 0:NS])
            done(mm)
            pe.wait_ge(s_wg_lo_ok, 2)
            for j in range(KT):
                evacuated(pe, "xn", j)
            pe.wait_ge(s_xs_ok, 1)
            for half in range(2):
                cols = slice(half * HALF, (half + 1) * HALF)
                out = open_job(pe, "gates", half)[:, 0:HALF]
                for k in range(KT):
                    pe.matmul(out, wg_hi[:, k, :], act_hi[:, k, cols], start=(k == 0), stop=False)
                    pe.matmul(out, wg_hi[:, k, :], act_lo[:, k, cols], start=False, stop=False)
                    mm = pe.matmul(out, wg_lo[:, k, :], act_hi[:, k, cols], start=False, stop=(k == KT - 1))
                done(mm)

            def task(name, *a):
                if name == "gcols":
                    pe.wait_ge(s_rows_ok, 1)
                    out = open_job(pe, "gcols", 0)
                    for r, row in enumerate((3, 5)):
                        for i in range(NT):
                            mm = pe.transpose(out[:, (r * NT + i) * MH:(r * NT + i + 1) * MH],
                                              rows[:, row, i * P:(i + 1) * P], ident[0:4, 0:4])
                    done(mm)
                elif name == "qs_tok":
                    pe.wait_ge(s_acc_evac, z_ready(QA + 3))
                    to_tok(("qs_tok", 0), QA, slice(SEQ, TOK), NS)
                elif name == "vs_tok":
                    pe.wait_ge(s_acc_evac, z_ready(VM + 3))
                    to_tok(("vs_tok", 0), VM, slice(SEQ, TOK), NS)
                elif name == "ks_tok":
                    to_tok(("ks_tok", 0), KA, slice(SEQ, TOK), NS)
                elif name == "va_s":
                    to_tok(("va_s", 0), VA, slice(SEQ, TOK), NS)
                elif name == "tok":
                    group, i = a
                    pe.wait_ge(s_acc_evac, z_ready(group + 3))
                    to_tok(("tok", group, i, 0), group, slice(i * P, (i + 1) * P), P)
                elif name == "qb":
                    b, = a
                    evacuated(pe, "qs_tok", 0)
                    out = open_job(pe, "qb", b, 0)
                    done(pe.matmul(out, every(ident[0:NS, b:b + 1], NS), qs_tok[:, :], start=True, stop=True))
                elif name == "sm_prep":
                    out = open_job(pe, "sm_prep", 0)
                    for h in range(MH):
                        mm = pe.matmul(out[:, h * 3 * NS:(h + 1) * 3 * NS], every(ident[0:4, h:h + 1], 4),
                                       s_rows[:, :, :].rearrange("p a b -> p (a b)"), start=True, stop=True)
                    done(mm)
                    pe.wait_ge(s_n_in, 16)
                    out = open_job(pe, "sm_prep", 1)
                    done(pe.transpose(out[:, 0:NS * MH], n_rows[:, :], ident[0:NS * MH, 0:NS * MH]))
                elif name == "sm_c":
                    b, = a
                    evacuated(pe, "vs_tok", 0)
                    out = open_job(pe, "sm_c", b, 0)
                    done(pe.matmul(out, every(ident[0:NS, b:b + 1], NS), vs_tok[:, :], start=True, stop=True))
                elif name == "sm_r":
                    b, = a
                    evacuated(pe, "sm_c", b, 0)
                    out = open_job(pe, "sm_r", b, 0)
                    for h in range(MH):
                        mm = pe.matmul(out[:, h:h + 1], Cs[:, b % 4, h, :], zT[:, QM + h, SEQ + b:SEQ + b + 1],
                                       start=True, stop=True)
                    done(mm)
                elif name == "sm_den":
                    pe.wait_ge(s_sm_dve, 1)
                    out = open_job(pe, "sm_den", 0)
                    done(pe.matmul(out[:, 0:NS * MH], every(ones[:, :]), sm_q[:, :, :].rearrange("p a b -> p (a b)"),
                                   start=True, stop=True))
                elif name == "sm_out":
                    pe.wait_ge(s_sm_dve, 2)
                    out = open_job(pe, "sm_out", 0)
                    done(pe.matmul(out[:, 0:NS * MH], every(ones[:, :]), sm_t[:, :, :].rearrange("p a b -> p (a b)"),
                                   start=True, stop=True))
                    out = open_job(pe, "sm_out", 1)
                    done(pe.transpose(out[0:NS * MH, 0:P], sm_n[:, :, :].rearrange("p a b -> p (a b)"), ident[:, :]))
                elif name == "ml_a":
                    h, = a
                    out = open_job(pe, "ml_a", h, 0)
                    done(pe.matmul(out, every(ident[0:4, h:h + 1], 4), M_row[:, 0:SEQ], start=True, stop=True))
                    for n, parts in enumerate(((0,), (1,), (2, 3))):
                        out = open_job(pe, "ml_a", h, n + 1)
                        col = 0
                        for j in parts:
                            w = SEQ - j * P
                            mm = pe.matmul(out[:, col:col + w], zT[:, KM + h, j * P:(j + 1) * P],
                                           zT[:, QM + h, j * P:SEQ], start=True, stop=True)
                            col += w
                        done(mm)
                elif name == "ml_o":
                    h, = a
                    if h == 0:
                        for i in range(NT):
                            evacuated(pe, "tok", VM, i, 0)
                    for n in range(3):
                        evacuated(pe, "ml_a", h, n + 1)
                    for half in range(2):
                        out = open_job(pe, "ml_o", h, half)
                        for n, i in enumerate((2 * half, 2 * half + 1)):
                            for j in range(i + 1):
                                mm = pe.matmul(out[:, n * (MD + 1):(n + 1) * (MD + 1)],
                                               mA[:, h % 2, A_COL[j] + (i - j) * P:A_COL[j] + (i - j + 1) * P],
                                               vm_tok[:, j, h, :], start=(j == 0), stop=(j == i))
                        done(mm)
                elif name == "ml_t":
                    h, = a
                    pe.wait_ge(s_ml_hr, h + 1)
                    out = open_job(pe, "ml_t", h, 0)
                    for i in range(NT):
                        mm = pe.transpose(out[:, i * P:(i + 1) * P], m_h[:, i, :], ident[:, :])
                    done(mm)
                elif name == "ml_mc":
                    h, = a
                    pe.wait_ge(s_ml_kw, h + 1)
                    out = open_job(pe, "ml_mc", h, 0)
                    for j in range(NT):
                        mm = pe.matmul(out[:, 0:MD + 1], m_kw[:, j, :], vm_tok[:, j, h, :],
                                       start=(j == 0), stop=(j == NT - 1))
                    done(mm)
                elif name == "gate":
                    pe.wait_ge(s_kred_ok, 4 * NS)
                    out = open_job(pe, "gate", 0)
                    done(pe.matmul(out, every(ones[:, :]), S[:, :, :, :].rearrange("p b g h -> p (b g h)"),
                                   start=True, stop=True))
                elif name == "mx_t":
                    pe.wait_ge(s_samp_dve, 1)
                    out = open_job(pe, "mx_t", 0)
                    done(pe.transpose(out[0:NS * AH, 0:P], page_max[:, :, :].rearrange("p b h -> p (b h)"),
                                      ident[:, :]))
                elif name == "own":
                    pe.wait_ge(s_samp_dve, 2)
                    out = open_job(pe, "own", 0)
                    for odd in range(2):
                        mm = pe.matmul(out[:, odd * 32:(odd + 1) * 32], every(even[:, odd:odd + 1]),
                                       own_prod[:, :, :].rearrange("p t b -> p (t b)"), start=True, stop=True)
                    done(mm)
                elif name == "mx_b":
                    evacuated(pe, "mx_t", 0)
                    out = open_job(pe, "mx_b", 0)
                    done(pe.matmul(out[:, 0:NS * AH], every(mx_col[:, :], NS * AH), ident[0:NS * AH, 0:NS * AH],
                                   start=True, stop=True))
                elif name == "zsum":
                    pe.wait_ge(s_samp_dve, 3)
                    out = open_job(pe, "zsum", 0)
                    done(pe.matmul(out[:, 0:NS * AH], every(ones[:, :]),
                                   page_max[:, :, :].rearrange("p b h -> p (b h)"), start=True, stop=True))
                elif name == "pv":
                    b, = a
                    pe.wait_ge(s_p_lo, 1)
                    out = open_job(pe, "pv", b, 0)
                    for j in range(PAGES):
                        pe.wait_ge(s_v_lo, 4 * b + j // 2 + 1)
                        pe.matmul(out[0:2 * AH, :], S_split[:, b, j, :], v_hi[:, j, 0:AW], start=(j == 0), stop=False)
                        mm = pe.matmul(out[0:2 * AH, :], S_split[:, b, j, :], v_lo[:, j, 0:AW], start=False,
                                       stop=(j == PAGES - 1))
                        if j in (1, 3, 5):
                            mm.then_inc(s_pv_used, 1)
                    done(mm)
                elif name == "pv_sum":
                    b, = a
                    evacuated(pe, "pv", b, 0)
                    if b == 0:
                        pe.wait_ge(s_acc_evac, 2 * (N_IN - 1))
                    pe.matmul(acc[0:NS, 0, :], pick[:, NS - 1 - b:2 * NS - 1 - b], pv_masked[:, b % 2, :],
                              start=(b == 0), stop=(b == NS - 1)).then_inc(s_pv_sum, 1)
                elif name == "pv_end":
                    pe.wait_ge(s_pv_tok, 1)
                    out = open_job(pe, "pv_end", 0)
                    for t in range(4):
                        mm = pe.transpose(out[:, t * NS:(t + 1) * NS], pv_tok[:, t * P:(t + 1) * P],
                                          ident[0:NS, 0:NS])
                    done(mm)
                elif name == "att_s":
                    h, = a
                    t, lo = h // 2, 64 * (h % 2)
                    for n, parts in enumerate(((0, 1), (2,), (3,))):
                        out = open_job(pe, "att_s", h, n)
                        col = 0
                        for i in parts:
                            w = (i + 1) * P
                            mm = pe.matmul(out[:, col:col + w], zT[lo:lo + 64, QA + t, i * P:(i + 1) * P],
                                           zT[lo:lo + 64, KA + t, 0:w], start=True, stop=True)
                            col += w
                        done(mm)
                elif name == "att_t":
                    h, = a
                    pe.wait_ge(s_norm_ok, h + 1)
                    for n in range(3):
                        evacuated(pe, "att_s", h, n)
                    for n, parts in enumerate(((0,), (1,), (2, 3))):
                        out = open_job(pe, "att_t", h, n)
                        for j in parts:
                            for i in range(j, NT):
                                col = A_COL[j] - A_COL[parts[0]] + (i - j) * P
                                mm = pe.matmul(out[:, col:col + P],
                                               pr[:, h % 2, P_COL[i] + j * P:P_COL[i] + (j + 1) * P],
                                               p_norm[:, h % 2, i, :], start=True, stop=True)
                        done(mm)
                elif name == "att_o":
                    h, = a
                    if h == 0:
                        for i in range(NT):
                            evacuated(pe, "tok", VA, i, 0)
                    pair = slice(h // 2 * P, (h // 2 + 1) * P)
                    out = open_job(pe, "att_o", h, 0)
                    for j in range(NT):
                        if j < 3:
                            evacuated(pe, "att_t", h, j)
                        mm = pe.matmul(out[:, j * P:SEQ], v_tok[:, j, pair], pT[:, A_COL[j]:A_COL[j] + SEQ - j * P],
                                       start=(j == 0), stop=(j == NT - 1))
                    done(mm)
                elif name == "xt":
                    j, = a
                    pe.wait_ge(s_x2_in, 16 * NT)
                    out = open_job(pe, "xt", j, 0)
                    for i in range(NT):
                        mm = pe.transpose(out[:, i * P:(i + 1) * P], x_tok2[:, i, j * P:(j + 1) * P], ident[:, :])
                    done(mm)
                elif name == "xt_s":
                    pe.wait_ge(s_x2s_in, 16)
                    out = open_job(pe, "xt_s", 0)
                    for j in range(KT):
                        mm = pe.transpose(out[:, j * NS:(j + 1) * NS], x_s2[:, j * P:(j + 1) * P],
                                          ident[0:NS, 0:NS])
                    done(mm)

            def sums_of_squares():
                pe.wait_ge(s_sq_added, KT - 1)
                out = open_job(pe, "sumsq", 0)
                for i in range(NT + 1):
                    n = P if i < NT else NS
                    mm = pe.matmul(out[0:n, i:i + 1], sq_sum[:, i * P:i * P + n], ones[:, :],
                                   start=True, stop=True)
                done(mm)

            def norm_to_rows():
                pe.wait_ge(s_rs2_pow, 2)
                for half, parts in enumerate((range(NT), (NT,))):
                    out = open_job(pe, "rstd2", half)
                    for n, c in enumerate(parts):
                        m = P if c < NT else NS
                        mm = pe.matmul(out[:, n * P:n * P + m], every(rs[0:m, c:c + 1], m),
                                       ident[0:m, 0:m], start=True, stop=True)
                    done(mm)

            for g in range(N_IN):
                main(g, g % WSLOTS, g % 2, x_parts)
                for name in TASKS[g]:
                    task(*name)
            for g in range(G_OUT, G_MLP):
                def mixed(k):
                    pe.wait_ge(s_mix_lo, k + 1)
                main(g, g % WSLOTS, g % 2, mix_parts, mixed if g == G_OUT else None, MIX_ORDER)
                for name in TASKS[g]:
                    task(*name)

            def quarter(i, first):
                for t in range(16):
                    g = G_MLP + 16 * i + t
                    if t < 8:
                        def normed(k):
                            pe.wait_ge(s_x2_lo, k + 1)
                        main(g, t % WSLOTS, t % 2, x_parts, normed if first and t == 0 else None,
                             between=norm_to_rows if first and t == 1 else None)
                        if first and t == 0:
                            sums_of_squares()
                    else:
                        def hidden(k):
                            pe.wait_ge(s_hs_lo, 8 * i + k + 1)
                        main(g, t % WSLOTS, t % 2, h_parts, hidden if t == 8 else None)

            quarter(0, True)
            with pe.Fori(1, QUARTERS) as i:
                quarter(i, False)
            pe.wait_ge(s_acc_evac, 2 * N_MAIN)
            for i in range(NT + 1):
                n = P if i < NT else NS
                for part in range(2):
                    out = open_job(pe, "yt", i, part)
                    for j in range(4):
                        mm = pe.transpose(out[0:n, j * P:(j + 1) * P],
                                          xT[:, 4 * part + j, i * P:i * P + n], ident[:, :])
                    done(mm)

        def weight_hi(act, g, slot, r_slot, r_round):
            act.wait_ge(raw_in[r_slot], 16 * (r_round + 1))
            if not isinstance(g, int) or g >= WSLOTS:
                act.wait_ge(s_half_done, 2 * (g - WSLOTS + 1))
            side = slot % 2
            act.activation(w_hi[:, slot, :, :], raw[:, r_slot, :, side * P:(side + 1) * P], ACT.Copy)\
               .then_inc(s_w_hi_ok, 1)

        def weight_lo(eng, g, slot, r_slot):
            eng.wait_ge(s_w_hi_ok, g + 1)
            side = slot % 2
            eng.tensor_tensor(w_lo[:, slot, :, :], raw[:, r_slot, :, side * P:(side + 1) * P],
                               w_hi[:, slot, :, :].bitcast(F32), ALU.subtract).then_inc(s_w_lo_ok, 1)

        @block.scalar
        def _(act):
            chain = [0]

            def link(ins):
                chain[0] += 1
                ins.then_inc(s_act_chain, 1)
                act.wait_ge(s_act_chain, chain[0])

            def split(g):
                weight_hi(act, g, g % WSLOTS, g // 2 % 2, g // 4)

            act.dma_start(pt[:, :], page_table.rearrange("(o b) n -> o (b n)", o=1)).then_inc(s_pt_in, 16)
            act.dma_start(x_s[:, :], x_sample[:, 0, :]).then_inc(x_in[NT], 16)
            act.dma_start(par_rows[0:8, :], ln1_w.rearrange("o (k p) -> (o k) p", p=P)).then_inc(s_par_in, 16)
            act.dma_start(par_rows[8:16, :], ln2_w.rearrange("o (k p) -> (o k) p", p=P)).then_inc(s_par_in, 16)
            act.dma_start(par_rows[16:20, :], mlstm_norm_w.rearrange("o (k p) -> (o k) p", p=P))\
               .then_inc(s_par_in, 16)
            act.dma_start(wg_raw[:, :, :], w_in[0, :, GATE_COL:GATE_COL + 8].rearrange("(k p) n -> p k n", p=P))\
               .then_inc(s_wg_in, 16)
            act.dma_start(bias_i[:, :], b_gates[0:1, 0:4].rearrange("o n -> n o")).then_inc(s_small_in, 16)
            act.dma_start(bias_f[32:36, :], b_gates[0:1, 4:8].rearrange("o n -> n o")).then_inc(s_small_in, 16)
            act.dma_start(m0_row[:, :], state_m[0].rearrange("b h -> h b")).then_inc(s_small_in, 16)
            act.dma_start(n_rows[:, :], state_n[0].rearrange("b h d -> (b h) d")).then_inc(s_n_in, 16)
            for i in range(NT + 1):
                act.wait_ge(x_in[i], 16)
                n = P if i < NT else NS
                x = x_tok[:, i, :] if i < NT else x_s[:, :]
                if i >= 1:
                    act.wait_ge(s_x_sq_ok, i)
                act.activation(junk[0:n, :], x, ACT.Square, accum_out=ss[0:n, i:i + 1]).then_inc(s_x_sq_ok, 1)
            act.wait_ge(s_wg_in, 16)
            act.wait_ge(s_wg_zero, 2)
            act.activation(wg_hi[:, :, 0:4], wg_raw[:, :, 0:4], ACT.Copy).then_inc(s_wg_hi_ok, 1)
            act.activation(wg_hi[:, :, 32:36], wg_raw[:, :, 4:8], ACT.Copy).then_inc(s_wg_hi_ok, 1)
            out = full(act, "param", 0)
            ins = act.activation(par[:, :], out[:, 0:20], ACT.Copy)
            free(ins, "param", 0)
            evacuated(act, "param", 0)
            split(0)
            for j in range(KT):
                out = full(act, "xn", j)
                act.activation(act_hi[:, j, 0:SEQ], out, ACT.Copy, scale=par[:, j:j + 1]).then_inc(s_xhi_ok, 1)
                if j == 3:
                    split(1)
            split(2)

            def copy_out(dst, src, *key):
                free(act.activation(dst, src, ACT.Copy), *key)

            def task(name, *a):
                if name == "rows":
                    act.wait_ge(s_f_abs, 1)
                    link(act.activation(rows[:, 2, :], rows[:, 2, :], ACT.Exp, scale=-1.0))
                    act.activation(rows[:, 2, :], rows[:, 2, :], ACT.Ln, bias=1.0).then_inc(s_f_log, 1)
                    act.wait_ge(s_m_ok, 1)
                    act.activation(rows[:, 5, 0:SEQ], rows[:, 2, 0:SEQ], ACT.Exp, scale=-1.0)\
                       .then_inc(s_rows_ok, 1)
                    act.dma_start(m_prompt[0, 0:1, :].rearrange("o h -> h o"), rows[:, 2, SEQ - 1:SEQ])\
                       .then_inc(s_out_small, 16)
                    act.wait_ge(s_srow_ok, 1)
                    act.activation(s_rows[:, 0:2, :], s_rows[:, 0:2, :], ACT.Exp).then_inc(s_srow_exp, 1)
                    act.activation(s_rows[:, 2, :], m_s[:, :], ACT.Exp, scale=-1.0).then_inc(s_srow_exp, 1)
                    act.dma_start(m_sample[0].rearrange("b h -> h b"), m_s[:, :]).then_inc(s_out_small, 16)
                    for b in range(4):
                        load_state(b)
                elif name == "qs_tok":
                    copy_out(qs_tok[:, :], full(act, "qs_tok", 0)[0:NS, :], "qs_tok", 0)
                elif name == "vs_tok":
                    copy_out(vs_tok[:, :], full(act, "vs_tok", 0)[0:NS, :], "vs_tok", 0)
                elif name == "ks_tok":
                    act.wait_ge(s_kmul_ok, 4 * NS)
                    copy_out(Qb[0:NS, 0, :], full(act, "ks_tok", 0)[0:NS, :], "ks_tok", 0)
                    evacuated(act, "ks_tok", 0)
                    act.dma_start(k_sample[0, :, 0, :, :].rearrange("b h d -> b (h d)"), Qb[0:NS, 0, :])\
                       .then_inc(s_out_small, 16)
                elif name == "va_s":
                    copy_out(Qb[0:NS, 1, :], full(act, "va_s", 0)[0:NS, :], "va_s", 0)
                    evacuated(act, "va_s", 0)
                    act.dma_start(v_sample[0, :, 0, :, :].rearrange("b h d -> b (h d)"), Qb[0:NS, 1, :])\
                       .then_inc(s_out_small, 16)
                elif name == "qb":
                    b, = a
                    out = full(act, "qb", b, 0)
                    if b >= 2:
                        act.wait_ge(s_kmul_ok, 4 * (b - 1))
                    copy_out(Qb[:, b % 2, :], out, "qb", b, 0)
                elif name == "tok":
                    group, i = a
                    key = ("tok", group, i, 0)
                    out = full(act, *key)
                    if group == VM:
                        act.wait_ge(s_vm_ones, 1)
                        copy_out(vm_tok[:, i, :, 0:MD], out.rearrange("p (h d) -> p h d", h=MH), *key)
                    elif group == KM:
                        copy_out(km_tok[:, i, :], out, *key)
                    elif group == VA:
                        copy_out(v_tok[:, i, :], out, *key)
                        evacuated(act, *key)
                        act.dma_start(v_prompt[0, 0, i * P:(i + 1) * P, :, :].rearrange("t h d -> t (h d)"),
                                      v_tok[:, i, :]).then_inc(s_out_v, 16)
                    else:
                        if i >= 2:
                            act.wait_ge(k_out[i % 2], 16)
                        copy_out(k_stage[:, i % 2, :], out, *key)
                        evacuated(act, *key)
                        act.dma_start(k_prompt[0, 0, i * P:(i + 1) * P, :, :].rearrange("t h d -> t (h d)"),
                                      k_stage[:, i % 2, :]).then_inc(k_out[i % 2], 16)
                elif name == "sm_r":
                    b, = a
                    evacuated(act, "sm_c", b, 0)
                    act.dma_start(C_sample[0, b].rearrange("h d e -> d h e"), Cs[:, b % 4, :, :])\
                       .then_inc(C_out[b % 4], 16)
                    if 2 <= b < 6:
                        n = b - 2
                        full(act, "sm_r", n, 0)
                        act.wait_ge(C_out[n], 16)
                        load_state(n + 4)
                elif name == "sm_out":
                    evacuated(act, "sm_out", 1)
                    act.dma_start(n_sample[0].rearrange("b h d -> (b h) d"), n_new_rows[:, :])\
                       .then_inc(s_out_small, 16)
                elif name == "ml_a":
                    h, = a
                    out = full(act, "ml_a", h, 0)
                    if h == 0:
                        act.wait_ge(s_out_small, 32)
                        evacuated(act, "gcols", 0)
                    link(act.activation(MS[:, h:h + 1], out[:, SEQ - 1:SEQ], ACT.Copy, scale=-1.0))
                    act.activation(w_end[:, h, :], g_col[:, 0, :, h], ACT.Exp, bias=MS[:, h:h + 1])\
                       .then_inc(s_ml_wend, 1)
                    for j in range(NT):
                        w = SEQ - j * P
                        ins = act.activation(mA[:, h % 2, A_COL[j]:A_COL[j] + w], out[:, j * P:SEQ], ACT.Exp,
                                             scale=-1.0, bias=g_col[:, 0, j, h:h + 1])
                    free(ins, "ml_a", h, 0)
                elif name == "ml_t":
                    h, = a
                    out = full(act, "ml_t", h, 0)
                    free(act.activation(zT[:, QM + h, 0:SEQ], out, ACT.Copy, scale=par[:, 16 + h:17 + h]),
                         "ml_t", h, 0)
                elif name == "ml_mc":
                    h, = a
                    evacuated(act, "ml_mc", h, 0)
                    act.dma_start(C_prompt[0, 0, h, :, :], C_stage[:, h, :]).then_inc(s_out_C, 16)
                    if h == MH - 1:
                        act.dma_start(n_prompt[0, 0].rearrange("h d -> d h"), nc_col[:, :]).then_inc(s_out_C, 16)
                elif name == "mx_b":
                    act.wait_ge(s_samp_sub, 1)
                    flat = S[:, :, :, :].rearrange("p b g h -> p (b g h)")
                    act.activation(flat, flat, ACT.Exp, scale=ASCALE).then_inc(s_samp_exp, 1)
                    flat = own_p[:, :, :].rearrange("p b h -> p (b h)")
                    act.activation(flat, flat, ACT.Exp, scale=ASCALE).then_inc(s_samp_exp, 1)
                elif name == "att_s":
                    h, = a
                    if h == 0:
                        evacuated(act, "ml_t", MH - 1, 0)
                    for n, parts in enumerate(((0, 1), (2,), (3,))):
                        out = bank("att_s", h, n)
                        act.wait_ge(s_att_nmax, 3 * h + n + 1)
                        col = 0
                        for i in parts:
                            w = (i + 1) * P
                            ins = act.activation(pr[:, h % 2, P_COL[i]:P_COL[i] + w], out[:, col:col + w], ACT.Exp,
                                                 scale=ASCALE, bias=nmax[:, h % 2, i:i + 1],
                                                 accum_out=rsum[:, h % 2, i:i + 1])
                            col += w
                        free(ins, "att_s", h, n)
                elif name == "zsum":
                    act.wait_ge(s_out_C, 16 * (MH + 1))
                    act.activation(S_split[:, :, :, 0:AH], S[:, :, :, :], ACT.Copy).then_inc(s_p_hi, 1)
                elif name in ("vp_a", "vp_b"):
                    b, = a
                    if b == 0:
                        act.wait_ge(s_half_done, 2 * N_IN)
                    for n in page_pairs[name]:
                        for j in (2 * n, 2 * n + 1):
                            act.wait_ge(kv_in[j], 16 * (NS + b + 1))
                        if b >= 1:
                            if n < 3:
                                act.wait_ge(s_pv_used, 3 * (b - 1) + n + 1)
                            else:
                                full(act, "pv", b - 1, 0)
                        pair = slice(2 * n, 2 * n + 2)
                        act.activation(v_hi[:, pair, 0:AW], kv[:, pair, :], ACT.Copy).then_inc(s_v_hi, 1)
                elif name == "att_t":
                    h, = a
                    copy_out(pT[:, 0:A_COL[1]], full(act, "att_t", h, 0), "att_t", h, 0)
                    copy_out(pT[:, A_COL[2]:att], full(act, "att_t", h, 2)[:, 0:att - A_COL[2]], "att_t", h, 2)
                elif name == "att_o":
                    h, = a
                    own_rows = slice(64 * (h % 2), 64 * (h % 2) + 64)
                    out = full(act, "att_o", h, 0)
                    copy_out(zT[own_rows, QA + h // 2, 0:SEQ], out[own_rows, :], "att_o", h, 0)
                elif name == "om":
                    h, = a
                    act.wait_ge(s_acc_evac, z_ready(OM + h))
                    act.activation(zT[:, OM + h, :], zT[:, OM + h, :], ACT.Exp, scale=-1.0).then_inc(s_om_exp, 1)
                elif name == "mix":
                    n, = a
                    j = MIX_ORDER[n]
                    if j < 4:
                        act.wait_ge(s_pv_end_ok, 2)
                        evacuated(act, "att_o", 2 * j, 0)
                        evacuated(act, "att_o", 2 * j + 1, 0)
                        src = zT[:, QA + j, :]
                    else:
                        act.wait_ge(s_gated, j - 3)
                        src = zT[:, QM + j - 4, :]
                    act.activation(mix_hi[:, j, :], src, ACT.Copy).then_inc(s_mix_hi, 1)
                elif name == "xt":
                    j, = a
                    out = full(act, "xt", j, 0)
                    if j == 0:
                        act.wait_ge(s_mix_lo, KT)
                        act.wait_ge(s_out_small, 16 * 5)
                    copy_out(xT[:, j, 0:SEQ], out, "xt", j, 0)
                elif name == "xt_s":
                    copy_out(xT[:, :, SEQ:TOK], full(act, "xt_s", 0)[:, 0:KT * NS].rearrange("p (j b) -> p j b", j=KT),
                             "xt_s", 0)
                elif name == "x2":
                    j, = a
                    act.wait_ge(s_acc_evac, 2 * (G_OUT + j + 1))
                    act.activation(act_hi[:, j, :], xT[:, j, :], ACT.Copy, scale=par[:, 8 + j:9 + j])\
                       .then_inc(s_x2_hi, 1)
                    if j >= 2:
                        act.wait_ge(s_sq_added, max(j - 2, 1))
                    act.activation(x_sq[:, j % 2, :], xT[:, j, :], ACT.Square).then_inc(s_x1_sq, 1)

            def load_state(b):
                act.dma_start(Cs[:, b % 4, :, :], state_C[0, b].rearrange("h d e -> d h e")).then_inc(C_in[b % 4], 16)

            for g in range(G_MLP):
                split(g + AHEAD)
                for name in TASKS[g]:
                    task(*name)

            def quarter(i, last):
                for t in range(16):
                    g = G_MLP + 16 * i + t
                    if not last or t + AHEAD < 16:
                        n = t + AHEAD
                        weight_hi(act, g + AHEAD, n % WSLOTS, n // 2 % 2, (G_MLP // 4) + 4 * i + n // 4)
                    if t < 8:
                        act.wait_ge(s_acc_evac, 2 * (g + 1))
                        if t >= 2:
                            act.wait_ge(s_hs_lo, 8 * i + t - 1)
                        act.activation(relu2[:, t % 2, :], relu[:, t % 2, :], ACT.Square)
                        act.activation(h_hi[:, t, :], relu[:, t % 2, :], ACT.Square).then_inc(s_hs_hi, 1)

            with act.Fori(0, QUARTERS - 1) as i:
                quarter(i, False)
            quarter(QUARTERS - 1, True)
            for i in range(NT + 1):
                n = P if i < NT else NS
                for part in range(2):
                    out = full(act, "yt", i, part)
                    if i + part >= 1:
                        act.wait_ge(s_y_sq, 2 * i + part)
                    act.activation(y_junk[0:n, :], out[0:n, :], ACT.Square, accum_out=y_ss[0:n, i, part:part + 1])\
                       .then_inc(s_y_sq, 1)
            act.wait_ge(s_out_v, 16 * NT)
            act.wait_ge(s_out_C, 16 * (MH + 1))
            act.wait_ge(s_out_small, 16 * 5)
            act.wait_ge(s_k_out0, 32)
            act.wait_ge(s_k_out1, 32)
            for b in range(4):
                act.wait_ge(C_out[b], 32)

        @block.gpsimd
        def _(pool):
            def rsqrt(x, n, free_size):
                return pool.tensor_tensor(x, x, power[0:n, :].to_broadcast([n, free_size]), ALU.pow)

            pool.memset(ident[:, :], 0.0).then_inc(s_pool_chain, 1)
            pool.memset(causal[:, :], 0.0).then_inc(s_pool_chain, 1)
            pool.memset(ones[:, :], 1.0).then_inc(s_ones_ok, 1)
            pool.memset(power[:, :], -0.5).then_inc(s_pool_chain, 1)
            pool.memset(even[:, :], 0.0).then_inc(s_pool_chain, 1)
            pool.memset(pick[:, :], 0.0).then_inc(s_pool_chain, 1)
            pool.memset(wg_hi[:, :, :].bitcast(F32), 0.0).then_inc(s_wg_zero, 1)
            pool.memset(wg_lo[:, :, :].bitcast(F32), 0.0).then_inc(s_wg_zero, 1)
            pool.wait_ge(s_pool_chain, 5)
            pool.memset(pick[:, NS - 1:NS], 1.0).then_inc(s_ident_ok, 1)
            pool.affine_select(out=ident[:, :], in_=ident[:, :], compare_op=ALU.not_equal, fill=1.0, base=0,
                               pattern=[[-1, P]], channel_multiplier=1).then_inc(s_ident_ok, 1)
            pool.affine_select(out=causal[:, :], in_=causal[:, :], compare_op=ALU.is_ge, fill=MASKED, base=0,
                               pattern=[[-1, P]], channel_multiplier=1).then_inc(s_causal_ok, 1)
            pool.affine_select(out=even[:, 0:1], in_=even[:, 0:1], compare_op=ALU.is_ge, fill=1.0, base=-64,
                               pattern=[[1, 1]], channel_multiplier=1).then_inc(s_ident_ok, 1)
            pool.affine_select(out=even[:, 1:2], in_=even[:, 1:2], compare_op=ALU.is_ge, fill=1.0, base=63,
                               pattern=[[1, 1]], channel_multiplier=-1).then_inc(s_ident_ok, 1)
            for i in range(NT + 1):
                n = P if i < NT else NS
                pool.wait_ge(s_x_ms_ok, i + 1)
                rsqrt(rs[0:n, i:i + 1], n, 1).then_inc(s_x_rs_ok, 1)
            pool.wait_ge(s_wg_hi_ok, 2)
            pool.tensor_tensor(wg_lo[:, :, 0:4], wg_raw[:, :, 0:4], wg_hi[:, :, 0:4].bitcast(F32), ALU.subtract)\
                .then_inc(s_wg_lo_ok, 1)
            pool.tensor_tensor(wg_lo[:, :, 32:36], wg_raw[:, :, 4:8], wg_hi[:, :, 32:36].bitcast(F32),
                               ALU.subtract).then_inc(s_wg_lo_ok, 1)
            for g in range(AHEAD):
                weight_lo(pool, g, g % WSLOTS, g // 2 % 2)

            def task(name, *a):
                if name == "rows":
                    full(pool, "gates", 1)
                    pool.memset(vm_tok[:, :, :, MD:MD + 1], 1.0).then_inc(s_vm_ones, 1)
                elif name == "score":
                    b, c = a
                    n = 4 * b + c
                    if c == 0:
                        evacuated(pool, "qb", b, 0)
                    for j in (2 * c, 2 * c + 1):
                        pool.wait_ge(kv_in[j], 16 * (b + 1))
                    if n >= 2:
                        pool.wait_ge(s_kred_ok, n - 1)
                    pool.tensor_tensor(prod[:, n % 2, :].rearrange("p (j n) -> p j n", j=2),
                                       kv[:, 2 * c:2 * c + 2, :],
                                       Qb[:, b % 2:b % 2 + 1, :].to_broadcast([P, 2, AW]), ALU.mult)\
                        .then_inc(s_kmul_ok, 1)
                elif name == "sm_c":
                    b, = a
                    pool.wait_ge(s_sm_b_ok, 1)
                    pool.wait_ge(C_in[b % 4], 16 * (b // 4 + 1))
                    pool.tensor_tensor(Cs[:, b % 4, :, :], Cs[:, b % 4, :, :],
                                       sm_b[:, :, 0, b:b + 1].to_broadcast([P, MH, MD]), ALU.mult)\
                        .then_inc(s_C_decayed, 1)
                elif name == "sm_out":
                    evacuated(pool, "sm_out", 0)
                    rsqrt(sm_t[:, :, :].rearrange("p b h -> p (b h)"), P, NS * MH).then_inc(s_sm_pow, 1)
                elif name == "ml_a":
                    h, = a
                    evacuated(pool, "ml_a", h, 0)
                    for j in range(NT):
                        blk = mA[:, h % 2, A_COL[j]:A_COL[j] + P]
                        pool.affine_select(out=blk, in_=blk, compare_op=ALU.is_ge, fill=0.0, base=0,
                                           pattern=[[1, P]], channel_multiplier=-1).then_inc(s_ml_tri, 1)
                elif name == "ml_o":
                    h, = a
                    pool.wait_ge(s_ml_ms, h + 1)
                    rsqrt(m_rs[:, :], P, NT).then_inc(s_ml_pow, 1)
                elif name in ("vp_a", "vp_b"):
                    b, = a
                    for n in page_pairs[name]:
                        pool.wait_ge(s_v_hi, 4 * b + n + 1)
                        pair = slice(2 * n, 2 * n + 2)
                        pool.tensor_tensor(v_lo[:, pair, 0:AW], kv[:, pair, :], v_hi[:, pair, 0:AW].bitcast(F32),
                                           ALU.subtract).then_inc(s_v_lo, 1)

            for g in range(G_MLP):
                n = g + AHEAD
                if n >= DVE_LO:
                    if n == DVE_LO:
                        pool.wait_ge(s_w_lo_ok, DVE_LO)
                    weight_lo(pool, n, n % WSLOTS, n // 2 % 2)
                for name in TASKS[g]:
                    task(*name)
            pool.wait_ge(s_rs2_ms, 1)
            evacuated(pool, "sumsq", 0)
            rsqrt(rs[:, 0:NT], P, NT).then_inc(s_rs2_pow, 1)
            rsqrt(rs[0:NS, NT:NT + 1], NS, 1).then_inc(s_rs2_pow, 1)

            def quarter(i, last):
                for t in range(16):
                    g = G_MLP + 16 * i + t
                    if not last or t + AHEAD < 16:
                        n = t + AHEAD
                        weight_lo(pool, g + AHEAD, n % WSLOTS, n // 2 % 2)
                    if t < 8:
                        pool.wait_ge(s_hs_hi, 8 * i + t + 1)
                        pool.tensor_tensor(h_lo[:, t, :], relu2[:, t % 2, :], h_hi[:, t, :].bitcast(F32),
                                           ALU.subtract).then_inc(s_hs_lo, 1)

            with pool.Fori(0, QUARTERS - 1) as i:
                quarter(i, False)
            quarter(QUARTERS - 1, True)
            for i in range(NT + 1):
                n = P if i < NT else NS
                pool.wait_ge(s_y_ms_ok, i + 1)
                rsqrt(y_ms[0:n, i:i + 1], n, 1).then_inc(s_y_pow, 1)

        @block.vector
        def _(dve):
            chain = [0]

            def link(ins):
                chain[0] += 1
                ins.then_inc(s_dve_chain, 1)
                dve.wait_ge(s_dve_chain, chain[0])

            dve.wait_ge(s_ident_ok, 4)
            dve.tensor_tensor(own_head[:, :], ident[0:2 * AH, 0:AH], ident[0:2 * AH, AH:2 * AH], ALU.add)\
               .then_inc(s_own_head, 1)
            for i in range(NT + 1):
                n = P if i < NT else NS
                dve.wait_ge(s_x_sq_ok, i + 1)
                dve.tensor_scalar(rs[0:n, i:i + 1], ss[0:n, i:i + 1], 1.0 / D, EPS, ALU.mult, ALU.add)\
                   .then_inc(s_x_ms_ok, 1)
            for i in range(NT + 1):
                n = P if i < NT else NS
                x = x_tok[:, i, :] if i < NT else x_s[:, :]
                dve.wait_ge(s_x_rs_ok, i + 1)
                dve.tensor_scalar(x, x, rs[0:n, i:i + 1], None, ALU.mult).then_inc(s_xn_ready, 1)
            for j in range(KT):
                out = full(dve, "xn", j)
                dve.wait_ge(s_xhi_ok, j + 1)
                free(dve.scalar_tensor_tensor(out=act_lo[:, j, 0:SEQ], in0=out, scalar=par[:, j:j + 1],
                                              in1=act_hi[:, j, 0:SEQ].bitcast(F32), op0=ALU.mult,
                                              op1=ALU.subtract), "xn", j)
            out = full(dve, "xn", KT)[:, 0:KT * NS].rearrange("p (j b) -> p j b", j=KT)
            free(dve.tensor_tensor(xn_s[:, :, :], out, par[:, 0:KT].unsqueeze(2).to_broadcast([P, KT, NS]),
                                   ALU.mult), "xn", KT)
            evacuated(dve, "xn", KT)
            link(dve.tensor_copy(act_hi[:, :, SEQ:TOK], xn_s[:, :, :]))
            dve.tensor_tensor(act_lo[:, :, SEQ:TOK], xn_s[:, :, :], act_hi[:, :, SEQ:TOK].bitcast(F32),
                              ALU.subtract).then_inc(s_xs_ok, 1)

            def sample_bh(c):
                return zT[:, c:c + MH, SEQ:TOK].rearrange("p h b -> p b h")

            def heads(r):
                return sm_b[:, :, r, :].rearrange("p h b -> p b h")

            def per_page(x):
                return x[:, :, :].unsqueeze(2).to_broadcast([P, NS, PAGES, AH])

            def task(name, *a):
                if name == "rows":
                    dve.wait_ge(s_small_in, 48)
                    for half in range(2):
                        cols = slice(half * HALF, (half + 1) * HALF)
                        out = full(dve, "gates", half)
                        dve.tensor_scalar(rows[:, 0, cols], out[0:4, 0:HALF], bias_i[:, :], None, ALU.add)
                        free(dve.tensor_scalar(rows[:, 1, cols], out[32:36, 0:HALF], bias_f[32:36, :], None,
                                               ALU.add), "gates", half)
                    evacuated(dve, "gates", 0)
                    evacuated(dve, "gates", 1)
                    dve.scalar_tensor_tensor(out=rows[:, 2, :], in0=rows[:, 1, :], scalar=-1.0, in1=rows[:, 1, :],
                                             op0=ALU.mult, op1=ALU.max).then_inc(s_f_abs, 1)
                    dve.memset(rows[:, 5, :], 0.0)
                    dve.wait_ge(s_f_log, 1)
                    link(dve.scalar_tensor_tensor(out=rows[:, 1, :], in0=rows[:, 1, :], scalar=0.0,
                                                  in1=rows[:, 2, :], op0=ALU.min, op1=ALU.subtract))
                    link(dve.tensor_tensor_scan(rows[:, 4, 0:SEQ], rows[:, 1, 0:SEQ], rows[:, 5, 0:SEQ], 0.0,
                                                ALU.add, ALU.add))
                    link(dve.tensor_tensor(rows[:, 3, 0:SEQ], rows[:, 0, 0:SEQ], rows[:, 4, 0:SEQ], ALU.subtract))
                    link(dve.tensor_tensor_scan(M_row[:, 0:SEQ], rows[:, 3, 0:SEQ], rows[:, 3, 0:SEQ], 0.0,
                                                ALU.max, ALU.max))
                    dve.tensor_tensor(rows[:, 2, 0:SEQ], rows[:, 4, 0:SEQ], M_row[:, 0:SEQ], ALU.add)\
                       .then_inc(s_m_ok, 1)
                    i_s, lf_s = rows[:, 0, SEQ:TOK], rows[:, 1, SEQ:TOK]
                    link(dve.tensor_tensor(s_rows[:, 0, :], lf_s, m0_row[:, :], ALU.add))
                    link(dve.tensor_tensor(m_s[:, :], s_rows[:, 0, :], i_s, ALU.max))
                    dve.tensor_tensor(s_rows[:, 1, :], i_s, m_s[:, :], ALU.subtract)
                    dve.tensor_tensor(s_rows[:, 0, :], s_rows[:, 0, :], m_s[:, :], ALU.subtract)\
                       .then_inc(s_srow_ok, 1)
                elif name == "gcols":
                    out = full(dve, "gcols", 0)
                    free(dve.tensor_copy(g_col[:, :, :, :].rearrange("p r i h -> p (r i h)"),
                                         out[:, 0:2 * NT * MH]), "gcols", 0)
                elif name == "score":
                    b, c = a
                    n = 4 * b + c
                    dve.wait_ge(s_kmul_ok, n + 1)
                    dve.tensor_reduce(S[:, b, 2 * c:2 * c + 2, :].rearrange("p j h -> p (j h)"),
                                      prod[:, n % 2, :].rearrange("p (g d) -> p g d", d=AD), AX.X, ALU.add)\
                       .then_inc(s_kred_ok, 1)
                elif name == "sm_prep":
                    out = full(dve, "sm_prep", 0)
                    free(dve.tensor_copy(sm_b[:, :, :, :].rearrange("p h r b -> p (h r b)"),
                                         out[:, 0:MH * 3 * NS]), "sm_prep", 0)
                    evacuated(dve, "sm_prep", 0)
                    dve.tensor_tensor(sm_kw[:, :, :], zT[:, KM:KM + MH, SEQ:TOK], sm_b[:, :, 1, :], ALU.mult)\
                       .then_inc(s_sm_b_ok, 1)
                    out = full(dve, "sm_prep", 1)
                    free(dve.tensor_tensor(sm_n[:, :, :], out[:, 0:NS * MH].rearrange("p (b h) -> p b h", b=NS),
                                           heads(0), ALU.mult), "sm_prep", 1)
                    evacuated(dve, "sm_prep", 1)
                    dve.wait_ge(s_sm_b_ok, 1)
                    link(dve.tensor_tensor(sm_n[:, :, :], sm_n[:, :, :],
                                           sm_kw[:, :, :].rearrange("p h b -> p b h"), ALU.add))
                    dve.tensor_tensor(sm_q[:, :, :], sample_bh(QM), sm_n[:, :, :], ALU.mult).then_inc(s_sm_dve, 1)
                elif name == "sm_c":
                    b, = a
                    out = full(dve, "sm_c", b, 0)
                    dve.wait_ge(s_C_decayed, b + 1)
                    for h in range(MH):
                        ins = dve.scalar_tensor_tensor(out=Cs[:, b % 4, h, :], in0=out[:, h * MD:(h + 1) * MD],
                                                       scalar=sm_kw[:, h, b:b + 1], in1=Cs[:, b % 4, h, :],
                                                       op0=ALU.mult, op1=ALU.add)
                    free(ins, "sm_c", b, 0)
                elif name == "sm_r":
                    b, = a
                    out = full(dve, "sm_r", b, 0)
                    free(dve.tensor_copy(sm_h[:, b, :], out[:, 0:MH]), "sm_r", b, 0)
                elif name == "sm_den":
                    for b in range(NS):
                        evacuated(dve, "sm_r", b, 0)
                    out = full(dve, "sm_den", 0)[:, 0:NS * MH].rearrange("p (b h) -> p b h", b=NS)
                    link(dve.scalar_tensor_tensor(out=sm_t[:, :, :], in0=out, scalar=-MSCALE, in1=heads(2),
                                                  op0=ALU.mult, op1=ALU.max))
                    free(dve.scalar_tensor_tensor(out=sm_t[:, :, :], in0=out, scalar=MSCALE, in1=sm_t[:, :, :],
                                                  op0=ALU.mult, op1=ALU.max), "sm_den", 0)
                    evacuated(dve, "sm_den", 0)
                    link(dve.reciprocal(sm_t[:, :, :], sm_t[:, :, :]))
                    link(dve.scalar_tensor_tensor(out=sm_h[:, :, :], in0=sm_h[:, :, :], scalar=MSCALE,
                                                  in1=sm_t[:, :, :], op0=ALU.mult, op1=ALU.mult))
                    dve.tensor_tensor(sm_t[:, :, :], sm_h[:, :, :], sm_h[:, :, :], ALU.mult).then_inc(s_sm_dve, 1)
                elif name == "sm_out":
                    out = full(dve, "sm_out", 0)
                    free(dve.tensor_scalar(sm_t[:, :, :].rearrange("p b h -> p (b h)"), out[:, 0:NS * MH],
                                           1.0 / MD, EPS, ALU.mult, ALU.add), "sm_out", 0)
                    out = full(dve, "sm_out", 1)
                    free(dve.tensor_copy(n_new_rows[:, :], out[0:NS * MH, 0:P]), "sm_out", 1)
                    dve.wait_ge(s_sm_pow, 1)
                    link(dve.tensor_tensor(sm_h[:, :, :], sm_h[:, :, :], sm_t[:, :, :], ALU.mult))
                    dve.tensor_tensor(sample_bh(QM), sm_h[:, :, :],
                                      par[:, 16:20].unsqueeze(1).to_broadcast([P, NS, MH]), ALU.mult)\
                       .then_inc(s_sm_end, 1)
                elif name == "ml_a":
                    h, = a
                    for n, parts in enumerate(((0,), (1,), (2, 3))):
                        out = full(dve, "ml_a", h, n + 1)
                        col = 0
                        for j in parts:
                            w = SEQ - j * P
                            dve.wait_ge(s_ml_tri, 4 * h + j + 1)
                            blk = mA[:, h % 2, A_COL[j]:A_COL[j] + w]
                            ins = dve.scalar_tensor_tensor(out=blk, in0=out[:, col:col + w], scalar=MSCALE,
                                                           in1=blk, op0=ALU.mult, op1=ALU.mult)
                            col += w
                        free(ins, "ml_a", h, n + 1)
                elif name == "ml_o":
                    h, = a
                    if h >= 1:
                        full(dve, "ml_t", h - 1, 0)
                    for half in range(2):
                        out = full(dve, "ml_o", h, half)[:, 0:2 * (MD + 1)].rearrange("p (i e) -> p i e", i=2)
                        two = slice(2 * half, 2 * half + 2)
                        link(dve.scalar_tensor_tensor(out=m_den[:, two], in0=out[:, :, MD], scalar=-1.0,
                                                      in1=g_col[:, 1, two, h], op0=ALU.mult, op1=ALU.max))
                        link(dve.tensor_tensor(m_den[:, two], out[:, :, MD], m_den[:, two], ALU.max))
                        link(dve.reciprocal(m_den[:, two], m_den[:, two]))
                        free(dve.tensor_tensor(m_h[:, two, :], out[:, :, 0:MD],
                                               m_den[:, two].unsqueeze(2).to_broadcast([P, 2, MD]), ALU.mult),
                             "ml_o", h, half)
                    evacuated(dve, "ml_o", h, 0)
                    evacuated(dve, "ml_o", h, 1)
                    link(dve.tensor_tensor(m_kw[:, :, :], m_h[:, :, :], m_h[:, :, :], ALU.mult))
                    link(dve.tensor_reduce(m_ss[:, :], m_kw[:, :, :], AX.X, ALU.add))
                    dve.tensor_scalar(m_rs[:, :], m_ss[:, :], 1.0 / MD, EPS, ALU.mult, ALU.add).then_inc(s_ml_ms, 1)
                    dve.wait_ge(s_ml_pow, h + 1)
                    dve.tensor_tensor(m_h[:, :, :], m_h[:, :, :],
                                      m_rs[:, :].unsqueeze(2).to_broadcast([P, NT, MD]), ALU.mult)\
                       .then_inc(s_ml_hr, 1)
                elif name == "ml_kw":
                    h, = a
                    dve.wait_ge(s_ml_wend, h + 1)
                    if h == 0:
                        for i in range(NT):
                            evacuated(dve, "tok", KM, i, 0)
                    else:
                        full(dve, "ml_mc", h - 1, 0)
                    dve.tensor_tensor(m_kw[:, :, :], km_tok[:, :, h * MD:(h + 1) * MD],
                                      w_end[:, h, :].unsqueeze(2).to_broadcast([P, NT, MD]), ALU.mult)\
                       .then_inc(s_ml_kw, 1)
                elif name == "ml_mc":
                    h, = a
                    out = full(dve, "ml_mc", h, 0)
                    dve.tensor_copy(nc_col[:, h:h + 1], out[:, MD:MD + 1])
                    free(dve.tensor_copy(C_stage[:, h, :], out[:, 0:MD]), "ml_mc", h, 0)
                elif name == "gate":
                    out = full(dve, "gate", 0)
                    blocks = gate[:, :, :, :]
                    free(dve.tensor_reduce(blocks.rearrange("p b n h -> p (b n) h"),
                                           out.rearrange("p (m two h) -> p m h two", two=2, h=AH), AX.X, ALU.add),
                         "gate", 0)
                    evacuated(dve, "gate", 0)
                    link(dve.tensor_reduce(gate_min[:, :, :], blocks.rearrange("p b n h -> p b h n"), AX.X, ALU.min))
                    link(dve.tensor_tensor(blocks, blocks,
                                           gate_min[:, :, :].unsqueeze(2).to_broadcast([P, NS, 4, AH]),
                                           ALU.is_equal))
                    later = gate[:, :, 3, :]
                    for n, into in ((2, taken), (1, gate_min), (0, None)):
                        if into is not None:
                            link(dve.tensor_tensor(into[:, :, :], gate[:, :, n, :], later, ALU.max))
                        link(dve.tensor_tensor(gate[:, :, n, :], gate[:, :, n, :], later, ALU.is_gt))
                        if into is not None:
                            later = into[:, :, :]
                    link(dve.tensor_scalar(blocks, blocks, MASKED, None, ALU.mult))
                    by_page = S[:, :, :, :].rearrange("p b (n two) h -> p (b n) two h", two=2)
                    for two in range(2):
                        link(dve.tensor_tensor(by_page[:, :, two, :], by_page[:, :, two, :],
                                               blocks.rearrange("p b n h -> p (b n) h"), ALU.add))
                    dve.tensor_reduce(page_max[:, :, :], S[:, :, :, :].rearrange("p b g h -> p b h g"), AX.X,
                                      ALU.max).then_inc(s_samp_dve, 1)
                elif name == "mx_t":
                    out = full(dve, "mx_t", 0)
                    free(dve.reduce_max(mx_col[:, :], out[0:NS * AH, 0:P], AX.X), "mx_t", 0)
                    dve.tensor_tensor(own_prod[:, :, :], zT[:, QA:QA + 4, SEQ:TOK], zT[:, KA:KA + 4, SEQ:TOK],
                                      ALU.mult).then_inc(s_samp_dve, 1)
                elif name == "own":
                    out = full(dve, "own", 0)
                    for odd in range(2):
                        ins = dve.tensor_copy(own[:, :, :].rearrange("p b (t o) -> p t b o", o=2)[:, :, :, odd],
                                              out[:, odd * 32:(odd + 1) * 32].rearrange("p (t b) -> p t b", t=4))
                    free(ins, "own", 0)
                elif name == "mx_b":
                    evacuated(dve, "own", 0)
                    out = full(dve, "mx_b", 0)[:, 0:NS * AH].rearrange("p (b h) -> p b h", b=NS)
                    free(dve.tensor_tensor(smax[:, :, :], out, own[:, :, :], ALU.max), "mx_b", 0)
                    evacuated(dve, "mx_b", 0)
                    dve.tensor_tensor(own_p[:, :, :], own[:, :, :], smax[:, :, :], ALU.subtract)
                    dve.tensor_tensor(S[:, :, :, :], S[:, :, :, :], per_page(smax), ALU.subtract)\
                       .then_inc(s_samp_sub, 1)
                    dve.wait_ge(s_samp_exp, 1)
                    dve.tensor_reduce(page_max[:, :, :], S[:, :, :, :].rearrange("p b g h -> p b h g"), AX.X,
                                      ALU.add).then_inc(s_samp_dve, 1)
                elif name == "zsum":
                    dve.wait_ge(s_samp_exp, 2)
                    out = full(dve, "zsum", 0)[:, 0:NS * AH].rearrange("p (b h) -> p b h", b=NS)
                    free(dve.tensor_tensor(zrec[:, :, :], out, own_p[:, :, :], ALU.add), "zsum", 0)
                    evacuated(dve, "zsum", 0)
                    link(dve.reciprocal(zrec[:, :, :], zrec[:, :, :]))
                    dve.wait_ge(s_p_hi, 1)
                    dve.tensor_tensor(S_split[:, :, :, AH:2 * AH], S[:, :, :, :],
                                      S_split[:, :, :, 0:AH].bitcast(F32), ALU.subtract).then_inc(s_p_lo, 1)
                elif name == "pv":
                    b, = a
                    out = full(dve, "pv", b, 0)
                    dve.wait_ge(s_own_head, 1)
                    if b >= 2:
                        dve.wait_ge(s_pv_sum, b - 1)
                    free(dve.tensor_tensor(pv_masked[:, b % 2, :].rearrange("p (h d) -> p h d", h=AH),
                                           out[0:2 * AH, :].rearrange("p (h d) -> p h d", h=AH),
                                           own_head[:, :].unsqueeze(2).to_broadcast([2 * AH, AH, AD]), ALU.mult),
                         "pv", b, 0)
                elif name == "pv_end":
                    dve.wait_ge(s_pv_sum, NS)
                    dve.wait_ge(s_out_small, 16 * 5)
                    dve.tensor_copy(pv_tok[:, :], acc[0:NS, 0, :]).then_inc(s_pv_tok, 1)
                    out = full(dve, "pv_end", 0)
                    for odd in range(2):
                        rows64 = slice(64 * odd, 64 * odd + 64)

                        def by_tile(x):
                            return x[rows64, :, :].rearrange("p b (t o) -> p t b o", o=2)[:, :, :, odd]

                        tmp = own_prod[rows64, :, :]
                        link(dve.tensor_tensor(tmp, zT[rows64, VA:VA + 4, SEQ:TOK], by_tile(own_p), ALU.mult))
                        cache_part = out[rows64, 0:4 * NS].rearrange("p (t b) -> p t b", t=4)
                        ins = dve.tensor_tensor(tmp, tmp, cache_part, ALU.add)
                        if odd == 0:
                            link(ins)
                        else:
                            free(ins, "pv_end", 0)
                            evacuated(dve, "pv_end", 0)
                        dve.tensor_tensor(zT[rows64, QA:QA + 4, SEQ:TOK], tmp, by_tile(zrec), ALU.mult)\
                           .then_inc(s_pv_end_ok, 1)
                elif name == "att_d":
                    h, = a
                    for n in range(3):
                        evacuated(dve, "att_s", h, n)
                    link(dve.reciprocal(rrec[:, h % 2, :], rsum[:, h % 2, :]))
                    dve.tensor_tensor(p_norm[:, h % 2, :, :], ident[:, :].unsqueeze(1).to_broadcast([P, NT, P]),
                                      rrec[:, h % 2, :].unsqueeze(2).to_broadcast([P, NT, P]), ALU.mult)\
                       .then_inc(s_norm_ok, 1)
                elif name == "att_s":
                    h, = a
                    if h == 0:
                        dve.wait_ge(s_causal_ok, 1)
                    for n, parts in enumerate(((0, 1), (2,), (3,))):
                        out = full(dve, "att_s", h, n)
                        col = 0
                        for i in parts:
                            blk = out[:, col + i * P:col + (i + 1) * P]
                            ins = dve.tensor_tensor(blk, blk, causal[:, :], ALU.add)
                            col += (i + 1) * P
                        link(ins)
                        col = 0
                        for i in parts:
                            w = (i + 1) * P
                            ins = dve.reduce_max(rmax[:, h % 2, i:i + 1], out[:, col:col + w], AX.X)
                            col += w
                        link(ins)
                        dve.tensor_scalar(nmax[:, h % 2, parts[0]:parts[-1] + 1],
                                          rmax[:, h % 2, parts[0]:parts[-1] + 1], -ASCALE, None, ALU.mult)\
                           .then_inc(s_att_nmax, 1)
                elif name == "att_t":
                    h, = a
                    if h >= 1:
                        full(dve, "att_o", h - 1, 0)
                    out = full(dve, "att_t", h, 1)
                    free(dve.tensor_copy(pT[:, A_COL[1]:A_COL[2]], out[:, 0:A_COL[2] - A_COL[1]]), "att_t", h, 1)
                elif name == "om":
                    h, = a
                    dve.wait_ge(s_om_exp, h + 1)
                    dve.wait_ge(s_sm_end, 1)
                    evacuated(dve, "ml_t", h, 0)
                    link(dve.tensor_scalar(zT[:, OM + h, :], zT[:, OM + h, :], 1.0, None, ALU.add))
                    link(dve.reciprocal(zT[:, OM + h, :], zT[:, OM + h, :]))
                    dve.tensor_tensor(zT[:, QM + h, :], zT[:, QM + h, :], zT[:, OM + h, :], ALU.mult)\
                       .then_inc(s_gated, 1)
                elif name == "mix":
                    n, = a
                    j = MIX_ORDER[n]
                    dve.wait_ge(s_mix_hi, n + 1)
                    src = zT[:, QA + j, :] if j < 4 else zT[:, QM + j - 4, :]
                    dve.tensor_tensor(mix_parts[1][j], src, mix_hi[:, j, :].bitcast(F32), ALU.subtract)\
                       .then_inc(s_mix_lo, 1)
                elif name == "x2":
                    j, = a
                    dve.wait_ge(s_x2_hi, j + 1)
                    dve.scalar_tensor_tensor(out=act_lo[:, j, :], in0=xT[:, j, :], scalar=par[:, 8 + j:9 + j],
                                             in1=act_hi[:, j, :].bitcast(F32), op0=ALU.mult, op1=ALU.subtract)\
                       .then_inc(s_x2_lo, 1)
                    if j >= 1:
                        dve.wait_ge(s_x1_sq, j + 1)
                        if j >= 2:
                            dve.wait_ge(s_sq_added, j - 1)
                        so_far = x_sq[:, 0, :] if j == 1 else sq_sum[:, :]
                        dve.tensor_tensor(sq_sum[:, :], so_far, x_sq[:, j % 2, :], ALU.add).then_inc(s_sq_added, 1)

            def evac_copy(g):
                for half in range(2):
                    dve.wait_ge(s_half_done, 2 * g + half + 1)
                    dve.tensor_copy(zT[:, IN_ORDER[g], half * HALF:(half + 1) * HALF],
                                    acc[:, 2 * (g % 2) + half, 0:HALF]).then_inc(s_acc_evac, 1)

            def evac_add(g, side, j, half):
                dve.wait_ge(s_half_done, 2 * g + half + 1)
                x = xT[:, j, half * HALF:(half + 1) * HALF]
                dve.tensor_tensor(x, acc[:, 2 * side + half, 0:HALF], x, ALU.add).then_inc(s_acc_evac, 1)

            for g in range(N_IN):
                if IN_ORDER[g] == VA:
                    for b in range(4):
                        dve.wait_ge(C_out[b], 32)
                if IN_ORDER[g] == OM:
                    dve.wait_ge(s_k_out0, 32)
                    dve.wait_ge(s_k_out1, 32)
                n = g + AHEAD
                if n < DVE_LO:
                    if n == AHEAD:
                        dve.wait_ge(s_w_lo_ok, AHEAD)
                    weight_lo(dve, n, n % WSLOTS, n // 2 % 2)
                evac_copy(g)
                for name in TASKS[g]:
                    task(*name)
            for g in range(G_OUT, G_MLP):
                j = g - G_OUT
                evacuated(dve, "xt", j, 0)
                evacuated(dve, "xt_s", 0)
                for half in range(2):
                    evac_add(g, g % 2, j, half)
                for name in TASKS[g]:
                    task(*name)
            out = full(dve, "sumsq", 0)
            dve.tensor_scalar(rs[:, 0:NT], out[:, 0:NT], 1.0 / D, EPS, ALU.mult, ALU.add).then_inc(s_rs2_ms, 1)
            free(dve.tensor_scalar(rs[0:NS, NT:NT + 1], out[0:NS, NT:NT + 1], 1.0 / D, EPS, ALU.mult, ALU.add),
                 "sumsq", 0)
            free(dve.tensor_copy(rstd2[:, 0:SEQ], full(dve, "rstd2", 0)), "rstd2", 0)
            free(dve.tensor_copy(rstd2[:, SEQ:TOK], full(dve, "rstd2", 1)[:, 0:NS]), "rstd2", 1)
            evacuated(dve, "rstd2", 0)
            evacuated(dve, "rstd2", 1)

            with dve.Fori(0, QUARTERS) as i:
                for t in range(16):
                    g = G_MLP + 16 * i + t
                    for half in range(2):
                        cols = slice(half * HALF, (half + 1) * HALF)
                        if t < 8:
                            dve.wait_ge(s_half_done, 2 * g + half + 1)
                            if t >= 2:
                                dve.wait_ge(s_hs_hi, 8 * i + t - 1)
                            dve.scalar_tensor_tensor(out=relu[:, t % 2, cols], in0=acc[:, 2 * (t % 2) + half, 0:HALF],
                                                     scalar=0.0, in1=rstd2[:, cols], op0=ALU.max, op1=ALU.mult)\
                               .then_inc(s_acc_evac, 1)
                        else:
                            evac_add(g, t % 2, t - 8, half)

            dve.wait_ge(s_lnf_in, 16)
            for i in range(NT + 1):
                n = P if i < NT else NS
                dve.wait_ge(s_y_sq, 2 * i + 2)
                link(dve.tensor_tensor(y_ms[0:n, i:i + 1], y_ss[0:n, i, 0:1], y_ss[0:n, i, 1:2], ALU.add))
                dve.tensor_scalar(y_ms[0:n, i:i + 1], y_ms[0:n, i:i + 1], 1.0 / D, EPS, ALU.mult, ALU.add)\
                   .then_inc(s_y_ms_ok, 1)
                dve.wait_ge(s_y_pow, i + 1)
                if i >= 2:
                    dve.wait_ge(st_y[i % 2], 16 * (i // 2))
                for part in range(2):
                    cols = slice(part * 512, part * 512 + 512)
                    out = full(dve, "yt", i, part)
                    free(dve.scalar_tensor_tensor(out=y_out[0:n, i % 2, cols], in0=out[0:n, :],
                                                  scalar=y_ms[0:n, i:i + 1], in1=lnf_b[0:n, cols], op0=ALU.mult,
                                                  op1=ALU.mult), "yt", i, part)


_INS = ["x_prompt", "x_sample", "cache_k", "cache_v", "page_table", "state_C", "state_n", "state_m", "ln1_w",
        "w_in", "b_gates", "mlstm_norm_w", "w_out", "ln2_w", "w_up", "w_down", "lnf_w"]
_OUTS = [(1, SEQ, D), (NS, 1, D), (1, 1, SEQ, AH, AD), (1, 1, SEQ, AH, AD), (1, 1, MH, MD, MD), (1, 1, MH, MD),
         (1, 1, MH), (1, NS, 1, AH, AD), (1, NS, 1, AH, AD), (1, NS, MH, MD, MD), (1, NS, MH, MD), (1, NS, MH)]


def kernel(**inputs):
    import numpy as _np
    import concourse.bacc as _bacc
    from concourse import mybir as _mybir
    from concourse.bass_utils import run_bass_kernel_spmd as _run

    nc = _bacc.Bacc("TRN2", target_bir_lowering=False, num_devices=1)
    arrays, args = {}, []
    for name in _INS:
        a = _np.ascontiguousarray(inputs[name])
        arrays[f"in_{name}_dram"] = a
        args.append(nc.dram_tensor(f"in_{name}_dram", a.shape, _mybir.dt.from_np(a.dtype), kind="ExternalInput").ap())
    for i, shape in enumerate(_OUTS):
        args.append(nc.dram_tensor(f"out_{i}_dram", shape, _mybir.dt.float32, kind="ExternalOutput").ap())
    build(nc, *args)
    r = _run(nc, [arrays], core_ids=[0])
    return tuple(r.results[0][f"out_{i}_dram"] for i in range(len(_OUTS)))
```

```python
from contextlib import ExitStack

import concourse.bass as bass
from concourse import mybir

ALU = mybir.AluOpType
ACT = mybir.ActivationFunctionType
AX = mybir.AxisListType
F32 = mybir.dt.float32
F32R = mybir.dt.float32r
I32 = mybir.dt.int32

P = 128
D = 1024
KT = D // P
SEQ = 512
NT = SEQ // P
NS = 8
TOK = SEQ + NS
HALF = TOK // 2
AH, AD = 8, 64
MH, MD = 4, 128
PAGES, PAGE = 8, 128
AW = AH * AD
EPS = 1e-6
MASKED = -1e30
ASCALE = AD ** -0.5
MSCALE = MD ** -0.5

QA, KA, VA, QM, KM, VM, OM = (4 * i for i in range(7))
GATE_COL = 28 * P
IN_ORDER = [c + t for c in (QA, QM, KM, VM, KA, VA, OM) for t in range(4)]
N_IN, N_OUT = 28, 8
G_OUT = N_IN
G_MLP = N_IN + N_OUT
QUARTERS = 4
N_MAIN = G_MLP + 16 * QUARTERS
WSLOTS = 4
AHEAD = 3
DVE_LO = 28
MIX_ORDER = (4, 5, 6, 7, 0, 1, 2, 3)

LOW = 32

BASE = 16512


def z_ready(c):
    return 2 * (IN_ORDER.index(c) + 1)


def plan():
    tasks = [[] for _ in range(G_MLP)]

    def at(g, *names):
        tasks[g] += names

    at(1, ("gates",))
    at(2, ("rows",))
    at(3, ("rows_m",))
    at(4, ("qs_tok",), ("rows_end",))
    at(5, ("qb", 0), ("qb", 1), ("gcols",))

    def scores(g, n=2):
        for _ in range(n):
            at(g, ("score", *divmod(chunks[0], 4)))
            chunks[0] += 1

    chunks = [0]
    for g in range(6, 17):
        if g in (8, 10, 12, 14, 16):
            at(g, ("qb", (g - 4) // 2))
        scores(g, 2 if g < 16 else 0)
    at(16, ("sm_prep",), ("vs_tok",), ("tok", VM, 0), ("tok", VM, 1), ("sm_c", 0), ("sm_c", 1))
    scores(16)
    at(17, ("sm_r", 0), ("sm_r", 1), ("sm_c", 2), ("tok", VM, 2), ("tok", VM, 3), ("sm_c", 3), ("sm_r", 2),
       ("tok", KM, 0), ("tok", KM, 1))
    scores(17)
    at(18, ("qb", 7), ("sm_r", 3), ("sm_c", 4), ("tok", KM, 2))
    scores(18, 1)
    at(18, ("ml_m", 0), ("tok", KM, 3), ("sm_c", 5), ("sm_r", 4), ("ml_k", 0))
    scores(18, 1)
    at(18, ("ml_m", 1))
    at(19, ("ml_k", 1), ("sm_r", 5), ("sm_c", 6))
    scores(19, 1)
    at(19, ("sm_c", 7), ("ml_o", 0), ("sm_r", 6))
    scores(19, 1)
    at(19, ("ml_m", 2))
    at(20, ("ml_k", 2), ("ml_n", 0), ("sm_r", 7))
    scores(20, 1)
    at(20, ("ml_o", 1), ("ml_t", 0))
    scores(20, 1)
    at(20, ("ml_m", 3))
    at(21, ("ml_k", 3), ("ml_n", 1), ("tok", KA, 0))
    scores(21, 1)
    at(21, ("ml_o", 2), ("tok", KA, 1), ("ml_t", 1))
    scores(21, 1)
    at(21, ("sm_den",))
    at(22, ("ml_n", 2), ("ml_o", 3), ("tok", KA, 2), ("tok", KA, 3), ("ml_t", 2), ("ml_kw", 0))
    at(23, ("ml_mc", 0), ("ml_n", 3), ("gate",), ("ml_kw", 1), ("sm_out",))
    at(24, ("ml_mc", 1), ("ml_t", 3), ("ks_tok",), ("tok", VA, 0), ("tok", VA, 1), ("tok", VA, 2), ("mx_t",),
       ("ml_kw", 2), ("tok", VA, 3), ("own",), ("sm_end",), ("om", 0, 0))
    at(25, ("ml_mc", 2), ("mx_b",), ("att_s", 0), ("va_s",), ("ml_kw", 3))
    at(26, ("ml_mc", 3), ("p_sum",), ("att_s", 1), ("zsum",), ("att_d", 0), ("om", 0, 1))
    at(27, ("v_hi", 0, 0), ("v_hi", 0, 1), ("pv_zero",))
    for h in range(AH):
        if h > 0:
            at(27, ("att_d", h))
            if h + 1 < AH:
                at(27, ("att_s", h + 1))
        at(27, ("v_lo", h), ("att_t", h))
        if h < 6:
            at(27, ("om", (h + 2) // 2, (h + 2) % 2))
        if h == AH - 1:
            at(27, ("mix", 0), ("mix", 1))
        at(27, ("pv", h))
        if h == 0:
            at(27, ("weights", N_IN - 1))
        if h + 1 < NS:
            at(27, ("v_hi", h + 1, 0))
        at(27, ("att_o", h))
        if h + 1 < NS:
            at(27, ("v_hi", h + 1, 1))
        if h % 4 == 3:
            at(27, ("pv_sum", h // 4))
    at(27, ("pv_tok",), ("mix", 2), ("mix", 3), ("pv_end",))
    for n in range(4, KT):
        at(27, ("mix", n))
    for j in range(KT):
        at(G_OUT + j // 2, ("xt", j))
    at(G_OUT, ("xt_s",))
    for j in range(KT):
        at(min(G_OUT + j + 1, G_MLP - 1), ("x2", j))

    scratch = {
        "gates": 2, "gcols": 1, "qs_tok": 1, "qb": 1, "vs_tok": 1, "tok": 1, "sm_prep": 2, "sm_c": 1,
        "sm_r": 1, "ml_m": 1, "ml_k": 3,
        "ml_o": 2, "ml_t": 1, "ml_mc": 1, "sm_den": 1, "sm_out": 2, "ks_tok": 1, "gate": 1, "mx_t": 1,
        "own": 1, "va_s": 1, "mx_b": 1, "zsum": 1, "att_s": 3, "att_t": 2, "att_o": 1,
        "pv_end": 1, "xt": 1, "xt_s": 1,
    }
    jobs = {}

    def job(*key):
        jobs[key] = len(jobs)

    job("param", 0)
    for j in range(4, KT):
        job("xn", j)
    job("par2", 0)
    job("rstd1", 0)
    job("rstd1", 1)
    for names in tasks:
        for name in names:
            n = scratch.get(name[0], 0)
            for i in range(n):
                job(*name, i)
    job("sumsq", 0)
    job("rstd2", 0)
    job("rstd2", 1)
    for part in range(2):
        for i in range(NT + 1):
            job("yt", i, part)
    return tasks, jobs


TASKS, JOBS = plan()


def build(nc, x_prompt, x_sample, cache_k, cache_v, page_table, state_C, state_n, state_m, ln1_w, w_in,
          b_gates, mlstm_norm_w, w_out, ln2_w, w_up, w_down, lnf_w, y_prompt, y_sample, k_prompt, v_prompt,
          C_prompt, n_prompt, m_prompt, k_sample, v_sample, C_sample, n_sample, m_sample):
    n_phys = cache_k.shape[1]
    ctx = ExitStack()
    with ctx:
        ctx.enter_context(nc.allow_non_contiguous_dma(reason="a few hundred elements of gates and states"))
        end = [BASE]

        def place(name, shape, dt=F32, at=None):
            size = 4
            for n in shape[1:]:
                size *= n
            off = end[0] if at is None else at
            t = nc.alloc_sbuf_tensor_at(name, shape, dt, offset=off)
            if at is None:
                end[0] = off + (size + 31) // 32 * 32
            return t, off

        raw, _ = place("raw", [P, 2, KT, 2 * P])
        w_hi, _ = place("w_hi", [P, WSLOTS, KT, P], F32R)
        w_lo, _ = place("w_lo", [P, WSLOTS, KT, P], F32R)
        act_hi, act_hi_at = place("act_hi", [P, KT, TOK], F32R)
        act_lo, act_lo_at = place("act_lo", [P, KT, TOK], F32R)
        v_hi, _ = place("v_hi", [P, PAGES, TOK], F32R, at=act_hi_at)
        v_lo, _ = place("v_lo", [P, PAGES, TOK], F32R, at=act_lo_at)
        y_out, _ = place("y_out", [P, NT + 1, D], at=act_hi_at)
        y_junk, _ = place("y_junk", [P, 512], at=act_hi_at + 4 * (NT + 1) * D)
        zT, z_at = place("zT", [P, N_IN, TOK])
        h_hi, _ = place("h_hi", [P, KT, TOK], F32R, at=z_at)
        h_lo, _ = place("h_lo", [P, KT, TOK], F32R, at=z_at + 4 * KT * TOK)
        tail_at = z_at + 4 * 2 * KT * TOK
        relu, _ = place("relu", [P, 2, TOK], at=tail_at)
        relu2, _ = place("relu2", [P, 2, TOK], at=tail_at + 4 * 2 * TOK)
        rstd2, _ = place("rstd2", [P, TOK], at=tail_at + 4 * 4 * TOK)
        mix_hi, _ = place("mix_hi", [P, KT, TOK], F32R, at=z_at + 4 * KM * TOK)
        mix_lo_att, _ = place("mix_lo_att", [P, 4, TOK], F32R, at=z_at + 4 * OM * TOK)
        mix_lo_ml, _ = place("mix_lo_ml", [P, 4, TOK], F32R, at=z_at + 4 * KA * TOK)
        x_sq, _ = place("x_sq", [P, 2, TOK], at=z_at + 4 * VA * TOK)
        sq_sum, _ = place("sq_sum", [P, TOK], at=z_at + 4 * (VA + 2) * TOK)
        km_tok, _ = place("km_tok", [P, NT, AW], at=z_at + 4 * VM * TOK)
        om_at = z_at + 4 * OM * TOK
        qs_split, _ = place("qs_split", [LOW + NS, AW], F32R, at=om_at)
        vs_split, _ = place("vs_split", [LOW + NS, AW], F32R, at=om_at + 4 * AW)
        k_stage, _ = place("k_stage", [P, 2, AW], at=om_at + 8 * AW)
        xT, x_at = place("xT", [P, KT, TOK])
        rows, _ = place("rows", [4, 6, TOK], at=x_at)
        att = 1280
        mA, _ = place("mA", [P, 2, att], at=x_at)
        m_h0, _ = place("m_h0", [P, NT, MD], at=x_at + 8 * att)
        m_kw, _ = place("m_kw", [P, NT, MD], at=x_at + 8 * att + 2048)
        sm_at = x_at + 8 * att + 4096
        sm_b, _ = place("sm_b", [P, MH, 3, NS], at=sm_at)
        sm_kw, _ = place("sm_kw", [P, MH, NS], at=sm_at + 384)
        sm_n, _ = place("sm_n", [P, NS, MH], at=sm_at + 512)
        sm_q, _ = place("sm_q", [P, NS, MH], at=sm_at + 640)
        sm_h, _ = place("sm_h", [P, NS, MH], at=sm_at + 768)
        sm_t, _ = place("sm_t", [P, NS, MH], at=sm_at + 896)
        n_rows, _ = place("n_rows", [NS * MH, MD], at=sm_at + 1024)
        n_new_rows, _ = place("n_new_rows", [NS * MH, MD], at=sm_at + 1536)
        pr, _ = place("pr", [P, 2, att], at=x_at)
        pT, _ = place("pT", [P, att], at=x_at + 8 * att)
        kv, kv_at = place("kv", [P, PAGES, AW])
        x_tok, _ = place("x_tok", [P, NT, D], at=kv_at)
        x_tok2, _ = place("x_tok2", [P, NT, D], at=kv_at)
        prod, prod_at = place("prod", [P, 2, 2 * AW])
        x_s, _ = place("x_s", [NS, D], at=prod_at)
        x_s2, _ = place("x_s2", [NS, D], at=prod_at)
        C_stage, _ = place("C_stage", [P, MH, MD], at=prod_at + 2048)
        S_split, _ = place("S_split", [P, NS, PAGES, 2 * AH], F32R, at=prod_at)
        junk, _ = place("junk", [P, D], at=x_at)
        lnf_b, _ = place("lnf_b", [P, D], at=prod_at + 4096)
        t_at = prod_at + 4096
        gate, _ = place("gate", [P, NS, 4, AH], at=t_at)
        gate_min, _ = place("gate_min", [P, NS, AH], at=t_at + 1024)
        taken, _ = place("taken", [P, NS, AH], at=t_at + 1280)
        page_max, _ = place("page_max", [P, NS, AH], at=t_at + 1536)
        own, _ = place("own", [P, NS, AH], at=t_at + 1792)
        smax, _ = place("smax", [P, NS, AH], at=t_at + 2048)
        own_p, _ = place("own_p", [P, NS, AH], at=t_at + 2304)
        zrec, _ = place("zrec", [P, NS, AH], at=t_at + 2560)
        own_prod, _ = place("own_prod", [P, 4, NS], at=t_at + 3072)
        mx_col, _ = place("mx_col", [NS * AH, 1], at=t_at + 3200)
        v_tok, v_at = place("v_tok", [P, NT, AW])
        m_h1, _ = place("m_h1", [P, NT, MD], at=v_at)
        m_hs = m_h0, m_h1
        vm_tok, vm_at = place("vm_tok", [P, NT, MH, MD + 1])
        wg_hi, _ = place("wg_hi", [P, KT, P], F32R, at=vm_at)
        wg_lo, _ = place("wg_lo", [P, KT, P], F32R, at=vm_at + 4 * D)
        p_norm, _ = place("p_norm", [P, 2, NT, P], at=vm_at)
        pv_masked, _ = place("pv_masked", [P, 2, AW], at=vm_at + 8 * AW)
        cs_at = z_at + 4 * VA * TOK
        Cs, _ = place("Cs", [P, 4, MH, MD], at=cs_at)
        par_rows, _ = place("par_rows", [KT + MH, P], at=cs_at)
        ln1_rows, _ = place("ln1_rows", [KT, P], at=cs_at + 2048)
        wg_raw, _ = place("wg_raw", [P, KT, 8], at=cs_at + 512)
        xn_s, _ = place("xn_s", [P, KT, NS], at=cs_at + 768)
        S, _ = place("S", [P, NS, PAGES, AH])
        Qb, qb_at = place("Qb", [P, 2, AW])
        pv_tok, _ = place("pv_tok", [NS, AW], at=qb_at)
        pick, _ = place("pick", [P, 12])
        own_head, _ = place("own_head", [2 * AH, AH])
        M_split, _ = place("M_split", [LOW + MH, SEQ], F32R)
        both, _ = place("both", [LOW + NS, NS], F32R)
        ident, _ = place("ident", [P, P])
        causal, _ = place("causal", [P, P])
        ones, _ = place("ones", [P, 1])
        even, _ = place("even", [P, 2])
        par, _ = place("par", [P, 20])
        ss, _ = place("ss", [P, 8])
        rs, _ = place("rs", [P, 8])
        power, _ = place("power", [P, 1])
        rstd1, _ = place("rstd1", [P, TOK])
        g_col, _ = place("g_col", [P, 2, NT, MH])
        MS, _ = place("MS", [P, MH])
        w_end, _ = place("w_end", [P, MH, NT])
        m_den, _ = place("m_den", [P, NT])
        m_ss, _ = place("m_ss", [P, NT])
        m_rs, _ = place("m_rs", [P, NT])
        m_s, _ = place("m_s", [4, NS])
        y_ss, _ = place("y_ss", [P, NT + 1, 2])
        y_ms, _ = place("y_ms", [P, NT + 1])
        nc_col, _ = place("nc_col", [P, MH])
        rmax, _ = place("rmax", [P, 2, NT])
        nmax, _ = place("nmax", [P, 2, NT])
        rsum, _ = place("rsum", [P, 2, NT])
        rrec, _ = place("rrec", [P, 2, NT])
        bias_i, _ = place("bias_i", [4, 1])
        bias_f, _ = place("bias_f", [4, 1])
        m0_row, _ = place("m0_row", [4, NS])
        s_rows, _ = place("s_rows", [4, 3, NS])
        pt, _ = place("pt", [1, NS * PAGES], I32)
        assert end[0] <= nc.sbuf_usable_end, (end[0], nc.sbuf_usable_end)

        acc = ctx.enter_context(nc.psum_tensor("acc", [P, 4, 512], F32))
        scr = ctx.enter_context(nc.psum_tensor("scr", [P, 4, 512], F32))

        def sem(name):
            return ctx.enter_context(nc.semaphore(name))

        s_x_in0 = sem("x_in0")
        s_x_in1 = sem("x_in1")
        s_x_in2 = sem("x_in2")
        s_x_in3 = sem("x_in3")
        s_x_in4 = sem("x_in4")
        s_ln1_in = sem("ln1_in")
        s_par_in = sem("par_in")
        s_par_ok = sem("par_ok")
        s_wg_in = sem("wg_in")
        s_small_in = sem("small_in")
        s_n_in = sem("n_in")
        s_pt_in = sem("pt_in")
        s_raw0 = sem("raw0")
        s_raw1 = sem("raw1")
        s_x2_in = sem("x2_in")
        s_x2s_in = sem("x2s_in")
        s_lnf_in = sem("lnf_in")
        s_C_in0 = sem("C_in0")
        s_C_in1 = sem("C_in1")
        s_C_in2 = sem("C_in2")
        s_C_in3 = sem("C_in3")
        s_C_out0 = sem("C_out0")
        s_C_out1 = sem("C_out1")
        s_C_out2 = sem("C_out2")
        s_C_out3 = sem("C_out3")
        s_k_out0 = sem("k_out0")
        s_k_out1 = sem("k_out1")
        s_ident_ok = sem("ident_ok")
        s_causal_ok = sem("causal_ok")
        s_wg_zero = sem("wg_zero")
        s_wg_hi_ok = sem("wg_hi_ok")
        s_wg_lo_ok = sem("wg_lo_ok")
        s_x_sq_ok = sem("x_sq_ok")
        s_x_ms_ok = sem("x_ms_ok")
        s_x_rs_ok = sem("x_rs_ok")
        s_x_acc = sem("x_acc")
        s_x_lo = sem("x_lo")
        s_xhi_ok = sem("xhi_ok")
        s_xs_ok = sem("xs_ok")
        s_w_hi_ok = sem("w_hi_ok")
        s_w_lo_ok = sem("w_lo_ok")
        s_half_done = sem("half_done")
        s_acc_evac = sem("acc_evac")
        s_scr_full = sem("scr_full")
        s_f_abs = sem("f_abs")
        s_zero_row = sem("zero_row")
        s_sel_ok = sem("sel_ok")
        s_M_split = sem("M_split")
        s_f_log = sem("f_log")
        s_m_ok = sem("m_ok")
        s_srow_ok = sem("srow_ok")
        s_rows_ok = sem("rows_ok")
        s_srow_exp = sem("srow_exp")
        s_vm_ones = sem("vm_ones")
        s_kmul_ok = sem("kmul_ok")
        s_kred_ok = sem("kred_ok")
        s_samp_dve = sem("samp_dve")
        s_samp_sub = sem("samp_sub")
        s_samp_exp = sem("samp_exp")
        s_pv_end_ok = sem("pv_end_ok")
        s_sm_b_ok = sem("sm_b_ok")
        s_C_decayed = sem("C_decayed")
        s_sm_dve = sem("sm_dve")
        s_sm_pow = sem("sm_pow")
        s_sm_end = sem("sm_end")
        s_ml_tri = sem("ml_tri")
        s_ml_ms = sem("ml_ms")
        s_ml_pow = sem("ml_pow")
        s_ml_hr = sem("ml_hr")
        s_ml_wend = sem("ml_wend")
        s_ml_kw = sem("ml_kw")
        s_att_nmax = sem("att_nmax")
        s_norm_ok = sem("norm_ok")
        s_own_head = sem("own_head")
        s_qs_hi = sem("qs_hi")
        s_vs_hi = sem("vs_hi")
        s_pv_used = sem("pv_used")
        s_pv_masked = sem("pv_masked")
        s_pv_zero = sem("pv_zero")
        s_pick_ok = sem("pick_ok")
        s_att_t1 = sem("att_t1")
        s_att_t1_out = sem("att_t1_out")
        s_v_hi = sem("v_hi")
        s_v_lo_a = sem("v_lo_a")
        s_v_lo_b = sem("v_lo_b")
        s_p_hi = sem("p_hi")
        s_p_lo = sem("p_lo")
        s_pv_sum = sem("pv_sum")
        s_pv_tok = sem("pv_tok")
        s_om_exp = sem("om_exp")
        s_gated = sem("gated")
        s_mix_hi = sem("mix_hi")
        s_mix_lo = sem("mix_lo")
        s_x1_sq = sem("x1_sq")
        s_sq_added = sem("sq_added")
        s_rs2_ms = sem("rs2_ms")
        s_rs2_pow = sem("rs2_pow")
        s_x2_hi = sem("x2_hi")
        s_x2_lo = sem("x2_lo")
        s_hs_hi = sem("hs_hi")
        s_hs_lo = sem("hs_lo")
        s_y_sq = sem("y_sq")
        s_y_ms_ok = sem("y_ms_ok")
        s_y_pow = sem("y_pow")
        s_out_v = sem("out_v")
        s_out_small = sem("out_small")
        s_out_C = sem("out_C")
        s_y_half = sem("y_half")
        s_y_stored = sem("y_stored")
        s_dve_chain = sem("dve_chain")
        s_act_chain = sem("act_chain")
        s_pool_chain = sem("pool_chain")
        scr_free = [sem(f"scr_free{i}") for i in range(4)]
        kv_in = [sem(f"kv_in{i}") for i in range(PAGES)]
        raw_in = [s_raw0, s_raw1]
        x_in = [s_x_in0, s_x_in1, s_x_in2, s_x_in3, s_x_in4]
        C_in = [s_C_in0, s_C_in1, s_C_in2, s_C_in3]
        C_out = [s_C_out0, s_C_out1, s_C_out2, s_C_out3]
        k_out = [s_k_out0, s_k_out1]

        def bank(*key):
            return scr[:, JOBS[key] % 4, :]

        def open_job(pe, *key):
            n = JOBS[key]
            if n >= 4:
                pe.wait_ge(scr_free[n % 4], n // 4)
            return scr[:, n % 4, :]

        def full(eng, *key):
            eng.wait_ge(s_scr_full, JOBS[key] + 1)
            return bank(*key)

        def free(ins, *key):
            ins.then_inc(scr_free[JOBS[key] % 4], 1)

        def evacuated(eng, *key):
            n = JOBS[key]
            eng.wait_ge(scr_free[n % 4], n // 4 + 1)

        def value_split(eng, b, j):
            n = j // 2
            if n < 2:
                eng.wait_ge(s_v_lo_a, 2 * b + n + 1)
            else:
                eng.wait_ge(s_v_lo_b, 2 * b + n - 1)

        block = ctx.enter_context(nc.Block())

        A_COL = [0, 512, 896, 1152]
        P_COL = [0, 128, 384, 768]

        def tiles(t):
            return [t[:, k, :] for k in range(t.shape[1])]

        Y_FIRST = {12: (0, 1), 13: (2, 3), 14: (NT,)}
        x_parts = tiles(act_hi), tiles(act_lo)
        h_parts = tiles(h_hi), tiles(h_lo)
        mix_parts = tiles(mix_hi), tiles(mix_lo_att) + tiles(mix_lo_ml)

        @block.sync
        def _(sp):
            for i in range(NT):
                sp.dma_start(x_tok[:, i, :], x_prompt[0, i * P:(i + 1) * P, :]).then_inc(x_in[i], 16)

            def unit(r, src, first=True):
                if r >= 2:
                    sp.wait_ge(s_w_lo_ok, 2 * (r - 1))
                sp.dma_start(raw[:, r % 2, :, :], src.rearrange("(k p) n -> p k n", p=P))\
                  .then_inc(raw_in[r % 2], 16)

            def in_unit(r):
                c = IN_ORDER[2 * r] * P
                unit(r, w_in[0, :, c:c + 2 * P])

            def pages(cache, b, step):
                for j in range(PAGES):
                    page = sp.value_load(pt[0:1, b * PAGES + j:b * PAGES + j + 1], min_val=0, max_val=n_phys - 1)
                    if 1 <= step <= NS:
                        sp.wait_ge(s_kmul_ok, 4 * (step - 1) + j // 2 + 1)
                    elif step > NS:
                        value_split(sp, b - 1, j)
                    src = cache[0, bass.ds(page, 1), :, :, :].rearrange("o p h d -> p (o h d)")
                    sp.dma_start(kv[:, j, :], src).then_inc(kv_in[j], 16)

            in_unit(0)
            sp.dma_start(wg_raw[:, :, :], w_in[0, :, GATE_COL:GATE_COL + 8].rearrange("(k p) n -> p k n", p=P))\
              .then_inc(s_wg_in, 16)
            sp.dma_start(pt[:, :], page_table.rearrange("(o b) n -> o (b n)", o=1)).then_inc(s_pt_in, 16)
            in_unit(1)
            sp.dma_start(bias_i[:, :], b_gates[0:1, 0:4].rearrange("o n -> n o")).then_inc(s_small_in, 16)
            sp.dma_start(bias_f[:, :], b_gates[0:1, 4:8].rearrange("o n -> n o")).then_inc(s_small_in, 16)
            sp.dma_start(m0_row[:, :], state_m[0].rearrange("b h -> h b")).then_inc(s_small_in, 16)
            sp.wait_ge(s_pt_in, 16)
            full(sp, "xn", KT - 1)
            sp.wait_ge(s_x_sq_ok, NT + 1)
            pages(cache_k, 0, 0)
            for r in range(2, 14):
                in_unit(r)
                if 1 <= r - 5 < NS:
                    pages(cache_k, r - 5, r - 5)
                elif r - 5 == NS:
                    pages(cache_v, 0, NS)
            unit(14, w_out[0, :, 0:2 * P])
            unit(15, w_out[0, :, 2 * P:4 * P])
            for b in range(1, NS):
                pages(cache_v, b, NS + b)
            for i in range(NT):
                value_split(sp, NS - 1, 2 * i)
                sp.dma_start(x_tok2[:, i, :], x_prompt[0, i * P:(i + 1) * P, :]).then_inc(s_x2_in, 16)
            sp.wait_ge(s_pv_used, 4 * NS)
            sp.dma_start(x_s2[:, :], x_sample[:, 0, :]).then_inc(s_x2s_in, 16)
            sp.wait_ge(s_pv_end_ok, 2)
            sp.dma_start(lnf_b[:, :], lnf_w.rearrange("(o n) -> o n", o=1).broadcast_to([P, D])
                         ).then_inc(s_lnf_in, 16)
            for r in range(16, 18):
                unit(r, w_out[0, :, (r - 14) * 2 * P:(r - 13) * 2 * P])

            def mlp(i):
                for u in range(8):
                    r = 18 + 8 * i + u
                    sp.wait_ge(s_w_lo_ok, 2 * (r - 1))
                    if u < 4:
                        src = w_up[0, :, bass.ds(i * D + u * 2 * P, 2 * P)]
                    else:
                        src = w_down[0, bass.ds(i * D, D), (u - 4) * 2 * P:(u - 3) * 2 * P]
                    sp.dma_start(raw[:, u % 2, :, :], src.rearrange("(k p) n -> p k n", p=P))\
                      .then_inc(raw_in[u % 2], 16)

            with sp.Fori(0, QUARTERS) as i:
                mlp(i)
            for i in range(NT + 1):
                sp.wait_ge(s_y_half, i + 1)
                evacuated(sp, "yt", i, 1)
                if i < NT:
                    sp.dma_start(y_prompt[0, i * P:(i + 1) * P, :], y_out[:, i, :]).then_inc(s_y_stored, 16)
                else:
                    sp.dma_start(y_sample[:, 0, :], y_out[0:NS, i, :]).then_inc(s_y_stored, 16)
            sp.wait_ge(s_y_stored, 16 * (NT + 1))

        @block.tensor
        def _(pe):
            def main(g, slot, side, parts, k_ready=None, order=range(KT), between=None, first_half=None):
                hi, lo = parts
                pe.wait_ge(s_w_lo_ok, g + 1)

                def three(half, n, k):
                    cols = slice(half * HALF, (half + 1) * HALF)
                    out = acc[:, 2 * side + half, 0:HALF]
                    pe.matmul(out, w_hi[:, slot, k, :], hi[k][:, cols], start=(n == 0), stop=False)
                    pe.matmul(out, w_hi[:, slot, k, :], lo[k][:, cols], start=False, stop=False)
                    mm = pe.matmul(out, w_lo[:, slot, k, :], hi[k][:, cols], start=False, stop=(n == KT - 1))
                    if n == KT - 1:
                        mm.then_inc(s_half_done, 1)

                def bank_free(half):
                    if not isinstance(g, int) or g >= 2:
                        pe.wait_ge(s_acc_evac, 2 * (g - 2) + half + 1)

                if k_ready is not None:
                    bank_free(1)
                    for n, k in enumerate(order):
                        k_ready(n)
                        three(0, n, k)
                        three(1, n, k)
                    return
                for half in range(2):
                    bank_free(half)
                    for n, k in enumerate(order):
                        if half == 0 and first_half is not None:
                            first_half(n)
                        three(half, n, k)
                    if half == 0 and between is not None:
                        between()

            def done(mm):
                mm.then_inc(s_scr_full, 1)

            def to_tok(key, tiles, cols, n):
                out = open_job(pe, *key)
                for t in range(4):
                    mm = pe.transpose(out[0:n, t * P:(t + 1) * P], zT[:, tiles + t, cols], ident[:, :])
                done(mm)

            def every(col, n=P):
                return col.to_broadcast([n, P])

            pe.wait_ge(s_ident_ok, 3)
            for i in range(NT):
                pe.wait_ge(x_in[i], 16)
                if i == 2:
                    out = open_job(pe, "param", 0)
                    pe.wait_ge(s_ln1_in, 16)
                    pe.transpose(out[:, 0:KT], ln1_rows[:, :], ident[0:KT, 0:KT])
                    pe.wait_ge(x_in[NT], 16)
                    for j in range(KT):
                        mm = pe.transpose(out[:, 32 + j * NS:32 + (j + 1) * NS], x_s[:, j * P:(j + 1) * P],
                                          ident[0:NS, 0:NS])
                    done(mm)
                for j in range(KT):
                    if j == 7 and i < 2:
                        continue
                    out = acc[:, j, :] if j < 4 else bank("xn", j)
                    if j == 7 and i == 2:
                        open_job(pe, "xn", j)
                    for n in range(3) if j == 7 and i == 2 else (i,):
                        mm = pe.transpose(out[:, n * P:(n + 1) * P], x_tok[:, n, j * P:(j + 1) * P], ident[:, :])
                    if i == NT - 1 and j < 4:
                        mm.then_inc(s_x_acc, 1)
                    elif i == NT - 1:
                        done(mm)
            def task(name, *a):
                if name == "gates":
                    pe.wait_ge(s_wg_lo_ok, 2)
                    for half in range(2):
                        cols = slice(half * HALF, (half + 1) * HALF)
                        out = open_job(pe, "gates", half)[:, 0:HALF]
                        for k in range(KT):
                            pe.matmul(out, wg_hi[:, k, :], act_hi[:, k, cols], start=(k == 0), stop=False)
                            pe.matmul(out, wg_hi[:, k, :], act_lo[:, k, cols], start=False, stop=False)
                            mm = pe.matmul(out, wg_lo[:, k, :], act_hi[:, k, cols], start=False, stop=(k == KT - 1))
                        done(mm)
                elif name == "gcols":
                    pe.wait_ge(s_rows_ok, 1)
                    out = open_job(pe, "gcols", 0)
                    for r, row in enumerate((3, 5)):
                        for i in range(NT):
                            mm = pe.transpose(out[:, (r * NT + i) * MH:(r * NT + i + 1) * MH],
                                              rows[:, row, i * P:(i + 1) * P], ident[0:4, 0:4])
                    done(mm)
                elif name == "qs_tok":
                    pe.wait_ge(s_acc_evac, z_ready(QA + 3))
                    to_tok(("qs_tok", 0), QA, slice(SEQ, TOK), NS)
                elif name == "vs_tok":
                    pe.wait_ge(s_acc_evac, z_ready(VM + 3))
                    to_tok(("vs_tok", 0), VM, slice(SEQ, TOK), NS)
                elif name == "ks_tok":
                    to_tok(("ks_tok", 0), KA, slice(SEQ, TOK), NS)
                elif name == "va_s":
                    to_tok(("va_s", 0), VA, slice(SEQ, TOK), NS)
                elif name == "tok":
                    group, i = a
                    pe.wait_ge(s_acc_evac, z_ready(group + 3))
                    to_tok(("tok", group, i, 0), group, slice(i * P, (i + 1) * P), P)
                elif name == "qb":
                    b, = a
                    evacuated(pe, "qs_tok", 0)
                    pe.wait_ge(s_sel_ok, 4)
                    out = open_job(pe, "qb", b, 0)
                    done(pe.matmul(out, every(both[:, b:b + 1], LOW + NS), qs_split[:, :], start=True, stop=True))
                elif name == "sm_prep":
                    out = open_job(pe, "sm_prep", 0)
                    for h in range(MH):
                        mm = pe.matmul(out[:, h * 3 * NS:(h + 1) * 3 * NS], every(ident[0:4, h:h + 1], 4),
                                       s_rows[:, :, :].rearrange("p a b -> p (a b)"), start=True, stop=True)
                    done(mm)
                    pe.wait_ge(s_n_in, 16)
                    out = open_job(pe, "sm_prep", 1)
                    done(pe.transpose(out[:, 0:NS * MH], n_rows[:, :], ident[0:NS * MH, 0:NS * MH]))
                elif name == "sm_c":
                    b, = a
                    evacuated(pe, "vs_tok", 0)
                    out = open_job(pe, "sm_c", b, 0)
                    done(pe.matmul(out, every(both[:, b:b + 1], LOW + NS), vs_split[:, :], start=True, stop=True))
                elif name == "sm_r":
                    b, = a
                    evacuated(pe, "sm_c", b, 0)
                    out = open_job(pe, "sm_r", b, 0)
                    for h in range(MH):
                        mm = pe.matmul(out[:, h:h + 1], Cs[:, b % 4, h, :], zT[:, QM + h, SEQ + b:SEQ + b + 1],
                                       start=True, stop=True)
                    done(mm)
                elif name == "sm_den":
                    pe.wait_ge(s_sm_dve, 1)
                    out = open_job(pe, "sm_den", 0)
                    done(pe.matmul(out[:, 0:NS * MH], every(ones[:, :]), sm_q[:, :, :].rearrange("p a b -> p (a b)"),
                                   start=True, stop=True))
                elif name == "sm_out":
                    pe.wait_ge(s_sm_dve, 2)
                    out = open_job(pe, "sm_out", 0)
                    done(pe.matmul(out[:, 0:NS * MH], every(ones[:, :]), sm_t[:, :, :].rearrange("p a b -> p (a b)"),
                                   start=True, stop=True))
                    out = open_job(pe, "sm_out", 1)
                    done(pe.transpose(out[0:NS * MH, 0:P], sm_n[:, :, :].rearrange("p a b -> p (a b)"), ident[:, :]))
                elif name == "ml_m":
                    h, = a
                    out = open_job(pe, "ml_m", h, 0)
                    pe.wait_ge(s_M_split, 2)
                    done(pe.matmul(out, every(both[0:LOW + MH, h:h + 1], LOW + MH), M_split[:, :], start=True,
                                   stop=True))
                elif name == "ml_k":
                    h, = a
                    for n, parts in enumerate(((0,), (1,), (2, 3))):
                        out = open_job(pe, "ml_k", h, n)
                        col = 0
                        for j in parts:
                            w = SEQ - j * P
                            mm = pe.matmul(out[:, col:col + w], zT[:, KM + h, j * P:(j + 1) * P],
                                           zT[:, QM + h, j * P:SEQ], start=True, stop=True)
                            col += w
                        done(mm)
                elif name == "ml_o":
                    h, = a
                    if h == 0:
                        for i in range(NT):
                            evacuated(pe, "tok", VM, i, 0)
                    for n in range(3):
                        evacuated(pe, "ml_k", h, n)
                    for half in range(2):
                        out = open_job(pe, "ml_o", h, half)
                        for n, i in enumerate((2 * half, 2 * half + 1)):
                            for j in range(i + 1):
                                mm = pe.matmul(out[:, n * (MD + 1):(n + 1) * (MD + 1)],
                                               mA[:, h % 2, A_COL[j] + (i - j) * P:A_COL[j] + (i - j + 1) * P],
                                               vm_tok[:, j, h, :], start=(j == 0), stop=(j == i))
                        done(mm)
                elif name == "ml_t":
                    h, = a
                    pe.wait_ge(s_ml_hr, h + 1)
                    out = open_job(pe, "ml_t", h, 0)
                    for i in range(NT):
                        mm = pe.transpose(out[:, i * P:(i + 1) * P], m_hs[h % 2][:, i, :], ident[:, :])
                    done(mm)
                elif name == "ml_mc":
                    h, = a
                    pe.wait_ge(s_ml_kw, h + 1)
                    out = open_job(pe, "ml_mc", h, 0)
                    for j in range(NT):
                        mm = pe.matmul(out[:, 0:MD + 1], m_kw[:, j, :], vm_tok[:, j, h, :],
                                       start=(j == 0), stop=(j == NT - 1))
                    done(mm)
                elif name == "gate":
                    pe.wait_ge(s_kred_ok, 4 * NS)
                    out = open_job(pe, "gate", 0)
                    done(pe.matmul(out, every(ones[:, :]), S[:, :, :, :].rearrange("p b g h -> p (b g h)"),
                                   start=True, stop=True))
                elif name == "mx_t":
                    pe.wait_ge(s_samp_dve, 1)
                    out = open_job(pe, "mx_t", 0)
                    done(pe.transpose(out[0:NS * AH, 0:P], page_max[:, :, :].rearrange("p b h -> p (b h)"),
                                      ident[:, :]))
                elif name == "own":
                    pe.wait_ge(s_samp_dve, 2)
                    out = open_job(pe, "own", 0)
                    for odd in range(2):
                        mm = pe.matmul(out[:, odd * 32:(odd + 1) * 32], every(even[:, odd:odd + 1]),
                                       own_prod[:, :, :].rearrange("p t b -> p (t b)"), start=True, stop=True)
                    done(mm)
                elif name == "mx_b":
                    evacuated(pe, "mx_t", 0)
                    out = open_job(pe, "mx_b", 0)
                    done(pe.matmul(out[:, 0:NS * AH], every(mx_col[:, :], NS * AH), ident[0:NS * AH, 0:NS * AH],
                                   start=True, stop=True))
                elif name == "zsum":
                    pe.wait_ge(s_samp_dve, 3)
                    out = open_job(pe, "zsum", 0)
                    done(pe.matmul(out[:, 0:NS * AH], every(ones[:, :]),
                                   page_max[:, :, :].rearrange("p b h -> p (b h)"), start=True, stop=True))
                elif name == "pv":
                    b, = a
                    pe.wait_ge(s_p_lo, 1)
                    pe.wait_ge(s_acc_evac, 2 * (N_IN - 1 + b) if b < 2 else 2 * N_IN)
                    if b >= 2:
                        pe.wait_ge(s_pv_masked, b - 1)
                    out = acc[:, 1 + b % 2, :]
                    for j in range(PAGES):
                        value_split(pe, b, j)
                        pe.matmul(out[0:2 * AH, :], S_split[:, b, j, :], v_hi[:, j, 0:AW], start=(j == 0), stop=False)
                        mm = pe.matmul(out[0:2 * AH, :], S_split[:, b, j, :], v_lo[:, j, 0:AW], start=False,
                                       stop=(j == PAGES - 1))
                        if j % 2 == 1:
                            mm.then_inc(s_pv_used, 1)
                elif name == "pv_sum":
                    four, = a
                    pe.wait_ge(s_pv_masked, 4 * four + 4)
                    pe.wait_ge(s_pick_ok, 4)
                    if four == 0:
                        pe.wait_ge(s_acc_evac, 2 * (N_IN - 1))
                    pe.matmul(acc[0:NS, 0, :], pick[:, 4 - 4 * four:12 - 4 * four], pv_masked[:, four, :],
                              start=(four == 0), stop=(four == 1)).then_inc(s_pv_sum, 1)
                elif name == "pv_end":
                    pe.wait_ge(s_pv_tok, 1)
                    out = open_job(pe, "pv_end", 0)
                    for t in range(4):
                        mm = pe.transpose(out[:, t * NS:(t + 1) * NS], pv_tok[:, t * P:(t + 1) * P],
                                          ident[0:NS, 0:NS])
                    done(mm)
                elif name == "att_s":
                    h, = a
                    t, lo = h // 2, 64 * (h % 2)
                    for n, parts in enumerate(((0, 1), (2,), (3,))):
                        out = open_job(pe, "att_s", h, n)
                        col = 0
                        for i in parts:
                            w = (i + 1) * P
                            mm = pe.matmul(out[:, col:col + w], zT[lo:lo + 64, QA + t, i * P:(i + 1) * P],
                                           zT[lo:lo + 64, KA + t, 0:w], start=True, stop=True)
                            col += w
                        done(mm)
                elif name == "att_t":
                    h, = a
                    pe.wait_ge(s_norm_ok, h + 1)
                    for n in range(3):
                        evacuated(pe, "att_s", h, n)
                    for n, parts in enumerate(((0,), (1,), (2, 3))):
                        if n == 1:
                            pe.wait_ge(s_acc_evac, 2 * N_IN)
                            if h >= 1:
                                pe.wait_ge(s_att_t1_out, h)
                            out = acc[:, 3, :]
                        else:
                            out = open_job(pe, "att_t", h, n // 2)
                        for j in parts:
                            for i in range(j, NT):
                                col = A_COL[j] - A_COL[parts[0]] + (i - j) * P
                                mm = pe.matmul(out[:, col:col + P],
                                               pr[:, h % 2, P_COL[i] + j * P:P_COL[i] + (j + 1) * P],
                                               p_norm[:, h % 2, i, :], start=True, stop=True)
                        if n == 1:
                            mm.then_inc(s_att_t1, 1)
                        else:
                            done(mm)
                elif name == "att_o":
                    h, = a
                    if h == 0:
                        for i in range(NT):
                            evacuated(pe, "tok", VA, i, 0)
                    pair = slice(h // 2 * P, (h // 2 + 1) * P)
                    out = open_job(pe, "att_o", h, 0)
                    for j in range(NT):
                        if j == 1:
                            pe.wait_ge(s_att_t1_out, h + 1)
                        elif j < 3:
                            evacuated(pe, "att_t", h, j // 2)
                        mm = pe.matmul(out[:, j * P:SEQ], v_tok[:, j, pair], pT[:, A_COL[j]:A_COL[j] + SEQ - j * P],
                                       start=(j == 0), stop=(j == NT - 1))
                    done(mm)
                elif name == "xt":
                    j, = a
                    pe.wait_ge(s_x2_in, 16 * NT)
                    out = open_job(pe, "xt", j, 0)
                    for i in range(NT):
                        mm = pe.transpose(out[:, i * P:(i + 1) * P], x_tok2[:, i, j * P:(j + 1) * P], ident[:, :])
                    done(mm)
                elif name == "xt_s":
                    pe.wait_ge(s_x2s_in, 16)
                    out = open_job(pe, "xt_s", 0)
                    for j in range(KT):
                        mm = pe.transpose(out[:, j * NS:(j + 1) * NS], x_s2[:, j * P:(j + 1) * P],
                                          ident[0:NS, 0:NS])
                    done(mm)

            def sums_of_squares():
                pe.wait_ge(s_sq_added, KT - 1)
                out = open_job(pe, "sumsq", 0)
                for i in range(NT + 1):
                    n = P if i < NT else NS
                    mm = pe.matmul(out[0:n, i:i + 1], sq_sum[:, i * P:i * P + n], ones[:, :],
                                   start=True, stop=True)
                done(mm)

            def norm_to_rows(name="rstd2", made=s_rs2_pow):
                pe.wait_ge(made, 2)
                for half, parts in enumerate((range(NT), (NT,))):
                    out = open_job(pe, name, half)
                    for n, c in enumerate(parts):
                        m = P if c < NT else NS
                        mm = pe.matmul(out[:, n * P:n * P + m], every(rs[0:m, c:c + 1], m),
                                       ident[0:m, 0:m], start=True, stop=True)
                    done(mm)

            def x_split(k):
                if k < 4:
                    pe.wait_ge(s_x_lo, k + 1)
                else:
                    evacuated(pe, "xn", k)

            for g in range(N_IN):
                if g == 0:
                    main(g, g % WSLOTS, g % 2, x_parts, first_half=x_split,
                         between=lambda: pe.wait_ge(s_xs_ok, 1))
                    pe.wait_ge(s_par_in, 32)
                    out = open_job(pe, "par2", 0)
                    done(pe.transpose(out[:, 0:KT + MH], par_rows[:, :], ident[0:KT + MH, 0:KT + MH]))
                    norm_to_rows("rstd1", s_x_rs_ok)
                else:
                    main(g, g % WSLOTS, g % 2, x_parts)
                for name in TASKS[g]:
                    task(*name)
            for g in range(G_OUT, G_MLP):
                def mixed(k):
                    pe.wait_ge(s_mix_lo, k + 1)
                main(g, g % WSLOTS, g % 2, mix_parts, mixed if g == G_OUT else None, MIX_ORDER)
                for name in TASKS[g]:
                    task(*name)

            def y_to_tok(i, part):
                n = P if i < NT else NS
                out = open_job(pe, "yt", i, part)
                for j in range(4):
                    mm = pe.transpose(out[0:n, j * P:(j + 1) * P], xT[:, 4 * part + j, i * P:i * P + n], ident[:, :])
                done(mm)

            def quarter(i, first=False, last=False):
                for t in range(16):
                    g = G_MLP + 16 * i + t
                    if t < 8:
                        def normed(k):
                            pe.wait_ge(s_x2_lo, k + 1)
                        main(g, t % WSLOTS, t % 2, x_parts, normed if first and t == 0 else None,
                             between=norm_to_rows if first and t == 1 else None)
                        if first and t == 0:
                            sums_of_squares()
                    else:
                        def hidden(k):
                            pe.wait_ge(s_hs_lo, 8 * i + k + 1)
                        main(g, t % WSLOTS, t % 2, h_parts, hidden if t == 8 else None)
                        for n in Y_FIRST.get(t, ()) if last else ():
                            if n == 0:
                                pe.wait_ge(s_acc_evac, 2 * g)
                            y_to_tok(n, 0)

            quarter(0, first=True)
            with pe.Fori(1, QUARTERS - 1) as i:
                quarter(i)
            quarter(QUARTERS - 1, last=True)
            pe.wait_ge(s_acc_evac, 2 * N_MAIN)
            for i in range(NT + 1):
                y_to_tok(i, 1)

        def weight_hi(act, g, slot, r_slot, r_round):
            act.wait_ge(raw_in[r_slot], 16 * (r_round + 1))
            if not isinstance(g, int) or g >= WSLOTS:
                act.wait_ge(s_half_done, 2 * (g - WSLOTS + 1))
            side = slot % 2
            act.activation(w_hi[:, slot, :, :], raw[:, r_slot, :, side * P:(side + 1) * P], ACT.Copy)\
               .then_inc(s_w_hi_ok, 1)

        def weight_lo(eng, g, slot, r_slot):
            eng.wait_ge(s_w_hi_ok, g + 1)
            side = slot % 2
            eng.tensor_tensor(w_lo[:, slot, :, :], raw[:, r_slot, :, side * P:(side + 1) * P],
                               w_hi[:, slot, :, :].bitcast(F32), ALU.subtract).then_inc(s_w_lo_ok, 1)

        def value_lo(eng, b, n, made):
            eng.wait_ge(s_v_hi, 4 * b + n + 1)
            pair = slice(2 * n, 2 * n + 2)
            eng.tensor_tensor(v_lo[:, pair, 0:AW], kv[:, pair, :], v_hi[:, pair, 0:AW].bitcast(F32),
                              ALU.subtract).then_inc(made, 1)

        @block.scalar
        def _(act):
            chain = [0]

            def link(ins):
                chain[0] += 1
                ins.then_inc(s_act_chain, 1)
                act.wait_ge(s_act_chain, chain[0])

            def split(g):
                weight_hi(act, g, g % WSLOTS, g // 2 % 2, g // 4)

            act.dma_start(ln1_rows[:, :], ln1_w.rearrange("o (k p) -> (o k) p", p=P)).then_inc(s_ln1_in, 16)
            act.dma_start(x_s[:, :], x_sample[:, 0, :]).then_inc(x_in[NT], 16)
            act.dma_start(par_rows[0:8, :], ln2_w.rearrange("o (k p) -> (o k) p", p=P)).then_inc(s_par_in, 16)
            act.dma_start(par_rows[8:12, :], mlstm_norm_w.rearrange("o (k p) -> (o k) p", p=P))\
               .then_inc(s_par_in, 16)

            def square_sum(i):
                act.wait_ge(x_in[i], 16)
                n = P if i < NT else NS
                x = x_tok[:, i, :] if i < NT else x_s[:, :]
                done = (0, NT, 1, 2, NT - 1).index(i)
                if done >= 1:
                    act.wait_ge(s_x_sq_ok, done)
                act.activation(junk[0:n, :], x, ACT.Square, accum_out=ss[0:n, i:i + 1]).then_inc(s_x_sq_ok, 1)

            square_sum(0)
            square_sum(NT)
            out = full(act, "param", 0)
            act.activation(par[:, 0:KT], out[:, 0:KT], ACT.Copy).then_inc(s_par_ok, 1)
            free(act.activation(xn_s[:, :, :].rearrange("p j b -> p (j b)"), out[:, 32:32 + KT * NS], ACT.Copy),
                 "param", 0)
            square_sum(1)
            split(0)
            act.wait_ge(s_par_ok, 1)
            for j in range(KT):
                if j < 4:
                    act.wait_ge(s_x_acc, j + 1)
                    out = acc[:, j, :]
                else:
                    out = full(act, "xn", j)
                act.activation(act_hi[:, j, 0:SEQ], out, ACT.Copy, scale=par[:, j:j + 1]).then_inc(s_xhi_ok, 1)
                if j == 5:
                    split(1)
            square_sum(2)
            square_sum(NT - 1)
            split(2)
            free(act.activation(par[:, KT:20], full(act, "par2", 0)[:, 0:KT + MH], ACT.Copy), "par2", 0)
            act.dma_start(n_rows[:, :], state_n[0].rearrange("b h d -> (b h) d")).then_inc(s_n_in, 16)
            act.wait_ge(s_wg_in, 16)
            act.wait_ge(s_wg_zero, 2)
            act.activation(wg_hi[:, :, 0:4], wg_raw[:, :, 0:4], ACT.Copy).then_inc(s_wg_hi_ok, 1)
            act.activation(wg_hi[:, :, 32:36], wg_raw[:, :, 4:8], ACT.Copy).then_inc(s_wg_hi_ok, 1)

            def copy_out(dst, src, *key):
                free(act.activation(dst, src, ACT.Copy), *key)

            def task(name, *a):
                if name == "weights":
                    split(a[0] + AHEAD)
                elif name == "rows":
                    act.wait_ge(s_f_abs, 1)
                    link(act.activation(rows[:, 2, :], rows[:, 2, :], ACT.Exp, scale=-1.0))
                    act.activation(rows[:, 2, :], rows[:, 2, :], ACT.Ln, bias=1.0).then_inc(s_f_log, 1)
                elif name == "rows_end":
                    act.wait_ge(s_m_ok, 1)
                    act.activation(rows[:, 5, 0:SEQ], rows[:, 2, 0:SEQ], ACT.Exp, scale=-1.0)\
                       .then_inc(s_rows_ok, 1)
                    act.dma_start(m_prompt[0, 0:1, :].rearrange("o h -> h o"), rows[:, 2, SEQ - 1:SEQ])\
                       .then_inc(s_out_small, 16)
                    act.wait_ge(s_srow_ok, 1)
                    act.activation(s_rows[:, 0:2, :], s_rows[:, 0:2, :], ACT.Exp).then_inc(s_srow_exp, 1)
                    act.activation(s_rows[:, 2, :], m_s[:, :], ACT.Exp, scale=-1.0).then_inc(s_srow_exp, 1)
                    act.dma_start(m_sample[0].rearrange("b h -> h b"), m_s[:, :]).then_inc(s_out_small, 16)
                    for b in range(4):
                        load_state(b)
                elif name == "qs_tok":
                    act.wait_ge(s_sel_ok, 4)
                    act.activation(qs_split[0:NS, :], full(act, "qs_tok", 0)[0:NS, :], ACT.Copy)\
                       .then_inc(s_qs_hi, 1)
                elif name == "vs_tok":
                    act.activation(vs_split[0:NS, :], full(act, "vs_tok", 0)[0:NS, :], ACT.Copy)\
                       .then_inc(s_vs_hi, 1)
                elif name == "ks_tok":
                    act.wait_ge(s_kmul_ok, 4 * NS)
                    copy_out(Qb[0:NS, 0, :], full(act, "ks_tok", 0)[0:NS, :], "ks_tok", 0)
                    evacuated(act, "ks_tok", 0)
                    act.dma_start(k_sample[0, :, 0, :, :].rearrange("b h d -> b (h d)"), Qb[0:NS, 0, :])\
                       .then_inc(s_out_small, 16)
                elif name == "va_s":
                    copy_out(Qb[0:NS, 1, :], full(act, "va_s", 0)[0:NS, :], "va_s", 0)
                    evacuated(act, "va_s", 0)
                    act.dma_start(v_sample[0, :, 0, :, :].rearrange("b h d -> b (h d)"), Qb[0:NS, 1, :])\
                       .then_inc(s_out_small, 16)
                elif name == "qb":
                    b, = a
                    out = full(act, "qb", b, 0)
                    if b >= 2:
                        act.wait_ge(s_kmul_ok, 4 * (b - 1))
                    copy_out(Qb[:, b % 2, :], out, "qb", b, 0)
                elif name == "tok":
                    group, i = a
                    key = ("tok", group, i, 0)
                    out = full(act, *key)
                    if group == VM:
                        act.wait_ge(s_vm_ones, 1)
                        copy_out(vm_tok[:, i, :, 0:MD], out.rearrange("p (h d) -> p h d", h=MH), *key)
                    elif group == KM:
                        copy_out(km_tok[:, i, :], out, *key)
                    elif group == VA:
                        copy_out(v_tok[:, i, :], out, *key)
                        evacuated(act, *key)
                        act.dma_start(v_prompt[0, 0, i * P:(i + 1) * P, :, :].rearrange("t h d -> t (h d)"),
                                      v_tok[:, i, :]).then_inc(s_out_v, 16)
                    else:
                        if i >= 2:
                            act.wait_ge(k_out[i % 2], 16)
                        copy_out(k_stage[:, i % 2, :], out, *key)
                        evacuated(act, *key)
                        act.dma_start(k_prompt[0, 0, i * P:(i + 1) * P, :, :].rearrange("t h d -> t (h d)"),
                                      k_stage[:, i % 2, :]).then_inc(k_out[i % 2], 16)
                elif name == "sm_r":
                    b, = a
                    evacuated(act, "sm_c", b, 0)
                    act.dma_start(C_sample[0, b].rearrange("h d e -> d h e"), Cs[:, b % 4, :, :])\
                       .then_inc(C_out[b % 4], 16)
                    if 2 <= b < 6:
                        n = b - 2
                        full(act, "sm_r", n, 0)
                        act.wait_ge(C_out[n], 16)
                        load_state(n + 4)
                elif name == "sm_end":
                    evacuated(act, "sm_out", 1)
                    act.dma_start(n_sample[0].rearrange("b h d -> (b h) d"), n_new_rows[:, :])\
                       .then_inc(s_out_small, 16)
                elif name == "ml_m":
                    h, = a
                    out = full(act, "ml_m", h, 0)
                    if h >= 2:
                        full(act, "ml_o", h - 2, 1)
                    if h == 0:
                        act.wait_ge(s_out_small, 32)
                        evacuated(act, "gcols", 0)
                    link(act.activation(MS[:, h:h + 1], out[:, SEQ - 1:SEQ], ACT.Copy, scale=-1.0))
                    act.activation(w_end[:, h, :], g_col[:, 0, :, h], ACT.Exp, bias=MS[:, h:h + 1])\
                       .then_inc(s_ml_wend, 1)
                    for j in range(NT):
                        w = SEQ - j * P
                        ins = act.activation(mA[:, h % 2, A_COL[j]:A_COL[j] + w], out[:, j * P:SEQ], ACT.Exp,
                                             scale=-1.0, bias=g_col[:, 0, j, h:h + 1])
                    free(ins, "ml_m", h, 0)
                elif name == "ml_t":
                    h, = a
                    out = full(act, "ml_t", h, 0)
                    free(act.activation(zT[:, QM + h, 0:SEQ], out, ACT.Copy, scale=par[:, 16 + h:17 + h]),
                         "ml_t", h, 0)
                elif name == "ml_mc":
                    h, = a
                    evacuated(act, "ml_mc", h, 0)
                    act.dma_start(C_prompt[0, 0, h, :, :], C_stage[:, h, :]).then_inc(s_out_C, 16)
                    if h == MH - 1:
                        act.dma_start(n_prompt[0, 0].rearrange("h d -> d h"), nc_col[:, :]).then_inc(s_out_C, 16)
                elif name == "mx_b":
                    act.wait_ge(s_samp_sub, 1)
                    flat = S[:, :, :, :].rearrange("p b g h -> p (b g h)")
                    act.activation(flat, flat, ACT.Exp, scale=ASCALE).then_inc(s_samp_exp, 1)
                    flat = own_p[:, :, :].rearrange("p b h -> p (b h)")
                    act.activation(flat, flat, ACT.Exp, scale=ASCALE).then_inc(s_samp_exp, 1)
                elif name == "att_s":
                    h, = a
                    if h == 0:
                        evacuated(act, "ml_t", MH - 1, 0)
                    for n, parts in enumerate(((0, 1), (2,), (3,))):
                        out = bank("att_s", h, n)
                        act.wait_ge(s_att_nmax, 3 * h + n + 1)
                        col = 0
                        for i in parts:
                            w = (i + 1) * P
                            ins = act.activation(pr[:, h % 2, P_COL[i]:P_COL[i] + w], out[:, col:col + w], ACT.Exp,
                                                 scale=ASCALE, bias=nmax[:, h % 2, i:i + 1],
                                                 accum_out=rsum[:, h % 2, i:i + 1])
                            col += w
                        free(ins, "att_s", h, n)
                elif name == "zsum":
                    act.wait_ge(s_out_C, 16 * (MH + 1))
                    act.activation(S_split[:, :, :, 0:AH], S[:, :, :, :], ACT.Copy).then_inc(s_p_hi, 1)
                elif name == "v_hi":
                    b, part = a
                    if b == 0:
                        act.wait_ge(s_half_done, 2 * N_IN)
                    for n in (2 * part, 2 * part + 1):
                        for j in (2 * n, 2 * n + 1):
                            act.wait_ge(kv_in[j], 16 * (NS + b + 1))
                        if b >= 1:
                            act.wait_ge(s_pv_used, 4 * (b - 1) + n + 1)
                        pair = slice(2 * n, 2 * n + 2)
                        act.activation(v_hi[:, pair, 0:AW], kv[:, pair, :], ACT.Copy).then_inc(s_v_hi, 1)
                elif name == "att_t":
                    h, = a
                    copy_out(pT[:, 0:A_COL[1]], full(act, "att_t", h, 0), "att_t", h, 0)
                    copy_out(pT[:, A_COL[2]:att], full(act, "att_t", h, 1)[:, 0:att - A_COL[2]], "att_t", h, 1)
                elif name == "att_o":
                    h, = a
                    own_rows = slice(64 * (h % 2), 64 * (h % 2) + 64)
                    out = full(act, "att_o", h, 0)
                    copy_out(zT[own_rows, QA + h // 2, 0:SEQ], out[own_rows, :], "att_o", h, 0)
                elif name == "om":
                    h, half = a
                    act.wait_ge(s_acc_evac, z_ready(OM + h))
                    o = zT[:, OM + h, half * HALF:(half + 1) * HALF]
                    act.activation(o, o, ACT.Exp, scale=-1.0).then_inc(s_om_exp, 1)
                elif name == "mix":
                    n, = a
                    j = MIX_ORDER[n]
                    if j < 4:
                        act.wait_ge(s_pv_end_ok, 2)
                        evacuated(act, "att_o", 2 * j, 0)
                        evacuated(act, "att_o", 2 * j + 1, 0)
                        src = zT[:, QA + j, :]
                    else:
                        act.wait_ge(s_gated, 2 * (j - 3))
                        src = zT[:, QM + j - 4, :]
                    act.activation(mix_hi[:, j, :], src, ACT.Copy).then_inc(s_mix_hi, 1)
                elif name == "xt":
                    j, = a
                    out = full(act, "xt", j, 0)
                    if j == 0:
                        act.wait_ge(s_mix_lo, KT)
                        act.wait_ge(s_out_small, 16 * 5)
                    copy_out(xT[:, j, 0:SEQ], out, "xt", j, 0)
                elif name == "xt_s":
                    copy_out(xT[:, :, SEQ:TOK], full(act, "xt_s", 0)[:, 0:KT * NS].rearrange("p (j b) -> p j b", j=KT),
                             "xt_s", 0)
                elif name == "x2":
                    j, = a
                    act.wait_ge(s_acc_evac, 2 * (G_OUT + j + 1))
                    act.activation(act_hi[:, j, :], xT[:, j, :], ACT.Copy, scale=par[:, 8 + j:9 + j])\
                       .then_inc(s_x2_hi, 1)
                    if j >= 2:
                        act.wait_ge(s_sq_added, max(j - 2, 1))
                    act.activation(x_sq[:, j % 2, :], xT[:, j, :], ACT.Square).then_inc(s_x1_sq, 1)

            def load_state(b):
                act.dma_start(Cs[:, b % 4, :, :], state_C[0, b].rearrange("h d e -> d h e")).then_inc(C_in[b % 4], 16)

            squares = [0]

            def y_square(i, part):
                n = P if i < NT else NS
                out = full(act, "yt", i, part)
                if squares[0] >= 1:
                    act.wait_ge(s_y_sq, squares[0])
                act.activation(y_junk[0:n, :], out[0:n, :], ACT.Square, accum_out=y_ss[0:n, i, part:part + 1])\
                   .then_inc(s_y_sq, 1)
                squares[0] += 1

            def y_scale(i):
                n = P if i < NT else NS
                evacuated(act, "yt", i, 0)
                act.wait_ge(s_y_pow, i + 1)
                act.activation(y_out[0:n, i, 0:512], y_out[0:n, i, 0:512], ACT.Copy, scale=y_ms[0:n, i:i + 1])\
                   .then_inc(s_y_half, 1)

            for g in range(G_MLP):
                if g != N_IN - 1:
                    split(g + AHEAD)
                for name in TASKS[g]:
                    task(*name)

            def quarter(i, last):
                for t in range(16):
                    g = G_MLP + 16 * i + t
                    if not last or t + AHEAD < 16:
                        n = t + AHEAD
                        weight_hi(act, g + AHEAD, n % WSLOTS, n // 2 % 2, (G_MLP // 4) + 4 * i + n // 4)
                    if t < 8:
                        act.wait_ge(s_acc_evac, 2 * (g + 1))
                        if t >= 2:
                            act.wait_ge(s_hs_lo, 8 * i + t - 1)
                        act.activation(relu2[:, t % 2, :], relu[:, t % 2, :], ACT.Square)
                        act.activation(h_hi[:, t, :], relu[:, t % 2, :], ACT.Square).then_inc(s_hs_hi, 1)
                    for n in Y_FIRST.get(t, ()) if last else ():
                        y_square(n, 0)

            with act.Fori(0, QUARTERS - 1) as i:
                quarter(i, False)
            quarter(QUARTERS - 1, True)
            for i in range(NT + 1):
                y_square(i, 1)
                if i >= 1:
                    y_scale(i - 1)
            y_scale(NT)
            act.wait_ge(s_out_v, 16 * NT)
            act.wait_ge(s_out_C, 16 * (MH + 1))
            act.wait_ge(s_out_small, 16 * 5)
            act.wait_ge(s_k_out0, 32)
            act.wait_ge(s_k_out1, 32)
            for b in range(4):
                act.wait_ge(C_out[b], 32)

        @block.gpsimd
        def _(pool):
            def rsqrt(x, n, free_size):
                return pool.tensor_tensor(x, x, power[0:n, :].to_broadcast([n, free_size]), ALU.pow)

            pool.memset(ident[:, :], 0.0).then_inc(s_pool_chain, 1)
            pool.memset(causal[:, :], 0.0).then_inc(s_pool_chain, 1)
            pool.memset(ones[:, :], 1.0).then_inc(s_pool_chain, 1)
            pool.memset(power[:, :], -0.5).then_inc(s_pool_chain, 1)
            pool.memset(even[:, :], 0.0).then_inc(s_pool_chain, 1)
            pool.memset(wg_hi[:, :, :].bitcast(F32), 0.0).then_inc(s_wg_zero, 1)
            pool.memset(wg_lo[:, :, :].bitcast(F32), 0.0).then_inc(s_wg_zero, 1)
            pool.wait_ge(s_pool_chain, 5)
            pool.affine_select(out=ident[:, :], in_=ident[:, :], compare_op=ALU.not_equal, fill=1.0, base=0,
                               pattern=[[-1, P]], channel_multiplier=1).then_inc(s_ident_ok, 1)
            pool.affine_select(out=causal[:, :], in_=causal[:, :], compare_op=ALU.is_ge, fill=MASKED, base=0,
                               pattern=[[-1, P]], channel_multiplier=1).then_inc(s_causal_ok, 1)
            pool.affine_select(out=even[:, 0:1], in_=even[:, 0:1], compare_op=ALU.is_ge, fill=1.0, base=-64,
                               pattern=[[1, 1]], channel_multiplier=1).then_inc(s_ident_ok, 1)
            pool.affine_select(out=even[:, 1:2], in_=even[:, 1:2], compare_op=ALU.is_ge, fill=1.0, base=63,
                               pattern=[[1, 1]], channel_multiplier=-1).then_inc(s_ident_ok, 1)
            for rows_split in (qs_split, vs_split, M_split):
                pool.memset(rows_split[:, :].bitcast(F32), 0.0).then_inc(s_sel_ok, 1)
            weight_lo(pool, 0, 0, 0)
            weight_lo(pool, 1, 1, 0)
            pool.wait_ge(s_x_ms_ok, 2)
            rsqrt(rs[:, 0:NT], P, NT).then_inc(s_x_rs_ok, 1)
            rsqrt(rs[0:NS, NT:NT + 1], NS, 1).then_inc(s_x_rs_ok, 1)
            weight_lo(pool, 2, 2, 1)
            pool.wait_ge(s_wg_hi_ok, 2)
            pool.tensor_tensor(wg_lo[:, :, 0:4], wg_raw[:, :, 0:4], wg_hi[:, :, 0:4].bitcast(F32), ALU.subtract)\
                .then_inc(s_wg_lo_ok, 1)
            pool.tensor_tensor(wg_lo[:, :, 32:36], wg_raw[:, :, 4:8], wg_hi[:, :, 32:36].bitcast(F32),
                               ALU.subtract).then_inc(s_wg_lo_ok, 1)

            def task(name, *a):
                if name == "weights":
                    n = a[0] + AHEAD
                    weight_lo(pool, n, n % WSLOTS, n // 2 % 2)
                elif name == "rows":
                    full(pool, "gates", 1)
                    pool.memset(vm_tok[:, :, :, MD:MD + 1], 1.0).then_inc(s_vm_ones, 1)
                elif name == "score":
                    b, c = a
                    n = 4 * b + c
                    if c == 0:
                        evacuated(pool, "qb", b, 0)
                    for j in (2 * c, 2 * c + 1):
                        pool.wait_ge(kv_in[j], 16 * (b + 1))
                    if n >= 2:
                        pool.wait_ge(s_kred_ok, n - 1)
                    pool.tensor_tensor(prod[:, n % 2, :].rearrange("p (j n) -> p j n", j=2),
                                       kv[:, 2 * c:2 * c + 2, :],
                                       Qb[:, b % 2:b % 2 + 1, :].to_broadcast([P, 2, AW]), ALU.mult)\
                        .then_inc(s_kmul_ok, 1)
                elif name == "sm_c":
                    b, = a
                    pool.wait_ge(s_sm_b_ok, 1)
                    pool.wait_ge(C_in[b % 4], 16 * (b // 4 + 1))
                    pool.tensor_tensor(Cs[:, b % 4, :, :], Cs[:, b % 4, :, :],
                                       sm_b[:, :, 0, b:b + 1].to_broadcast([P, MH, MD]), ALU.mult)\
                        .then_inc(s_C_decayed, 1)
                elif name == "sm_out":
                    evacuated(pool, "sm_out", 0)
                    rsqrt(sm_t[:, :, :].rearrange("p b h -> p (b h)"), P, NS * MH).then_inc(s_sm_pow, 1)
                elif name == "ml_m":
                    h, = a
                    evacuated(pool, "ml_m", h, 0)
                    for j in range(NT):
                        blk = mA[:, h % 2, A_COL[j]:A_COL[j] + P]
                        pool.affine_select(out=blk, in_=blk, compare_op=ALU.is_ge, fill=0.0, base=0,
                                           pattern=[[1, P]], channel_multiplier=-1).then_inc(s_ml_tri, 1)
                elif name == "ml_n":
                    h, = a
                    pool.wait_ge(s_ml_ms, h + 1)
                    rsqrt(m_rs[:, :], P, NT).then_inc(s_ml_pow, 1)
                elif name == "pv_zero":
                    evacuated(pool, "ml_mc", MH - 1, 0)
                    pool.memset(pv_masked[:, :, :], 0.0).then_inc(s_pv_zero, 1)
                elif name == "v_lo":
                    b, = a
                    value_lo(pool, b, 0, s_v_lo_a)
                    value_lo(pool, b, 1, s_v_lo_a)

            for g in range(G_MLP):
                n = g + AHEAD
                if n >= DVE_LO and g != N_IN - 1:
                    if n == DVE_LO:
                        pool.wait_ge(s_w_lo_ok, DVE_LO)
                    weight_lo(pool, n, n % WSLOTS, n // 2 % 2)
                for name in TASKS[g]:
                    task(*name)
            pool.wait_ge(s_rs2_ms, 1)
            evacuated(pool, "sumsq", 0)
            rsqrt(rs[:, 0:NT], P, NT).then_inc(s_rs2_pow, 1)
            rsqrt(rs[0:NS, NT:NT + 1], NS, 1).then_inc(s_rs2_pow, 1)

            with pool.Fori(0, QUARTERS) as i:
                for t in range(8):
                    pool.wait_ge(s_hs_hi, 8 * i + t + 1)
                    pool.tensor_tensor(h_lo[:, t, :], relu2[:, t % 2, :], h_hi[:, t, :].bitcast(F32),
                                       ALU.subtract).then_inc(s_hs_lo, 1)
            for i in range(NT + 1):
                n = P if i < NT else NS
                pool.wait_ge(s_y_ms_ok, i + 1)
                rsqrt(y_ms[0:n, i:i + 1], n, 1).then_inc(s_y_pow, 1)

        @block.vector
        def _(dve):
            chain = [0]

            def link(ins):
                chain[0] += 1
                ins.then_inc(s_dve_chain, 1)
                dve.wait_ge(s_dve_chain, chain[0])

            link(dve.memset(pick[:, :], 0.0))
            for q in range(4):
                dve.memset(pick[32 * q:32 * q + 2 * AH, 4 + q:5 + q], 1.0).then_inc(s_pick_ok, 1)
            dve.wait_ge(s_ident_ok, 3)
            dve.tensor_tensor(own_head[:, :], ident[0:2 * AH, 0:AH], ident[0:2 * AH, AH:2 * AH], ALU.add)\
               .then_inc(s_own_head, 1)
            dve.tensor_tensor(both[:, :], ident[0:LOW + NS, 0:NS], ident[0:LOW + NS, LOW:LOW + NS], ALU.add)\
               .then_inc(s_sel_ok, 1)
            dve.wait_ge(s_par_ok, 1)
            for j in range(KT):
                dve.wait_ge(s_xhi_ok, j + 1)
                out = acc[:, j, :] if j < 4 else full(dve, "xn", j)
                ins = dve.scalar_tensor_tensor(out=act_lo[:, j, 0:SEQ], in0=out, scalar=par[:, j:j + 1],
                                               in1=act_hi[:, j, 0:SEQ].bitcast(F32), op0=ALU.mult, op1=ALU.subtract)
                if j < 4:
                    ins.then_inc(s_x_lo, 1)
                else:
                    free(ins, "xn", j)
            evacuated(dve, "param", 0)
            link(dve.tensor_tensor(xn_s[:, :, :], xn_s[:, :, :],
                                   par[:, 0:KT].unsqueeze(2).to_broadcast([P, KT, NS]), ALU.mult))
            link(dve.tensor_copy(act_hi[:, :, SEQ:TOK], xn_s[:, :, :]))
            dve.tensor_tensor(act_lo[:, :, SEQ:TOK], xn_s[:, :, :], act_hi[:, :, SEQ:TOK].bitcast(F32),
                              ALU.subtract).then_inc(s_xs_ok, 1)
            dve.wait_ge(s_x_sq_ok, NT + 1)
            dve.tensor_scalar(rs[:, 0:NT], ss[:, 0:NT], 1.0 / D, EPS, ALU.mult, ALU.add).then_inc(s_x_ms_ok, 1)
            dve.tensor_scalar(rs[0:NS, NT:NT + 1], ss[0:NS, NT:NT + 1], 1.0 / D, EPS, ALU.mult, ALU.add)\
               .then_inc(s_x_ms_ok, 1)
            free(dve.tensor_copy(rstd1[:, 0:SEQ], full(dve, "rstd1", 0)), "rstd1", 0)
            free(dve.tensor_copy(rstd1[:, SEQ:TOK], full(dve, "rstd1", 1)[:, 0:NS]), "rstd1", 1)
            evacuated(dve, "rstd1", 0)
            evacuated(dve, "rstd1", 1)

            def sample_bh(c):
                return zT[:, c:c + MH, SEQ:TOK].rearrange("p h b -> p b h")

            def heads(r):
                return sm_b[:, :, r, :].rearrange("p h b -> p b h")

            def per_page(x):
                return x[:, :, :].unsqueeze(2).to_broadcast([P, NS, PAGES, AH])

            def task(name, *a):
                if name == "rows":
                    dve.wait_ge(s_small_in, 48)
                    for half in range(2):
                        cols = slice(half * HALF, (half + 1) * HALF)
                        out = full(dve, "gates", half)
                        dve.tensor_tensor(rows[:, 0, cols], out[0:4, 0:HALF], rstd1[0:4, cols], ALU.mult)
                        free(dve.tensor_tensor(rows[:, 1, cols], out[32:36, 0:HALF], rstd1[32:36, cols],
                                               ALU.mult), "gates", half)
                    evacuated(dve, "gates", 0)
                    evacuated(dve, "gates", 1)
                    dve.tensor_scalar(rows[:, 0, :], rows[:, 0, :], bias_i[:, :], None, ALU.add)
                    link(dve.tensor_scalar(rows[:, 1, :], rows[:, 1, :], bias_f[:, :], None, ALU.add))
                    dve.scalar_tensor_tensor(out=rows[:, 2, :], in0=rows[:, 1, :], scalar=-1.0, in1=rows[:, 1, :],
                                             op0=ALU.mult, op1=ALU.max).then_inc(s_f_abs, 1)
                    dve.memset(rows[:, 5, :], 0.0).then_inc(s_zero_row, 1)
                elif name == "rows_m":
                    dve.wait_ge(s_f_log, 1)
                    dve.wait_ge(s_zero_row, 1)
                    link(dve.scalar_tensor_tensor(out=rows[:, 1, :], in0=rows[:, 1, :], scalar=0.0,
                                                  in1=rows[:, 2, :], op0=ALU.min, op1=ALU.subtract))
                    link(dve.tensor_tensor_scan(rows[:, 4, 0:SEQ], rows[:, 1, 0:SEQ], rows[:, 5, 0:SEQ], 0.0,
                                                ALU.add, ALU.add))
                    link(dve.tensor_tensor(rows[:, 3, 0:SEQ], rows[:, 0, 0:SEQ], rows[:, 4, 0:SEQ], ALU.subtract))
                    M = rows[:, 0, 0:SEQ]
                    link(dve.tensor_tensor_scan(M, rows[:, 3, 0:SEQ], rows[:, 3, 0:SEQ], 0.0, ALU.max, ALU.max))
                    dve.tensor_tensor(rows[:, 2, 0:SEQ], rows[:, 4, 0:SEQ], M, ALU.add).then_inc(s_m_ok, 1)
                    dve.wait_ge(s_sel_ok, 4)
                    dve.tensor_copy(M_split[0:MH, :], M).then_inc(s_M_split, 1)
                    dve.wait_ge(s_M_split, 1)
                    dve.tensor_tensor(M_split[LOW:LOW + MH, :], M, M_split[0:MH, :].bitcast(F32), ALU.subtract)\
                       .then_inc(s_M_split, 1)
                    i_s, lf_s = rows[:, 0, SEQ:TOK], rows[:, 1, SEQ:TOK]
                    link(dve.tensor_tensor(s_rows[:, 0, :], lf_s, m0_row[:, :], ALU.add))
                    link(dve.tensor_tensor(m_s[:, :], s_rows[:, 0, :], i_s, ALU.max))
                    dve.tensor_tensor(s_rows[:, 1, :], i_s, m_s[:, :], ALU.subtract)
                    dve.tensor_tensor(s_rows[:, 0, :], s_rows[:, 0, :], m_s[:, :], ALU.subtract)\
                       .then_inc(s_srow_ok, 1)
                elif name in ("qs_tok", "vs_tok"):
                    rows_hi, made = (qs_split, s_qs_hi) if name == "qs_tok" else (vs_split, s_vs_hi)
                    out = full(dve, name, 0)
                    dve.wait_ge(made, 1)
                    free(dve.tensor_tensor(rows_hi[LOW:LOW + NS, :], out[0:NS, :], rows_hi[0:NS, :].bitcast(F32),
                                           ALU.subtract), name, 0)
                elif name == "gcols":
                    out = full(dve, "gcols", 0)
                    free(dve.tensor_copy(g_col[:, :, :, :].rearrange("p r i h -> p (r i h)"),
                                         out[:, 0:2 * NT * MH]), "gcols", 0)
                elif name == "score":
                    b, c = a
                    n = 4 * b + c
                    dve.wait_ge(s_kmul_ok, n + 1)
                    dve.tensor_reduce(S[:, b, 2 * c:2 * c + 2, :].rearrange("p j h -> p (j h)"),
                                      prod[:, n % 2, :].rearrange("p (g d) -> p g d", d=AD), AX.X, ALU.add)\
                       .then_inc(s_kred_ok, 1)
                elif name == "sm_prep":
                    out = full(dve, "sm_prep", 0)
                    free(dve.tensor_copy(sm_b[:, :, :, :].rearrange("p h r b -> p (h r b)"),
                                         out[:, 0:MH * 3 * NS]), "sm_prep", 0)
                    evacuated(dve, "sm_prep", 0)
                    dve.tensor_tensor(sm_kw[:, :, :], zT[:, KM:KM + MH, SEQ:TOK], sm_b[:, :, 1, :], ALU.mult)\
                       .then_inc(s_sm_b_ok, 1)
                    out = full(dve, "sm_prep", 1)
                    free(dve.tensor_tensor(sm_n[:, :, :], out[:, 0:NS * MH].rearrange("p (b h) -> p b h", b=NS),
                                           heads(0), ALU.mult), "sm_prep", 1)
                    evacuated(dve, "sm_prep", 1)
                    dve.wait_ge(s_sm_b_ok, 1)
                    link(dve.tensor_tensor(sm_n[:, :, :], sm_n[:, :, :],
                                           sm_kw[:, :, :].rearrange("p h b -> p b h"), ALU.add))
                    dve.tensor_tensor(sm_q[:, :, :], sample_bh(QM), sm_n[:, :, :], ALU.mult).then_inc(s_sm_dve, 1)
                elif name == "sm_c":
                    b, = a
                    out = full(dve, "sm_c", b, 0)
                    dve.wait_ge(s_C_decayed, b + 1)
                    for h in range(MH):
                        ins = dve.scalar_tensor_tensor(out=Cs[:, b % 4, h, :], in0=out[:, h * MD:(h + 1) * MD],
                                                       scalar=sm_kw[:, h, b:b + 1], in1=Cs[:, b % 4, h, :],
                                                       op0=ALU.mult, op1=ALU.add)
                    free(ins, "sm_c", b, 0)
                elif name == "sm_r":
                    b, = a
                    out = full(dve, "sm_r", b, 0)
                    free(dve.tensor_copy(sm_h[:, b, :], out[:, 0:MH]), "sm_r", b, 0)
                elif name == "sm_den":
                    for b in range(NS):
                        evacuated(dve, "sm_r", b, 0)
                    out = full(dve, "sm_den", 0)[:, 0:NS * MH].rearrange("p (b h) -> p b h", b=NS)
                    link(dve.scalar_tensor_tensor(out=sm_t[:, :, :], in0=out, scalar=-MSCALE, in1=heads(2),
                                                  op0=ALU.mult, op1=ALU.max))
                    free(dve.scalar_tensor_tensor(out=sm_t[:, :, :], in0=out, scalar=MSCALE, in1=sm_t[:, :, :],
                                                  op0=ALU.mult, op1=ALU.max), "sm_den", 0)
                    evacuated(dve, "sm_den", 0)
                    link(dve.reciprocal(sm_t[:, :, :], sm_t[:, :, :]))
                    link(dve.scalar_tensor_tensor(out=sm_h[:, :, :], in0=sm_h[:, :, :], scalar=MSCALE,
                                                  in1=sm_t[:, :, :], op0=ALU.mult, op1=ALU.mult))
                    dve.tensor_tensor(sm_t[:, :, :], sm_h[:, :, :], sm_h[:, :, :], ALU.mult).then_inc(s_sm_dve, 1)
                elif name == "sm_out":
                    out = full(dve, "sm_out", 0)
                    free(dve.tensor_scalar(sm_t[:, :, :].rearrange("p b h -> p (b h)"), out[:, 0:NS * MH],
                                           1.0 / MD, EPS, ALU.mult, ALU.add), "sm_out", 0)
                    out = full(dve, "sm_out", 1)
                    free(dve.tensor_copy(n_new_rows[:, :], out[0:NS * MH, 0:P]), "sm_out", 1)
                elif name == "sm_end":
                    dve.wait_ge(s_sm_pow, 1)
                    link(dve.tensor_tensor(sm_h[:, :, :], sm_h[:, :, :], sm_t[:, :, :], ALU.mult))
                    dve.tensor_tensor(sample_bh(QM), sm_h[:, :, :],
                                      par[:, 16:20].unsqueeze(1).to_broadcast([P, NS, MH]), ALU.mult)\
                       .then_inc(s_sm_end, 1)
                elif name == "ml_k":
                    h, = a
                    for n, parts in enumerate(((0,), (1,), (2, 3))):
                        out = full(dve, "ml_k", h, n)
                        col = 0
                        for j in parts:
                            w = SEQ - j * P
                            dve.wait_ge(s_ml_tri, 4 * h + j + 1)
                            blk = mA[:, h % 2, A_COL[j]:A_COL[j] + w]
                            ins = dve.scalar_tensor_tensor(out=blk, in0=out[:, col:col + w], scalar=MSCALE,
                                                           in1=blk, op0=ALU.mult, op1=ALU.mult)
                            col += w
                        free(ins, "ml_k", h, n)
                elif name == "ml_o":
                    h, = a
                    m_h = m_hs[h % 2]
                    if h >= 2:
                        full(dve, "ml_t", h - 2, 0)
                    if h >= 1:
                        dve.wait_ge(s_ml_hr, h)
                    for half in range(2):
                        out = full(dve, "ml_o", h, half)[:, 0:2 * (MD + 1)].rearrange("p (i e) -> p i e", i=2)
                        two = slice(2 * half, 2 * half + 2)
                        link(dve.scalar_tensor_tensor(out=m_den[:, two], in0=out[:, :, MD], scalar=-1.0,
                                                      in1=g_col[:, 1, two, h], op0=ALU.mult, op1=ALU.max))
                        link(dve.tensor_tensor(m_den[:, two], out[:, :, MD], m_den[:, two], ALU.max))
                        link(dve.reciprocal(m_den[:, two], m_den[:, two]))
                        free(dve.tensor_tensor(m_h[:, two, :], out[:, :, 0:MD],
                                               m_den[:, two].unsqueeze(2).to_broadcast([P, 2, MD]), ALU.mult),
                             "ml_o", h, half)
                    evacuated(dve, "ml_o", h, 0)
                    evacuated(dve, "ml_o", h, 1)
                    link(dve.tensor_tensor(m_kw[:, :, :], m_h[:, :, :], m_h[:, :, :], ALU.mult))
                    link(dve.tensor_reduce(m_ss[:, :], m_kw[:, :, :], AX.X, ALU.add))
                    dve.tensor_scalar(m_rs[:, :], m_ss[:, :], 1.0 / MD, EPS, ALU.mult, ALU.add).then_inc(s_ml_ms, 1)
                elif name == "ml_n":
                    h, = a
                    m_h = m_hs[h % 2]
                    dve.wait_ge(s_ml_pow, h + 1)
                    dve.tensor_tensor(m_h[:, :, :], m_h[:, :, :],
                                      m_rs[:, :].unsqueeze(2).to_broadcast([P, NT, MD]), ALU.mult)\
                       .then_inc(s_ml_hr, 1)
                elif name == "ml_kw":
                    h, = a
                    dve.wait_ge(s_ml_wend, h + 1)
                    if h == 0:
                        for i in range(NT):
                            evacuated(dve, "tok", KM, i, 0)
                    else:
                        full(dve, "ml_mc", h - 1, 0)
                    dve.tensor_tensor(m_kw[:, :, :], km_tok[:, :, h * MD:(h + 1) * MD],
                                      w_end[:, h, :].unsqueeze(2).to_broadcast([P, NT, MD]), ALU.mult)\
                       .then_inc(s_ml_kw, 1)
                elif name == "ml_mc":
                    h, = a
                    out = full(dve, "ml_mc", h, 0)
                    dve.tensor_copy(nc_col[:, h:h + 1], out[:, MD:MD + 1])
                    free(dve.tensor_copy(C_stage[:, h, :], out[:, 0:MD]), "ml_mc", h, 0)
                elif name == "gate":
                    out = full(dve, "gate", 0)
                    blocks = gate[:, :, :, :]
                    free(dve.tensor_reduce(blocks.rearrange("p b n h -> p (b n) h"),
                                           out.rearrange("p (m two h) -> p m h two", two=2, h=AH), AX.X, ALU.add),
                         "gate", 0)
                    evacuated(dve, "gate", 0)
                    link(dve.tensor_reduce(gate_min[:, :, :], blocks.rearrange("p b n h -> p b h n"), AX.X, ALU.min))
                    link(dve.tensor_tensor(blocks, blocks,
                                           gate_min[:, :, :].unsqueeze(2).to_broadcast([P, NS, 4, AH]),
                                           ALU.is_equal))
                    later = gate[:, :, 3, :]
                    for n, into in ((2, taken), (1, gate_min), (0, None)):
                        if into is not None:
                            link(dve.tensor_tensor(into[:, :, :], gate[:, :, n, :], later, ALU.max))
                        link(dve.tensor_tensor(gate[:, :, n, :], gate[:, :, n, :], later, ALU.is_gt))
                        if into is not None:
                            later = into[:, :, :]
                    link(dve.tensor_scalar(blocks, blocks, MASKED, None, ALU.mult))
                    by_page = S[:, :, :, :].rearrange("p b (n two) h -> p (b n) two h", two=2)
                    for two in range(2):
                        link(dve.tensor_tensor(by_page[:, :, two, :], by_page[:, :, two, :],
                                               blocks.rearrange("p b n h -> p (b n) h"), ALU.add))
                    dve.tensor_reduce(page_max[:, :, :], S[:, :, :, :].rearrange("p b g h -> p b h g"), AX.X,
                                      ALU.max).then_inc(s_samp_dve, 1)
                elif name == "mx_t":
                    out = full(dve, "mx_t", 0)
                    free(dve.reduce_max(mx_col[:, :], out[0:NS * AH, 0:P], AX.X), "mx_t", 0)
                    dve.tensor_tensor(own_prod[:, :, :], zT[:, QA:QA + 4, SEQ:TOK], zT[:, KA:KA + 4, SEQ:TOK],
                                      ALU.mult).then_inc(s_samp_dve, 1)
                elif name == "own":
                    out = full(dve, "own", 0)
                    for odd in range(2):
                        ins = dve.tensor_copy(own[:, :, :].rearrange("p b (t o) -> p t b o", o=2)[:, :, :, odd],
                                              out[:, odd * 32:(odd + 1) * 32].rearrange("p (t b) -> p t b", t=4))
                    free(ins, "own", 0)
                elif name == "mx_b":
                    evacuated(dve, "own", 0)
                    out = full(dve, "mx_b", 0)[:, 0:NS * AH].rearrange("p (b h) -> p b h", b=NS)
                    free(dve.tensor_tensor(smax[:, :, :], out, own[:, :, :], ALU.max), "mx_b", 0)
                    evacuated(dve, "mx_b", 0)
                    dve.tensor_tensor(own_p[:, :, :], own[:, :, :], smax[:, :, :], ALU.subtract)
                    dve.tensor_tensor(S[:, :, :, :], S[:, :, :, :], per_page(smax), ALU.subtract)\
                       .then_inc(s_samp_sub, 1)
                elif name == "p_sum":
                    dve.wait_ge(s_samp_exp, 1)
                    dve.tensor_reduce(page_max[:, :, :], S[:, :, :, :].rearrange("p b g h -> p b h g"), AX.X,
                                      ALU.add).then_inc(s_samp_dve, 1)
                elif name == "zsum":
                    dve.wait_ge(s_samp_exp, 2)
                    out = full(dve, "zsum", 0)[:, 0:NS * AH].rearrange("p (b h) -> p b h", b=NS)
                    free(dve.tensor_tensor(zrec[:, :, :], out, own_p[:, :, :], ALU.add), "zsum", 0)
                    evacuated(dve, "zsum", 0)
                    link(dve.reciprocal(zrec[:, :, :], zrec[:, :, :]))
                    dve.wait_ge(s_p_hi, 1)
                    dve.tensor_tensor(S_split[:, :, :, AH:2 * AH], S[:, :, :, :],
                                      S_split[:, :, :, 0:AH].bitcast(F32), ALU.subtract).then_inc(s_p_lo, 1)
                elif name == "pv":
                    b, = a
                    dve.wait_ge(s_pv_used, 4 * (b + 1))
                    out = acc[:, 1 + b % 2, :]
                    dve.wait_ge(s_own_head, 1)
                    dve.wait_ge(s_pv_zero, 1)
                    own_rows = slice(32 * (b % 4), 32 * (b % 4) + 2 * AH)
                    dve.tensor_tensor(pv_masked[own_rows, b // 4, :].rearrange("p (h d) -> p h d", h=AH),
                                      out[0:2 * AH, :].rearrange("p (h d) -> p h d", h=AH),
                                      own_head[:, :].unsqueeze(2).to_broadcast([2 * AH, AH, AD]), ALU.mult)\
                       .then_inc(s_pv_masked, 1)
                elif name == "pv_tok":
                    dve.wait_ge(s_pv_sum, 2)
                    dve.wait_ge(s_out_small, 16 * 5)
                    dve.tensor_copy(pv_tok[:, :], acc[0:NS, 0, :]).then_inc(s_pv_tok, 1)
                elif name == "pv_end":
                    out = full(dve, "pv_end", 0)
                    for odd in range(2):
                        rows64 = slice(64 * odd, 64 * odd + 64)

                        def by_tile(x):
                            return x[rows64, :, :].rearrange("p b (t o) -> p t b o", o=2)[:, :, :, odd]

                        tmp = own_prod[rows64, :, :]
                        link(dve.tensor_tensor(tmp, zT[rows64, VA:VA + 4, SEQ:TOK], by_tile(own_p), ALU.mult))
                        cache_part = out[rows64, 0:4 * NS].rearrange("p (t b) -> p t b", t=4)
                        ins = dve.tensor_tensor(tmp, tmp, cache_part, ALU.add)
                        if odd == 0:
                            link(ins)
                        else:
                            free(ins, "pv_end", 0)
                            evacuated(dve, "pv_end", 0)
                        dve.tensor_tensor(zT[rows64, QA:QA + 4, SEQ:TOK], tmp, by_tile(zrec), ALU.mult)\
                           .then_inc(s_pv_end_ok, 1)
                elif name == "att_d":
                    h, = a
                    for n in range(3):
                        evacuated(dve, "att_s", h, n)
                    link(dve.reciprocal(rrec[:, h % 2, :], rsum[:, h % 2, :]))
                    dve.tensor_tensor(p_norm[:, h % 2, :, :], ident[:, :].unsqueeze(1).to_broadcast([P, NT, P]),
                                      rrec[:, h % 2, :].unsqueeze(2).to_broadcast([P, NT, P]), ALU.mult)\
                       .then_inc(s_norm_ok, 1)
                elif name == "att_s":
                    h, = a
                    if h == 0:
                        dve.wait_ge(s_causal_ok, 1)
                    for n, parts in enumerate(((0, 1), (2,), (3,))):
                        out = full(dve, "att_s", h, n)
                        col = 0
                        for i in parts:
                            blk = out[:, col + i * P:col + (i + 1) * P]
                            ins = dve.tensor_tensor(blk, blk, causal[:, :], ALU.add)
                            col += (i + 1) * P
                        link(ins)
                        col = 0
                        for i in parts:
                            w = (i + 1) * P
                            ins = dve.reduce_max(rmax[:, h % 2, i:i + 1], out[:, col:col + w], AX.X)
                            col += w
                        link(ins)
                        dve.tensor_scalar(nmax[:, h % 2, parts[0]:parts[-1] + 1],
                                          rmax[:, h % 2, parts[0]:parts[-1] + 1], -ASCALE, None, ALU.mult)\
                           .then_inc(s_att_nmax, 1)
                elif name == "v_lo":
                    b, = a
                    value_lo(dve, b, 2, s_v_lo_b)
                    value_lo(dve, b, 3, s_v_lo_b)
                elif name == "att_t":
                    h, = a
                    if h >= 1:
                        full(dve, "att_o", h - 1, 0)
                    dve.wait_ge(s_att_t1, h + 1)
                    dve.tensor_copy(pT[:, A_COL[1]:A_COL[2]], acc[:, 3, 0:A_COL[2] - A_COL[1]])\
                       .then_inc(s_att_t1_out, 1)
                elif name == "om":
                    h, half = a
                    dve.wait_ge(s_om_exp, 2 * h + half + 1)
                    dve.wait_ge(s_sm_end, 1)
                    evacuated(dve, "ml_t", h, 0)
                    cols = slice(half * HALF, (half + 1) * HALF)
                    o = zT[:, OM + h, cols]
                    link(dve.tensor_scalar(o, o, 1.0, None, ALU.add))
                    link(dve.reciprocal(o, o))
                    dve.tensor_tensor(zT[:, QM + h, cols], zT[:, QM + h, cols], o, ALU.mult).then_inc(s_gated, 1)
                elif name == "mix":
                    n, = a
                    j = MIX_ORDER[n]
                    dve.wait_ge(s_mix_hi, n + 1)
                    src = zT[:, QA + j, :] if j < 4 else zT[:, QM + j - 4, :]
                    dve.tensor_tensor(mix_parts[1][j], src, mix_hi[:, j, :].bitcast(F32), ALU.subtract)\
                       .then_inc(s_mix_lo, 1)
                elif name == "x2":
                    j, = a
                    dve.wait_ge(s_x2_hi, j + 1)
                    dve.scalar_tensor_tensor(out=act_lo[:, j, :], in0=xT[:, j, :], scalar=par[:, 8 + j:9 + j],
                                             in1=act_hi[:, j, :].bitcast(F32), op0=ALU.mult, op1=ALU.subtract)\
                       .then_inc(s_x2_lo, 1)
                    if j >= 1:
                        dve.wait_ge(s_x1_sq, j + 1)
                        if j >= 2:
                            dve.wait_ge(s_sq_added, j - 1)
                        so_far = x_sq[:, 0, :] if j == 1 else sq_sum[:, :]
                        dve.tensor_tensor(sq_sum[:, :], so_far, x_sq[:, j % 2, :], ALU.add).then_inc(s_sq_added, 1)

            def evac_copy(g):
                for half in range(2):
                    dve.wait_ge(s_half_done, 2 * g + half + 1)
                    cols = slice(half * HALF, (half + 1) * HALF)
                    dve.tensor_tensor(zT[:, IN_ORDER[g], cols], acc[:, 2 * (g % 2) + half, 0:HALF],
                                      rstd1[:, cols], ALU.mult).then_inc(s_acc_evac, 1)

            def evac_add(g, side, j, half):
                dve.wait_ge(s_half_done, 2 * g + half + 1)
                x = xT[:, j, half * HALF:(half + 1) * HALF]
                dve.tensor_tensor(x, acc[:, 2 * side + half, 0:HALF], x, ALU.add).then_inc(s_acc_evac, 1)

            for g in range(N_IN):
                if IN_ORDER[g] == VA:
                    for b in range(4):
                        dve.wait_ge(C_out[b], 32)
                if IN_ORDER[g] == OM:
                    dve.wait_ge(s_k_out0, 32)
                    dve.wait_ge(s_k_out1, 32)
                n = g + AHEAD
                if n < DVE_LO:
                    if n == AHEAD:
                        dve.wait_ge(s_w_lo_ok, AHEAD)
                    weight_lo(dve, n, n % WSLOTS, n // 2 % 2)
                evac_copy(g)
                for name in TASKS[g]:
                    task(*name)
            for g in range(G_OUT, G_MLP):
                j = g - G_OUT
                evacuated(dve, "xt", j, 0)
                evacuated(dve, "xt_s", 0)
                for half in range(2):
                    evac_add(g, g % 2, j, half)
                for name in TASKS[g]:
                    task(*name)
            out = full(dve, "sumsq", 0)
            dve.tensor_scalar(rs[:, 0:NT], out[:, 0:NT], 1.0 / D, EPS, ALU.mult, ALU.add).then_inc(s_rs2_ms, 1)
            free(dve.tensor_scalar(rs[0:NS, NT:NT + 1], out[0:NS, NT:NT + 1], 1.0 / D, EPS, ALU.mult, ALU.add),
                 "sumsq", 0)
            free(dve.tensor_copy(rstd2[:, 0:SEQ], full(dve, "rstd2", 0)), "rstd2", 0)
            free(dve.tensor_copy(rstd2[:, SEQ:TOK], full(dve, "rstd2", 1)[:, 0:NS]), "rstd2", 1)
            evacuated(dve, "rstd2", 0)
            evacuated(dve, "rstd2", 1)

            def quarter(i, last):
                for t in range(16):
                    g = G_MLP + 16 * i + t
                    if not last or t + AHEAD < 16:
                        n = t + AHEAD
                        weight_lo(dve, g + AHEAD, n % WSLOTS, n // 2 % 2)
                    for half in range(2):
                        cols = slice(half * HALF, (half + 1) * HALF)
                        if t < 8:
                            dve.wait_ge(s_half_done, 2 * g + half + 1)
                            if t >= 2:
                                dve.wait_ge(s_hs_hi, 8 * i + t - 1)
                            dve.scalar_tensor_tensor(out=relu[:, t % 2, cols], in0=acc[:, 2 * (t % 2) + half, 0:HALF],
                                                     scalar=0.0, in1=rstd2[:, cols], op0=ALU.max, op1=ALU.mult)\
                               .then_inc(s_acc_evac, 1)
                        else:
                            evac_add(g, t % 2, t - 8, half)
                    for n in Y_FIRST.get(t, ()) if last else ():
                        y_first(n)

            y_order = [(i, 0) for i in range(NT + 1)] + [(i, 1) for i in range(NT + 1)]

            def y_first(i):
                n = P if i < NT else NS
                out = full(dve, "yt", i, 0)
                dve.wait_ge(s_y_sq, y_order.index((i, 0)) + 1)
                dve.tensor_scalar(y_ms[0:n, i:i + 1], y_ss[0:n, i, 0:1], 1.0 / D, EPS, ALU.mult, ALU.add)
                free(dve.tensor_tensor(y_out[0:n, i, 0:512], out[0:n, :], lnf_b[0:n, 0:512], ALU.mult), "yt", i, 0)

            dve.wait_ge(s_w_lo_ok, G_MLP + AHEAD)
            with dve.Fori(0, QUARTERS - 1) as i:
                quarter(i, False)
            dve.wait_ge(s_lnf_in, 16)
            quarter(QUARTERS - 1, True)
            for i in range(NT + 1):
                n = P if i < NT else NS
                out = full(dve, "yt", i, 1)
                evacuated(dve, "yt", i, 0)
                dve.wait_ge(s_y_sq, y_order.index((i, 1)) + 1)
                dve.scalar_tensor_tensor(out=y_ms[0:n, i:i + 1], in0=y_ss[0:n, i, 1:2], scalar=1.0 / D,
                                         in1=y_ms[0:n, i:i + 1], op0=ALU.mult, op1=ALU.add).then_inc(s_y_ms_ok, 1)
                dve.wait_ge(s_y_pow, i + 1)
                free(dve.scalar_tensor_tensor(out=y_out[0:n, i, 512:D], in0=out[0:n, :], scalar=y_ms[0:n, i:i + 1],
                                              in1=lnf_b[0:n, 512:D], op0=ALU.mult, op1=ALU.mult), "yt", i, 1)


_INS = ["x_prompt", "x_sample", "cache_k", "cache_v", "page_table", "state_C", "state_n", "state_m", "ln1_w",
        "w_in", "b_gates", "mlstm_norm_w", "w_out", "ln2_w", "w_up", "w_down", "lnf_w"]
_OUTS = [(1, SEQ, D), (NS, 1, D), (1, 1, SEQ, AH, AD), (1, 1, SEQ, AH, AD), (1, 1, MH, MD, MD), (1, 1, MH, MD),
         (1, 1, MH), (1, NS, 1, AH, AD), (1, NS, 1, AH, AD), (1, NS, MH, MD, MD), (1, NS, MH, MD), (1, NS, MH)]


def kernel(**inputs):
    import numpy as _np
    import concourse.bacc as _bacc
    from concourse import mybir as _mybir
    from concourse.bass_utils import run_bass_kernel_spmd as _run

    nc = _bacc.Bacc("TRN2", target_bir_lowering=False, num_devices=1)
    arrays, args = {}, []
    for name in _INS:
        a = _np.ascontiguousarray(inputs[name])
        arrays[f"in_{name}_dram"] = a
        args.append(nc.dram_tensor(f"in_{name}_dram", a.shape, _mybir.dt.from_np(a.dtype), kind="ExternalInput").ap())
    for i, shape in enumerate(_OUTS):
        args.append(nc.dram_tensor(f"out_{i}_dram", shape, _mybir.dt.float32, kind="ExternalOutput").ap())
    build(nc, *args)
    r = _run(nc, [arrays], core_ids=[0])
    return tuple(r.results[0][f"out_{i}_dram"] for i in range(len(_OUTS)))
```
